# Optimizing a Trainium2 kernel written in Bass

```python
import jax, jax.numpy as jnp
from jax import lax
import numpy as np
import math

D_MODEL = 1024
BATCH = 1
SEQ = 256
DEPTH = 2

N_MIXERS = 2
N_RWKV_LAYERS = (DEPTH + 1) // 2
N_GMLP_LAYERS = DEPTH // 2
N_MEM = 256

RWKV_HEAD = 64
RWKV_HEADS = D_MODEL // RWKV_HEAD
LORA_DECAY = 64
LORA_AAA = 64
LORA_GATE = 160
GN_EPS = 64e-5

GMLP_CHUNK = 128
GMLP_WIDTH = 2 * D_MODEL
GMLP_GROUP_DIM = 128
GMLP_GROUPS = GMLP_WIDTH // GMLP_GROUP_DIM

XATTN_HEADS = 4
XATTN_HEAD_DIM = D_MODEL // XATTN_HEADS

D_FF = 2816
RMS_EPS = 1e-6


def rms_norm(x, g):
    x32 = x.astype(jnp.float32)
    y = x32 * lax.rsqrt(jnp.mean(x32 * x32, axis=-1, keepdims=True) + RMS_EPS)
    return (y * g.astype(jnp.float32)).astype(x.dtype)

def swiglu_ffn(h, w_in, w_out):
    gate, up = jnp.split(h @ w_in, 2, axis=-1)
    return (jax.nn.silu(gate) * up) @ w_out

def token_shift(x):
    return jnp.pad(x[:, :-1], ((0, 0), (1, 0), (0, 0)))

def rwkv7_time_mix(h, mu, w_rkv, w0, w1, w2, a0, a1, a2, g1, g2, k_k, k_a, r_k, ln_w, ln_b, w_o):
    B, S, C = h.shape
    H, N = RWKV_HEADS, RWKV_HEAD
    dx = token_shift(h) - h
    xr = h + dx * mu[0]
    xw = h + dx * mu[1]
    xk = h + dx * mu[2]
    xv = h + dx * mu[3]
    xa = h + dx * mu[4]
    xg = h + dx * mu[5]
    x3 = jnp.stack([xr, xk, xv], axis=0)
    rkv = jnp.einsum('nbsc,cnd->nbsd', x3, w_rkv.reshape(C, 3, C))
    r, k, v = rkv[0], rkv[1], rkv[2]
    w = -jax.nn.softplus(-(w0 + jnp.tanh(xw @ w1) @ w2)) - 0.5
    decay = jnp.exp(-jnp.exp(w.astype(jnp.float32)))
    a = jax.nn.sigmoid(a0 + (xa @ a1) @ a2)
    g = jax.nn.sigmoid(xg @ g1) @ g2
    kk = (k * k_k).reshape(B, S, H, N).astype(jnp.float32)
    kk = kk / jnp.maximum(jnp.linalg.norm(kk, axis=-1, keepdims=True), 1e-12)
    k = k * (1.0 + (a - 1.0) * k_a)

    def heads(t):
        return t.reshape(B, S, H, N).astype(jnp.float32)

    r_h, k_h, v_h, a_h = heads(r), heads(k), heads(v), heads(a)
    b_h = kk * a_h
    xs = tuple(jnp.moveaxis(t, 1, 0) for t in (r_h, heads(decay), k_h, v_h, kk, b_h))

    def step(state, inp):
        r_t, w_t, k_t, v_t, kk_t, b_t = inp
        sa = jnp.einsum('bhij,bhj->bhi', state, -kk_t)
        state = (state * w_t[:, :, None, :] + sa[..., None] * b_t[:, :, None, :]
                 + v_t[..., :, None] * k_t[:, :, None, :])
        y = jnp.einsum('bhij,bhj->bhi', state, r_t)
        return state, y

    s0 = jnp.zeros((B, H, N, N), jnp.float32)
    _, ys = lax.scan(step, s0, xs)
    y = jnp.moveaxis(ys, 0, 1)
    mean = jnp.mean(y, axis=-1, keepdims=True)
    var = jnp.mean(jnp.square(y - mean), axis=-1, keepdims=True)
    y = ((y - mean) * lax.rsqrt(var + GN_EPS)).reshape(B, S, C)
    y = y * ln_w.astype(jnp.float32) + ln_b.astype(jnp.float32)
    bonus = jnp.sum(r_h * k_h * r_k.astype(jnp.float32), axis=-1, keepdims=True) * v_h
    y = (y + bonus.reshape(B, S, C)).astype(h.dtype)
    return (y * g) @ w_o

def gmlp_chunk_mix(h, w_uv, v_norm, w_s, b_s, w_o):
    B, S, _ = h.shape
    z = jax.nn.gelu(h @ w_uv)
    u, v = jnp.split(z, 2, axis=-1)
    v = rms_norm(v, v_norm)
    v = v.reshape(B, S // GMLP_CHUNK, GMLP_CHUNK, GMLP_GROUPS, GMLP_GROUP_DIM)
    causal = jnp.tril(jnp.ones((GMLP_CHUNK, GMLP_CHUNK), dtype=bool))
    ws = jnp.where(causal[None], w_s, jnp.zeros_like(w_s))
    sv = jnp.einsum('gts,bcsgd->bctgd', ws, v) + jnp.transpose(b_s)[:, :, None]
    sv = sv.reshape(B, S, GMLP_WIDTH)
    return (u * sv) @ w_o

def memory_cross_attention(h, mem_k, mem_v, wq, wo):
    B, S, C = h.shape
    q = (h @ wq).reshape(B, S, XATTN_HEADS, XATTN_HEAD_DIM)
    s = jnp.einsum('bshd,bmhd->bhsm', q, mem_k).astype(jnp.float32) * (XATTN_HEAD_DIM ** -0.5)
    p = jax.nn.softmax(s, axis=-1).astype(h.dtype)
    o = jnp.einsum('bhsm,bmhd->bshd', p, mem_v).reshape(B, S, C)
    return o @ wo

def first_inputs(seed: int = 0) -> dict:
    key = jax.random.key(seed)
    ks = iter(jax.random.split(key, 48))
    C, F = D_MODEL, D_FF
    L, NA, NB = DEPTH, N_RWKV_LAYERS, N_GMLP_LAYERS

    def nrm(shape, scale):
        return jax.random.normal(next(ks), shape, jnp.float32) * scale

    def gain(shape):
        return 1.0 + 0.05 * jax.random.normal(next(ks), shape, jnp.float32)

    return {
        "x": jax.random.normal(next(ks), (BATCH, SEQ, C), jnp.float32),
        "mem": jax.random.normal(next(ks), (BATCH, N_MEM, C), jnp.float32),
        "mem_norm": gain((C,)),
        "mem_w_kv": nrm((C, 2 * C), C ** -0.5),
        "ffn1_norm": gain((L, C)),
        "ffn1_w_in": nrm((L, C, 2 * F), C ** -0.5),
        "ffn1_w_out": nrm((L, F, C), F ** -0.5),
        "mix_norm": gain((L, C)),
        "xattn_norm": gain((L, C)),
        "xattn_wq": nrm((L, C, C), C ** -0.5),
        "xattn_wo": nrm((L, C, C), C ** -0.5),
        "ffn2_norm": gain((L, C)),
        "ffn2_w_in": nrm((L, C, 2 * F), C ** -0.5),
        "ffn2_w_out": nrm((L, F, C), F ** -0.5),
        "rwkv_mu": jax.random.uniform(next(ks), (NA, 6, C), jnp.float32),
        "rwkv_w_rkv": nrm((NA, C, 3 * C), C ** -0.5),
        "rwkv_w0": jax.random.uniform(next(ks), (NA, C), jnp.float32, -6.0, -0.5),
        "rwkv_w1": nrm((NA, C, LORA_DECAY), C ** -0.5),
        "rwkv_w2": nrm((NA, LORA_DECAY, C), 0.5 * LORA_DECAY ** -0.5),
        "rwkv_a0": nrm((NA, C), 0.1),
        "rwkv_a1": nrm((NA, C, LORA_AAA), C ** -0.5),
        "rwkv_a2": nrm((NA, LORA_AAA, C), 0.5 * LORA_AAA ** -0.5),
        "rwkv_g1": nrm((NA, C, LORA_GATE), C ** -0.5),
        "rwkv_g2": nrm((NA, LORA_GATE, C), LORA_GATE ** -0.5),
        "rwkv_k_k": gain((NA, C)),
        "rwkv_k_a": gain((NA, C)),
        "rwkv_r_k": nrm((NA, RWKV_HEADS, RWKV_HEAD), 0.1),
        "rwkv_ln_w": gain((NA, C)),
        "rwkv_ln_b": nrm((NA, C), 0.01),
        "rwkv_w_o": nrm((NA, C, C), C ** -0.5),
        "gmlp_w_uv": nrm((NB, C, 2 * GMLP_WIDTH), C ** -0.5),
        "gmlp_v_norm": gain((NB, GMLP_WIDTH)),
        "gmlp_w_s": nrm((NB, GMLP_GROUPS, GMLP_CHUNK, GMLP_CHUNK), 0.5 * GMLP_CHUNK ** -0.5),
        "gmlp_b_s": gain((NB, GMLP_GROUPS, GMLP_CHUNK)),
        "gmlp_w_o": nrm((NB, GMLP_WIDTH, C), GMLP_WIDTH ** -0.5),
        "final_norm": gain((C,)),
    }

def first_block(x, mem, mem_norm, mem_w_kv,
              ffn1_norm, ffn1_w_in, ffn1_w_out, mix_norm, xattn_norm, xattn_wq, xattn_wo,
              ffn2_norm, ffn2_w_in, ffn2_w_out,
              rwkv_mu, rwkv_w_rkv, rwkv_w0, rwkv_w1, rwkv_w2, rwkv_a0, rwkv_a1, rwkv_a2,
              rwkv_g1, rwkv_g2, rwkv_k_k, rwkv_k_a, rwkv_r_k, rwkv_ln_w, rwkv_ln_b, rwkv_w_o,
              gmlp_w_uv, gmlp_v_norm, gmlp_w_s, gmlp_b_s, gmlp_w_o,
              final_norm):
    B = mem.shape[0]
    mem_k, mem_v = jnp.split(rms_norm(mem, mem_norm) @ mem_w_kv, 2, axis=-1)
    mem_k = mem_k.reshape(B, N_MEM, XATTN_HEADS, XATTN_HEAD_DIM)
    mem_v = mem_v.reshape(B, N_MEM, XATTN_HEADS, XATTN_HEAD_DIM)

    for i in range(DEPTH):
        x = x + 0.5 * swiglu_ffn(rms_norm(x, ffn1_norm[i]), ffn1_w_in[i], ffn1_w_out[i])
        h = rms_norm(x, mix_norm[i])
        j = i // N_MIXERS
        if i % N_MIXERS == 0:
            y = rwkv7_time_mix(h, rwkv_mu[j], rwkv_w_rkv[j], rwkv_w0[j], rwkv_w1[j], rwkv_w2[j],
                               rwkv_a0[j], rwkv_a1[j], rwkv_a2[j], rwkv_g1[j], rwkv_g2[j],
                               rwkv_k_k[j], rwkv_k_a[j], rwkv_r_k[j], rwkv_ln_w[j], rwkv_ln_b[j],
                               rwkv_w_o[j])
        else:
            y = gmlp_chunk_mix(h, gmlp_w_uv[j], gmlp_v_norm[j], gmlp_w_s[j], gmlp_b_s[j], gmlp_w_o[j])
        x = x + y
        x = x + memory_cross_attention(rms_norm(x, xattn_norm[i]), mem_k, mem_v,
                                       xattn_wq[i], xattn_wo[i])
        x = x + 0.5 * swiglu_ffn(rms_norm(x, ffn2_norm[i]), ffn2_w_in[i], ffn2_w_out[i])
    return rms_norm(x, final_norm)


N_A_LAYERS = DEPTH // 2
N_B_LAYERS = DEPTH - N_A_LAYERS
A_HEADS = 8
A_KEY_DIM = 128
A_VAL_DIM = D_MODEL // A_HEADS
A_FORGET_DIM = A_HEADS * A_KEY_DIM
A_VAL_WIDTH = A_HEADS * A_VAL_DIM
A_IN_WIDTH = 2 * A_FORGET_DIM + 2 * A_VAL_WIDTH
A_CHUNK = 64
B_WINDOWS = (128, 512, 2048)
B_DILATIONS = (1, 4, 16)
B_GROUPS = 3
B_HEADS = 16
B_HEAD_DIM = D_MODEL // B_HEADS
B_QKV_WIDTH = B_GROUPS * B_HEADS * B_HEAD_DIM
B_BLOCK = 128
NUM_BUCKETS = 32
MAX_DISTANCE = 2048
EPS = 1e-6


def _rms(x, gain):
    xf = x.astype(jnp.float32)
    y = xf * lax.rsqrt(jnp.mean(xf * xf, axis=-1, keepdims=True) + EPS)
    return (y * gain.astype(jnp.float32)).astype(x.dtype)

def _swiglu(h, w_in, w_out):
    gate, up = jnp.split(h @ w_in, 2, axis=-1)
    return (jax.nn.silu(gate) * up) @ w_out

def _lower_bounds(lb_logits):
    p = jax.nn.softmax(lb_logits.astype(jnp.float32), axis=0)
    return jnp.cumsum(p, axis=0)[:-1]

def _hgrn2(h, w_in, lb, out_gain, w_out):
    bsz, seq, _ = h.shape
    n_chunks = seq // A_CHUNK
    f32 = jnp.float32
    q, f, i, g = jnp.split(h @ w_in, [A_FORGET_DIM, 2 * A_FORGET_DIM, 2 * A_FORGET_DIM + A_VAL_WIDTH], axis=-1)
    log_f = jnp.logaddexp(jnp.log(lb), jnp.log1p(-lb) + jax.nn.log_sigmoid(f.astype(f32)))
    k = -jnp.expm1(log_f)
    q = jax.nn.silu(q.astype(f32))
    v = i.astype(f32)

    def to_chunks(t, dh):
        return t.reshape(bsz, n_chunks, A_CHUNK, A_HEADS, dh).transpose(1, 0, 3, 2, 4)

    qc, kc, gc = (to_chunks(t, A_KEY_DIM) for t in (q, k, log_f))
    vc = to_chunks(v, A_VAL_DIM)
    causal = jnp.tril(jnp.ones((A_CHUNK, A_CHUNK), dtype=bool))

    def step(state, inp):
        qb, kb, vb, gb = inp
        cum = jnp.cumsum(gb, axis=2)
        rel = cum[:, :, :, None, :] - cum[:, :, None, :, :]
        decay = jnp.exp(jnp.where(causal[:, :, None], rel, -jnp.inf))
        scores = jnp.einsum('bhtd,bhtsd,bhsd->bhts', qb, decay, kb)
        out = (jnp.einsum('bhts,bhse->bhte', scores, vb)
               + jnp.einsum('bhtd,bhde->bhte', qb * jnp.exp(cum), state))
        last = cum[:, :, -1, :]
        state = (jnp.exp(last)[..., None] * state
                 + jnp.einsum('bhsd,bhse->bhde', kb * jnp.exp(last[:, :, None, :] - cum), vb))
        return state, out

    state0 = jnp.zeros((bsz, A_HEADS, A_KEY_DIM, A_VAL_DIM), f32)
    _, o = lax.scan(step, state0, (qc, kc, vc, gc))
    o = o.transpose(1, 0, 3, 2, 4).reshape(bsz, seq, A_HEADS, A_VAL_DIM)
    o = _rms(o, out_gain) * jax.nn.silu(g.astype(f32)).reshape(bsz, seq, A_HEADS, A_VAL_DIM)
    return o.reshape(bsz, seq, A_VAL_WIDTH).astype(h.dtype) @ w_out

def _t5_bucket(dist):
    dist = np.asarray(dist, np.int32)
    max_exact = NUM_BUCKETS // 2
    large = max_exact + (np.log(np.maximum(dist, 1) / max_exact)
                         / math.log(MAX_DISTANCE / max_exact) * (NUM_BUCKETS - max_exact)).astype(np.int32)
    large = np.minimum(large, NUM_BUCKETS - 1)
    return np.where(dist < max_exact, dist, large).astype(np.int32)

def _band_static(window, dilation):
    nq = B_BLOCK // dilation
    wd = window // dilation
    nj = wd + nq
    m = np.arange(nj)[None, :] - np.arange(nq)[:, None]
    band = (m >= 0) & (m <= wd)
    bucket = _t5_bucket((wd - np.clip(m, 0, wd)) * dilation)
    return band, bucket

def _shared_kv(x, kv_norm, w_kv, k_gain):
    bsz, seq, _ = x.shape
    kv = (_rms(x, kv_norm) @ w_kv).reshape(bsz, seq, 2, B_GROUPS, B_HEADS, B_HEAD_DIM)
    k = _rms(kv[:, :, 0], k_gain[:, None, :])
    v = kv[:, :, 1]
    k_pads = [jnp.pad(k[:, :, g], ((0, 0), (w, 0), (0, 0), (0, 0))) for g, w in enumerate(B_WINDOWS)]
    v_pads = [jnp.pad(v[:, :, g], ((0, 0), (w, 0), (0, 0), (0, 0))) for g, w in enumerate(B_WINDOWS)]
    return k_pads, v_pads

def _dilated_attention(h, w_q, q_gain, w_o, k_pads, v_pads, rel_bias):
    bsz, seq, _ = h.shape
    n_blocks = seq // B_BLOCK
    f32 = jnp.float32
    q = (h @ w_q).reshape(bsz, seq, B_GROUPS, B_HEADS, B_HEAD_DIM)
    q = _rms(q, q_gain[:, None, :]) * (B_HEAD_DIM ** -0.5)
    q_groups = [q[:, :, g] for g in range(B_GROUPS)]
    statics = [_band_static(w, d) for w, d in zip(B_WINDOWS, B_DILATIONS)]
    biases = [rel_bias[bucket][..., g * B_HEADS:(g + 1) * B_HEADS].transpose(2, 0, 1).astype(f32)
              for g, (_, bucket) in enumerate(statics)]

    def block(b):
        start = b * B_BLOCK
        outs, lses = [], []
        for g, (window, dil) in enumerate(zip(B_WINDOWS, B_DILATIONS)):
            band = statics[g][0]
            nq = B_BLOCK // dil
            nj = window // dil + nq
            qb = lax.dynamic_slice_in_dim(q_groups[g], start, B_BLOCK, axis=1).reshape(bsz, nq, dil, B_HEADS, B_HEAD_DIM)
            kb = lax.dynamic_slice_in_dim(k_pads[g], start, window + B_BLOCK, axis=1).reshape(bsz, nj, dil, B_HEADS, B_HEAD_DIM)
            vb = lax.dynamic_slice_in_dim(v_pads[g], start, window + B_BLOCK, axis=1).reshape(bsz, nj, dil, B_HEADS, B_HEAD_DIM)
            s = jnp.einsum('birhd,bjrhd->bhrij', qb, kb).astype(f32) + biases[g][None, :, None]
            pos = start - window + jnp.arange(nj)[:, None] * dil + jnp.arange(dil)[None, :]
            valid = band[None, :, :] & (pos.T >= 0)[:, None, :]
            s = jnp.where(valid[None, None], s, -jnp.inf)
            lse = jax.nn.logsumexp(s, axis=-1)
            p = jnp.exp(s - lse[..., None]).astype(vb.dtype)
            o = jnp.einsum('bhrij,bjrhd->birhd', p, vb).reshape(bsz, B_BLOCK, B_HEADS, B_HEAD_DIM)
            outs.append(o.astype(f32))
            lses.append(lse.transpose(0, 3, 2, 1).reshape(bsz, B_BLOCK, B_HEADS))
        wts = jax.nn.softmax(jnp.stack(lses), axis=0)
        o = jnp.einsum('gbqh,gbqhd->bqhd', wts, jnp.stack(outs))
        return o.reshape(bsz, B_BLOCK, B_HEADS * B_HEAD_DIM).astype(h.dtype)

    o = lax.map(block, jnp.arange(n_blocks))
    o = o.transpose(1, 0, 2, 3).reshape(bsz, seq, B_HEADS * B_HEAD_DIM)
    return o @ w_o

def second_inputs(seed: int = 0) -> dict:
    key = jax.random.key(seed)
    ks = jax.random.split(key, 16)

    def dense(k, shape, fan_in):
        return jax.random.normal(k, shape, jnp.float32) * fan_in ** -0.5

    def gain(k, shape):
        return 1.0 + 0.1 * jax.random.normal(k, shape, jnp.float32)

    return {
        'x': jax.random.normal(ks[0], (BATCH, SEQ, D_MODEL), jnp.float32),
        'norm_gain': gain(ks[1], (DEPTH, 3, D_MODEL)),
        'ffn_w_in': dense(ks[2], (DEPTH, 2, D_MODEL, 2 * D_FF), D_MODEL),
        'ffn_w_out': dense(ks[3], (DEPTH, 2, D_FF, D_MODEL), D_FF),
        'a_w_in': dense(ks[4], (N_A_LAYERS, D_MODEL, A_IN_WIDTH), D_MODEL),
        'a_lb_logits': 0.5 * jax.random.normal(ks[5], (N_A_LAYERS + 1, A_FORGET_DIM), jnp.float32),
        'a_out_gain': gain(ks[6], (N_A_LAYERS, A_VAL_DIM)),
        'a_w_out': dense(ks[7], (N_A_LAYERS, A_VAL_WIDTH, D_MODEL), A_VAL_WIDTH),
        'kv_norm': gain(ks[8], (D_MODEL,)),
        'w_kv': dense(ks[9], (D_MODEL, 2 * B_QKV_WIDTH), D_MODEL),
        'k_gain': gain(ks[10], (B_GROUPS, B_HEAD_DIM)),
        'b_w_q': dense(ks[11], (N_B_LAYERS, D_MODEL, B_QKV_WIDTH), D_MODEL),
        'b_q_gain': gain(ks[12], (N_B_LAYERS, B_GROUPS, B_HEAD_DIM)),
        'b_w_o': dense(ks[13], (N_B_LAYERS, B_HEADS * B_HEAD_DIM, D_MODEL), B_HEADS * B_HEAD_DIM),
        'rel_bias': 0.5 * jax.random.normal(ks[14], (NUM_BUCKETS, B_GROUPS * B_HEADS), jnp.float32),
    }

def second_block(x, norm_gain, ffn_w_in, ffn_w_out, a_w_in, a_lb_logits, a_out_gain, a_w_out,
              kv_norm, w_kv, k_gain, b_w_q, b_q_gain, b_w_o, rel_bias):
    lower_bounds = _lower_bounds(a_lb_logits)
    k_pads, v_pads = None, None
    for layer in range(DEPTH):
        if layer == N_A_LAYERS:
            k_pads, v_pads = _shared_kv(x, kv_norm, w_kv, k_gain)
        x = x + 0.5 * _swiglu(_rms(x, norm_gain[layer, 0]), ffn_w_in[layer, 0], ffn_w_out[layer, 0])
        h = _rms(x, norm_gain[layer, 1])
        if layer < N_A_LAYERS:
            x = x + _hgrn2(h, a_w_in[layer], lower_bounds[layer], a_out_gain[layer], a_w_out[layer])
        else:
            j = layer - N_A_LAYERS
            x = x + _dilated_attention(h, b_w_q[j], b_q_gain[j], b_w_o[j], k_pads, v_pads, rel_bias)
        x = x + 0.5 * _swiglu(_rms(x, norm_gain[layer, 2]), ffn_w_in[layer, 1], ffn_w_out[layer, 1])
    return x


def setup_inputs(seed=0):
    out = dict(first_inputs(seed))
    for name, value in second_inputs(seed + 1).items():
        if name != "x":
            out[name + "_2"] = value
    return out


def reference(
    x, mem, mem_norm, mem_w_kv, ffn1_norm, ffn1_w_in, ffn1_w_out, mix_norm, xattn_norm,
    xattn_wq, xattn_wo, ffn2_norm, ffn2_w_in, ffn2_w_out, rwkv_mu, rwkv_w_rkv, rwkv_w0, rwkv_w1,
    rwkv_w2, rwkv_a0, rwkv_a1, rwkv_a2, rwkv_g1, rwkv_g2, rwkv_k_k, rwkv_k_a, rwkv_r_k,
    rwkv_ln_w, rwkv_ln_b, rwkv_w_o, gmlp_w_uv, gmlp_v_norm, gmlp_w_s, gmlp_b_s, gmlp_w_o,
    final_norm, norm_gain_2, ffn_w_in_2, ffn_w_out_2, a_w_in_2, a_lb_logits_2, a_out_gain_2,
    a_w_out_2, kv_norm_2, w_kv_2, k_gain_2, b_w_q_2, b_q_gain_2, b_w_o_2, rel_bias_2,
):
    x = first_block(
        x, mem, mem_norm, mem_w_kv, ffn1_norm, ffn1_w_in, ffn1_w_out, mix_norm, xattn_norm,
        xattn_wq, xattn_wo, ffn2_norm, ffn2_w_in, ffn2_w_out, rwkv_mu, rwkv_w_rkv, rwkv_w0,
        rwkv_w1, rwkv_w2, rwkv_a0, rwkv_a1, rwkv_a2, rwkv_g1, rwkv_g2, rwkv_k_k, rwkv_k_a,
        rwkv_r_k, rwkv_ln_w, rwkv_ln_b, rwkv_w_o, gmlp_w_uv, gmlp_v_norm, gmlp_w_s, gmlp_b_s,
        gmlp_w_o, final_norm,
    )
    return second_block(
        x, norm_gain_2, ffn_w_in_2, ffn_w_out_2, a_w_in_2, a_lb_logits_2, a_out_gain_2,
        a_w_out_2, kv_norm_2, w_kv_2, k_gain_2, b_w_q_2, b_q_gain_2, b_w_o_2, rel_bias_2,
    )


_drawn_inputs = setup_inputs


def setup_inputs(seed=0):
    import zlib

    import numpy as np

    out = dict(_drawn_inputs(seed))
    spreads = {}
    factors = {'mem_norm': 4.624,
     'xattn_norm': 7.285,
     'rwkv_w1': 3.633,
     'rwkv_w2': 3.595,
     'rwkv_k_k': 2.846,
     'rwkv_ln_b': 6.795,
     'gmlp_v_norm': 5.664,
     'k_gain_2': 4.108,
     'b_q_gain_2': 3.857}
    for name, (base, spread) in spreads.items():
        noise = np.random.default_rng([zlib.crc32(name.encode()), seed]).standard_normal(out[name].shape)
        drawn = base * np.exp(spread * noise) if base else spread * noise
        out[name] = __import__('jax').numpy.asarray(drawn.astype(out[name].dtype))
    for name, factor in factors.items():
        out[name] = (out[name] * factor).astype(out[name].dtype)
    return out
```

```python
from contextlib import ExitStack
import math

import numpy as np
import concourse.bass as bass
from concourse import mybir

F32 = mybir.dt.float32
F32R = mybir.dt.float32r
I32 = mybir.dt.int32
ALU = mybir.AluOpType
ACT = mybir.ActivationFunctionType
AX = mybir.AxisListType

P = 128
T = 256
D = 1024
NC = D // P
F = 2816
FC = F // P
RING = 4
WIDE = FC // 2
EPS = 1e-6
KB = 1024
POOL_TILES = {8: 5, 11: 7}


class Steps:

    def __init__(self, sem, counts):
        self.sem, self.counts, self.n = sem, counts, 0

    def done(self, ins, label):
        ins.then_inc(self.sem, 1)
        self.n += 1
        self.counts[label] = self.n

    def wait(self, eng, label):
        eng.wait_ge(self.sem, self.counts.get(label, 1))


class Stage:

    def __init__(self, name, tiles, per_tile, width):
        self.name, self.tiles, self.per_tile, self.width = name, tiles, per_tile, width
        self.slabs = tiles * per_tile
        self.iters = self.slabs // RING
        assert self.slabs % RING == 0


def pack_columns(names_and_widths):
    at, out = 0, {}
    for name, width in names_and_widths:
        out[name] = at
        at += width // P
    return out, at


VECTORS = (
    [("mem_norm", D), ("final_norm", D), ("kv_norm", D)]
    + [(f"{n}{l}", D) for l in range(2) for n in ("ffn1_norm", "mix_norm", "xattn_norm", "ffn2_norm")]
    + [(f"norm_gain{l}{j}", D) for l in range(2) for j in range(3)]
    + [(f"mu{j}", D) for j in range(6)]
    + [(n, D) for n in ("w0", "a0", "k_k", "k_a", "r_k", "ln_w", "ln_b", "lb0", "lb1")]
    + [("v_norm", 2 * D), ("a_out_gain", P), ("k_gain", 3 * P), ("q_gain", 3 * P)]
)
COL, N_COLS = pack_columns(VECTORS)

LORA_W, LORA_A, LORA_G = 64, 64, 160
CHUNK = 64
HEAD = 64
GROUPS = 3
WINDOWS, DILATIONS = (128, 512, 2048), (1, 4, 16)
BUCKETS, MAX_DISTANCE = 32, 2048
REACH = 3 * P
NEG = -1e30


def square_masks():
    r, c = np.arange(P)[:, None], np.arange(P)[None, :]
    same = r // CHUNK == c // CHUNK
    m = {"identity": r == c, "ones": r + c >= 0, "head_ones": same,
         "strict": same & (r < c), "incl": same & (r <= c), "causal": r <= c}
    for lv in range(6):
        b = 1 << lv
        m[f"pair{lv}"] = (r // (2 * b) == c // (2 * b)) & (r % (2 * b) < b) & (c % (2 * b) >= b)
    m["pair0_lower"] = m["pair0"].T
    m["reset"] = (r >= 0) & (c % CHUNK > 0)
    m["pair6"] = (r < CHUNK) & (c >= CHUNK)
    return m


def column_masks():
    low = (np.arange(P) < CHUNK).astype(np.float32)
    cols = [low, 1 - low, -low, low - 1, np.full(P, EPS), np.full(P, 64e-5), np.ones(P)]
    return np.stack(cols, 1).astype(np.float32)


LOW, HIGH, NEG_LOW, NEG_HIGH, C_EPS, C_GN_EPS, C_ONE = range(7)
MASKS = ["identity", "ones", "head_ones", "strict", "incl", "causal"] + [f"pair{lv}" for lv in range(7)] + ["pair0_lower", "reset"]


def bias_constants():
    dist = T - 1 - np.arange(REACH)
    d = np.maximum(dist, 0)
    exact = BUCKETS // 2
    large = exact + (np.log(np.maximum(d, 1) / exact) / math.log(MAX_DISTANCE / exact) * (BUCKETS - exact)).astype(np.int32)
    bucket = np.where(d < exact, d, np.minimum(large, BUCKETS - 1))
    table = np.zeros((BUCKETS + GROUPS, REACH), np.float32)
    table[bucket, np.arange(REACH)] = 1.0
    table[:BUCKETS, dist < 0] = 0.0
    for g in range(GROUPS):
        ok = (dist >= 0) & (dist <= WINDOWS[g]) & (dist % DILATIONS[g] == 0)
        table[BUCKETS + g] = np.where(ok, 0.0, NEG)
    pick = np.kron(np.eye(GROUPS), np.ones((1, 16))).astype(np.float32)
    return table, pick


def plan(blocks):
    st = []
    for b in blocks:
        if b.startswith("ffn"):
            st.append(Stage(f"ffn_in{b[3]}", 2 * FC, 1, 8))
            st.append(Stage(f"ffn_out{b[3]}", NC, 2, WIDE))
        elif b == "mem":
            st.append(Stage("mem_kv", 2 * NC, 1, 8))
        elif b == "rwkv":
            st.extend(Stage(f"rwkv_{x}", NC, 1, 8) for x in "rkv")
            if "mem" in blocks:
                st.append(Stage("mem_kv", 2 * NC, 1, 8))
            st.append(Stage("rwkv_o", NC, 1, 8))
        elif b.startswith("xattn"):
            st.extend(Stage(f"{b}_{x}", NC, 1, 8) for x in "qo")
        elif b == "gmlp":
            st.append(Stage("gmlp_uv", 4 * NC, 1, 8))
            st.append(Stage("gmlp_o", NC, 2, 8))
        elif b == "hgrn":
            st.extend(Stage(f"hgrn_{x}", NC, 1, 8) for x in "qfigo")
        elif b == "kv":
            st.extend(Stage(f"dil_{x}", 3 * NC, 1, 8) for x in "kv")
        elif b == "dil":
            st.append(Stage("dil_q", 3 * NC, 1, 8))
            st.append(Stage("dil_o", NC, 1, 8))
    seen, out = set(), []
    for s in st:
        if s.name not in seen:
            seen.add(s.name)
            out.append(s)
    base, row = 0, {8: 0, WIDE: 0}
    for s in out:
        s.base, s.row = base, row[s.width]
        base += s.slabs
        row[s.width] += s.slabs
    for s, nxt in zip(out, out[1:] + [None]):
        s.ahead = nxt.width if nxt else 0
    return out, base, row


BLOCKS = ["ffn0", "rwkv", "mem", "xattn0", "ffn1", "ffn2", "gmlp", "xattn1", "ffn3", "final",
          "ffn4", "hgrn", "ffn5", "kv", "ffn6", "dil", "ffn7"]
GAIN_OF = {"ffn0": "ffn1_norm0", "rwkv": "mix_norm0", "xattn0": "xattn_norm0", "ffn1": "ffn2_norm0",
           "ffn2": "ffn1_norm1", "gmlp": "mix_norm1", "xattn1": "xattn_norm1", "ffn3": "ffn2_norm1",
           "ffn4": "norm_gain00", "hgrn": "norm_gain01", "ffn5": "norm_gain02", "kv": "kv_norm",
           "ffn6": "norm_gain10", "dil": "norm_gain11", "ffn7": "norm_gain12"}

UNSPLIT = ("final_norm", "mix_norm0")


def run(eng, stage, body):
    full = stage.iters if stage.ahead == stage.width else stage.iters - 1
    if full > 1:
        with eng.Fori(0, full) as i:
            body(i, stage.width)
    elif full == 1:
        body(0, stage.width)
    if full < stage.iters:
        body(stage.iters - 1, stage.ahead)


def bcast(ap, n):
    return ap.unsqueeze(1).broadcast_to([P, n, ap.shape[-1]])


class Resources:

    def __init__(self, nc, ctx, io, counts):
        self.nc, self.io = nc, io

        def sb(name, shape, dt=F32):
            return ctx.enter_context(nc.sbuf_tensor(name, shape, dt))

        def sem(name):
            return ctx.enter_context(nc.semaphore(name))

        self.raw = sb("raw", [P, RING, WIDE * P])
        self.hi = sb("hi", [P, RING, WIDE * P], F32R)
        self.lo = sb("lo", [P, RING, WIDE * P], F32R)
        self.X = sb("X", [P, NC, T])
        self.R = sb("R", [P, T])
        self.STD = sb("STD", [P, T])
        self.SQSUM = sb("SQSUM", [P, T])
        self.SQ = sb("SQ", [P, 2, T])
        self.vec = sb("vec", [P, N_COLS])
        self.cols = sb("cols", [P, 7])
        self.masks = sb("masks", [P, len(MASKS), P])
        self.sel = sb("sel", [P, NC * 16])
        self.base = -(-nc.sbuf_base // 64) * 64
        self.room = nc.sbuf_usable_end - self.base
        self.arena = sb("arena", [P, (self.room - 128) // 4])
        self.limit = self.room - 128

        self.Hh = self.at("Hh", 0, [P, NC, T], F32R)
        self.Hl = self.at("Hl", 8 * KB, [P, NC, T], F32R)
        self.memk = self.at("memk", 16 * KB, [P, NC, T])
        self.memv = self.at("memv", 24 * KB, [P, 2, D])
        self.gate = self.at("gate", 32 * KB, [P, 2, T])
        self.sgate = self.at("sgate", 34 * KB, [P, 2, T])
        self.up = self.at("up", 36 * KB, [P, 2, T])
        self.act32 = self.at("act32", 38 * KB, [P, 2, T])
        self.A0 = 40 * KB
        self.Ah = self.at("Ah", self.A0, [P, FC, T], F32R)
        self.Al = self.at("Al", self.A0 + 22 * KB, [P, FC, T], F32R)

        self.bank = [ctx.enter_context(nc.psum_tensor(f"bank{b}", [P, 512], F32)) for b in range(8)]

        self.ident, self.ones, self.head_ones = self.mask("identity"), self.mask("ones"), self.mask("head_ones")

        self.landed = [sem(f"slab_landed{q}") for q in range(RING)]
        self.hi_ready = sem("hi_ready")
        self.lo_pool = sem("lo_ready_pool")
        self.lo_dve = sem("lo_ready_dve")
        self.slab_used = sem("slab_used")
        self.banks_freed = sem("banks_freed")
        self.h_hi, self.h_lo = sem("h_hi_ready"), sem("h_lo_ready")
        self.sq_ready, self.sq_added = sem("square_ready"), sem("square_added")
        self.ss_ready, self.std_ready, self.rstd_ready = sem("sumsq_ready"), sem("std_ready"), sem("rstd_ready")
        self.gate_scaled, self.silu_done = sem("gate_scaled"), sem("silu_done")
        self.a_ready, self.ah_ready, self.al_ready = sem("a_ready"), sem("ah_ready"), sem("al_ready")
        self.gelu_done = sem("gelu_done")
        self.proj_act = sem("projection_activated")
        self.loaded = sem("small_loads")
        self.mem_loaded = sem("mem_loaded")
        self.x_scaled = sem("x_scaled")
        self.mixer_loads = sem("mixer_loads")
        self.mixer_stores = sem("mixer_stores")
        self.values_stored = [sem(f"values_stored{q}") for q in range(4)]
        self.pair_loaded = [sem(f"pair_loaded{q}") for q in range(2)]
        self.out_stored = sem("out_stored")
        self.pe_done = Steps(sem("mixer_products"), counts.setdefault("mixer_products", {}))
        self.act_done = Steps(sem("mixer_activations"), counts.setdefault("mixer_activations", {}))
        self.dve_done = Steps(sem("mixer_vectors"), counts.setdefault("mixer_vectors", {}))
        self.pool_done = Steps(sem("mixer_pool"), counts.setdefault("mixer_pool", {}))

        self.loads_before = 0

    def at(self, name, offset, shape, dt=F32):
        size = 4 * int(np.prod(shape[1:]))
        assert offset + size <= self.limit, (name, offset, size, self.limit)
        return self.nc.alloc_sbuf_tensor_at(name, shape, dt, offset=self.base + offset)

    def mask(self, name, n=1):
        i = MASKS.index(name)
        return self.masks[:, i, :] if n == 1 else self.masks[:, i:i + n, :]

    def v1(self, name, c):
        return self.vec[:, COL[name] + c:COL[name] + c + 1]

    def col(self, i):
        return self.cols[:, i:i + 1]


class Shared:

    def __init__(self, k, blocks):
        self.k, self.blocks = k, blocks
        self.stages, self.n_slabs, self.rows = plan(blocks)
        self.stage = {s.name: s for s in self.stages}
        self.split_n = {"act": 0, "dve": 0, "pe": 0}
        self.square_n = {"act": 0, "dve": 0, "pe": 0}
        self.norm_n = {"act": 0, "dve": 0, "pe": 0}

    def act_hi(self, act, s, q, width, turn):
        k, w = self.k, width * P
        if not width:
            return
        act.wait_ge(k.landed[q], 16 * (turn + 1))
        if not (isinstance(s, int) and s < RING):
            act.wait_ge(k.slab_used, s - (RING - 1))
        act.activation(k.hi[:, q, :w], k.raw[:, q, :w], ACT.Copy).then_inc(k.hi_ready, 1)

    def dve_lo(self, dve, s, q, width):
        k = self.k
        if not width:
            return
        a, w = POOL_TILES[width] * P, width * P
        dve.wait_ge(k.hi_ready, s + 1)
        dve.tensor_tensor(k.lo[:, q, a:w], k.raw[:, q, a:w], k.hi[:, q, a:w].bitcast(F32),
                          ALU.subtract).then_inc(k.lo_dve, 1)

    def pool_lo(self, pool, s, q, width):
        k = self.k
        if not width:
            return
        a = POOL_TILES[width] * P
        pool.wait_ge(k.hi_ready, s + 1)
        pool.tensor_tensor(k.lo[:, q, :a], k.raw[:, q, :a], k.hi[:, q, :a].bitcast(F32),
                           ALU.subtract).then_inc(k.lo_pool, 1)

    def sp_stage(self, sp, st):
        k = self.k
        src, w = (k.io["w8"], 8 * P) if st.width == 8 else (k.io["w11"], WIDE * P)

        def body(i, _):
            for q in range(RING):
                s = st.base + RING * i + q
                if not (isinstance(s, int) and s < RING):
                    sp.wait_ge(k.lo_pool, s - (RING - 1))
                    sp.wait_ge(k.lo_dve, s - (RING - 1))
                sp.dma_start(k.raw[:, q, :w], src[bass.ds(st.row + RING * i + q, 1), :, :].rearrange(
                    "a p w -> p (a w)")).then_inc(k.landed[q], 16)

        first = 1 if st.base == 0 else 0
        if first:
            body(0, 0)
        if st.iters - first > 1:
            with sp.Fori(first, st.iters) as i:
                body(i, 0)
        elif st.iters > first:
            body(first, 0)

    def pool_stage(self, pool, st):
        def body(i, ahead):
            for q in range(RING):
                self.pool_lo(pool, st.base + RING * i + q + RING, q, ahead)
        run(pool, st, body)

    def act_stage(self, act, st, follow=None):
        k = self.k

        def body(i, ahead):
            for q in range(RING):
                if follow:
                    follow(i, q)
                self.act_hi(act, st.base + RING * i + q + RING, q, ahead, st.base // RING + i + 1)
        run(act, st, body)

    def pe_stage(self, pe, st, moving, ready):
        k = self.k
        with pe.Fori(0, st.iters) as i:
            for q in range(RING):
                s, kg = st.base + RING * i + q, q % st.per_tile
                pe.wait_ge(k.lo_pool, s + 1)
                pe.wait_ge(k.lo_dve, s + 1)
                if kg == 0:
                    pe.wait_ge(k.banks_freed, s + 1)
                out = k.bank[q - kg][:, :T]
                for kc in range(st.width):
                    if q < st.per_tile:
                        ready(kg, kc)
                    xh, xl = moving(kg, kc)
                    wh, wl = (w[:, q, kc * P:(kc + 1) * P] for w in (k.hi, k.lo))
                    first, last = kg == kc == 0, kg == st.per_tile - 1 and kc == st.width - 1
                    pe.matmul(out, wh, xh, start=first, stop=False)
                    pe.matmul(out, wh, xl, start=False, stop=False)
                    mm = pe.matmul(out, wl, xh, start=False, stop=last)
                mm.then_inc(k.slab_used, 1)

    def pe_stage_h(self, pe, st):
        k, n = self.k, self.split_n["pe"] - NC
        self.pe_stage(pe, st, lambda kg, kc: (k.Hh[:, kc, :], k.Hl[:, kc, :]),
                      lambda kg, kc: pe.wait_ge(k.h_lo, n + kc + 1))

    def dve_project(self, dve, st, dest, scaled=True, before=None):
        k = self.k
        if scaled:
            dve.wait_ge(k.rstd_ready, self.norm_n["dve"])

        def body(i, ahead):
            for q in range(RING):
                s = st.base + RING * i + q
                dve.wait_ge(k.slab_used, s + 1)
                if before:
                    before(i, q)
                if scaled:
                    ins = dve.tensor_tensor(dest(i, q), k.bank[q][:, :T], k.R[:], ALU.mult)
                else:
                    ins = dve.tensor_copy(dest(i, q), k.bank[q][:, :T])
                ins.then_inc(k.banks_freed, 1)
                self.dve_lo(dve, s + RING, q, ahead)
        run(dve, st, body)

    def prep(self, eng, e, src, gain, c, split=True, square=True, wait=None):
        k = self.k
        ns, nq = self.split_n[e] + c, self.square_n[e] + c
        if e == "act":
            if wait:
                wait(c)
            if split:
                eng.activation(k.Hh[:, c, :], src[:, c, :], ACT.Copy, scale=k.v1(gain, c)).then_inc(k.h_hi, 1)
            if square:
                if nq >= 2:
                    eng.wait_ge(k.sq_added, nq - 1)
                eng.activation(k.SQ[:, c % 2, :], src[:, c, :], ACT.Square).then_inc(k.sq_ready, 1)
        else:
            if split:
                eng.wait_ge(k.h_hi, ns + 1)
                eng.scalar_tensor_tensor(k.Hl[:, c, :], src[:, c, :], k.v1(gain, c),
                                         k.Hh[:, c, :].bitcast(F32), ALU.mult, ALU.subtract).then_inc(k.h_lo, 1)
            if square:
                eng.wait_ge(k.sq_ready, nq + 1)
                if c == 0:
                    if self.norm_n["dve"]:
                        eng.wait_ge(k.ss_ready, self.norm_n["dve"])
                    ins = eng.tensor_copy(k.SQSUM[:], k.SQ[:, 0, :])
                else:
                    eng.wait_ge(k.sq_added, nq)
                    ins = eng.tensor_tensor(k.SQSUM[:], k.SQSUM[:], k.SQ[:, c % 2, :], ALU.add)
                ins.then_inc(k.sq_added, 1)

    def prep_all(self, eng, e, src, gain, split=True, square=True, wait=None):
        for c in range(NC):
            self.prep(eng, e, src, gain, c, split, square, wait)
        self.prepped(e, split, square)

    def prepped(self, e, split=True, square=True):
        self.split_n[e] += NC * split
        self.square_n[e] += NC * square

    def act_resid(self, act, st, gain):
        k, split = self.k, gain not in UNSPLIT
        for c in range(NC):
            s = st.base + c * st.per_tile
            if gain:
                self.prep(act, "act", k.X, gain, c, split,
                          wait=lambda _: act.wait_ge(k.banks_freed, RING + s + st.per_tile))
            for kg in range(st.per_tile):
                w = st.width if s + kg + RING < st.base + st.slabs else st.ahead
                self.act_hi(act, s + kg + RING, (s + kg) % RING, w, (s + kg) // RING + 1)
        if gain:
            self.prepped("act", split)

    def dve_resid(self, dve, st, coef, gain):
        k, split = self.k, gain not in UNSPLIT
        for c in range(NC):
            s = st.base + c * st.per_tile
            dve.wait_ge(k.slab_used, s + st.per_tile)
            dve.scalar_tensor_tensor(k.X[:, c, :], k.bank[s % RING][:, :T], coef, k.X[:, c, :],
                                     ALU.mult, ALU.add).then_inc(k.banks_freed, st.per_tile)
            if gain:
                dve.wait_ge(k.banks_freed, RING + s + st.per_tile)
                self.prep(dve, "dve", k.X, gain, c, split)
            for kg in range(st.per_tile):
                w = st.width if s + kg + RING < st.base + st.slabs else st.ahead
                self.dve_lo(dve, s + kg + RING, (s + kg) % RING, w)
        if gain:
            self.prepped("dve", split)

    def norm(self, eng, e):
        k, n = self.k, self.norm_n[e]
        if e == "pe":
            self.square_n["pe"] += NC
            eng.wait_ge(k.sq_added, self.square_n["pe"])
            eng.matmul(k.bank[4][:, :T], k.ones, k.SQSUM[:], start=True, stop=True).then_inc(k.ss_ready, 1)
        elif e == "act":
            eng.wait_ge(k.ss_ready, n + 1)
            if n:
                eng.wait_ge(k.rstd_ready, n)
            eng.activation(k.STD[:], k.bank[4][:, :T], ACT.Sqrt, bias=k.col(C_EPS), scale=1.0 / D).then_inc(k.std_ready, 1)
        else:
            eng.wait_ge(k.std_ready, n + 1)
            eng.reciprocal(k.R[:], k.STD[:]).then_inc(k.rstd_ready, 1)
        self.norm_n[e] += 1


class FeedForward:

    def __init__(self, sh, name, order, nxt, own_norm=True):
        self.sh, self.k, self.n, self.next_gain, self.own_norm = sh, sh.k, order, nxt, own_norm
        self.st_in, self.st_out = sh.stage[f"ffn_in{name[3]}"], sh.stage[f"ffn_out{name[3]}"]

    def pe(self, pe):
        sh, k = self.sh, self.k
        if self.own_norm:
            sh.norm(pe, "pe")
        sh.split_n["pe"] += NC
        sh.pe_stage_h(pe, self.st_in)
        done = 2 + FC * self.n
        sh.pe_stage(pe, self.st_out,
                    lambda kg, kc: (k.Ah[:, kg * WIDE + kc, :], k.Al[:, kg * WIDE + kc, :]),
                    lambda kg, kc: pe.wait_ge(k.al_ready, done + WIDE * (kg + 1)) if kc == 0 else None)

    def act(self, act):
        sh, k, st = self.sh, self.k, self.st_in
        if self.own_norm:
            sh.norm(act, "act")

        def body(i, ahead):
            for j in range(2):
                m, s = 2 * i + j, st.base + RING * i + 2 * j
                g = FC * self.n + m
                turn = st.base // RING + i + 1
                act.wait_ge(k.gate_scaled, g + 1)
                act.wait_ge(k.a_ready, g + 1)
                act.activation(k.sgate[:, j, :], k.gate[:, j, :], ACT.Silu).then_inc(k.silu_done, 1)
                sh.act_hi(act, s + RING, 2 * j, ahead, turn)
                act.wait_ge(k.a_ready, g + 3)
                act.activation(k.Ah[:, bass.ds(m, 1), :].rearrange("p a t -> p (a t)"), k.act32[:, j, :],
                               ACT.Copy).then_inc(k.ah_ready, 1)
                sh.act_hi(act, s + 1 + RING, 2 * j + 1, ahead, turn)
        run(act, st, body)
        sh.act_resid(act, self.st_out, self.next_gain)

    def dve(self, dve):
        sh, k, st = self.sh, self.k, self.st_in
        if self.own_norm:
            sh.norm(dve, "dve")
        dve.wait_ge(k.rstd_ready, sh.norm_n["dve"])

        def body(i, ahead):
            for j in range(2):
                m, s = 2 * i + j, st.base + RING * i + 2 * j
                g = FC * self.n + m
                dve.wait_ge(k.slab_used, s + 1)
                dve.wait_ge(k.silu_done, g + 1)
                dve.tensor_tensor(k.gate[:, j, :], k.bank[2 * j][:, :T], k.R[:], ALU.mult).then_inc(k.gate_scaled, 1)
                dve.wait_ge(k.slab_used, s + 2)
                dve.wait_ge(k.a_ready, g + 1)
                dve.tensor_tensor(k.up[:, j, :], k.bank[2 * j + 1][:, :T], k.R[:], ALU.mult).then_inc(k.banks_freed, 2)
                sh.dve_lo(dve, s + RING, 2 * j, ahead)
                dve.wait_ge(k.silu_done, g + 3)
                dve.wait_ge(k.banks_freed, RING + s + 2)
                dve.wait_ge(k.al_ready, g + 1)
                dve.tensor_tensor(k.act32[:, j, :], k.sgate[:, j, :], k.up[:, j, :], ALU.mult).then_inc(k.a_ready, 1)
                dve.wait_ge(k.ah_ready, g + 1)
                dve.wait_ge(k.a_ready, g + 3)
                dve.tensor_tensor(k.Al[:, bass.ds(m, 1), :].rearrange("p a t -> p (a t)"), k.act32[:, j, :],
                                  k.Ah[:, bass.ds(m, 1), :].rearrange("p a t -> p (a t)").bitcast(F32),
                                  ALU.subtract).then_inc(k.al_ready, 1)
                sh.dve_lo(dve, s + 1 + RING, 2 * j + 1, ahead)
        run(dve, st, body)
        sh.dve_resid(dve, self.st_out, 0.5, self.next_gain)

    def stage_list(self):
        return [self.st_in, self.st_out]

    def pool(self, pool):
        for st in self.stage_list():
            self.sh.pool_stage(pool, st)


class Memory:

    def __init__(self, sh):
        self.sh, self.k, self.st = sh, sh.k, sh.stage["mem_kv"]
        k = sh.k
        self.M = k.at("mem_x", k.A0, [P, NC, T])
        self.VT = k.at("mem_vt", k.A0 + 8 * KB, [P, NC, T])

    def pe(self, pe):
        sh, k = self.sh, self.k
        sh.norm(pe, "pe")
        sh.split_n["pe"] += NC
        sh.pe_stage_h(pe, self.st)
        for b in range(4):
            pe.wait_ge(k.banks_freed, RING + self.st.base + NC + 2 * b + 2)
            for j in range(4):
                c, half = 2 * b + j // 2, j % 2
                ins = pe.transpose(k.bank[4 + b][:, j * P:(j + 1) * P], self.VT[:, c, half * P:(half + 1) * P], k.ident)
            k.pe_done.done(ins, f"mem.vt{b}")

    def act(self, act):
        sh, k = self.sh, self.k
        sh.prep_all(act, "act", self.M, "mem_norm", wait=lambda _: act.wait_ge(k.mem_loaded, 16))
        sh.norm(act, "act")
        sh.act_stage(act, self.st)
        for b in range(4):
            k.pe_done.wait(act, f"mem.vt{b}")
            src = k.bank[4 + b][:].rearrange("p (c h j) -> p c h j", c=2, h=2)
            dst = k.memv[:, :, 2 * b * P:(2 * b + 2) * P].rearrange("p h (c j) -> p c h j", c=2)
            k.act_done.done(act.activation(dst, src, ACT.Copy), f"mem.v{b}")

    def dve(self, dve):
        sh, k = self.sh, self.k
        dve.wait_ge(k.mem_loaded, 16)
        sh.prep_all(dve, "dve", self.M, "mem_norm")
        sh.norm(dve, "dve")

        dve.wait_ge(k.rstd_ready, sh.norm_n["dve"])
        for s in range(self.st.slabs):
            at, q = self.st.base + s, s % RING
            out = (k.memk if s < NC else self.VT)[:, s % NC, :]
            dve.wait_ge(k.slab_used, at + 1)
            dve.tensor_tensor(out, k.bank[q][:, :T], k.R[:], ALU.mult).then_inc(k.banks_freed, 1)
            sh.dve_lo(dve, at + RING, q, self.st.width if s + RING < self.st.slabs else self.st.ahead)

    def pool(self, pool):
        self.sh.pool_stage(pool, self.st)


class CrossAttention:
    HEADS, DH = 4, 256

    def __init__(self, sh, name, nxt):
        self.sh, self.k, self.name, self.next_gain = sh, sh.k, name, nxt
        self.sq, self.so = sh.stage[f"{name}_q"], sh.stage[f"{name}_o"]
        k = sh.k
        a, n = k.A0, name
        self.Q = k.at(n + "Q", a, [P, NC, T])
        self.Oh = k.at(n + "Oh", a + 8 * KB, [P, NC, T], F32R)
        self.Ol = k.at(n + "Ol", a + 16 * KB, [P, NC, T], F32R)
        self.E = k.at(n + "E", a + 24 * KB, [P, 2, 2, T])
        self.ET = k.at(n + "ET", a + 28 * KB, [P, 2, 2 * T])
        self.st = k.at(n + "st", a + 32 * KB, [P, 4, 4, 2])

    def pe(self, pe):
        sh, k, n = self.sh, self.k, self.name
        sh.norm(pe, "pe")
        sh.split_n["pe"] += NC
        sh.pe_stage_h(pe, self.sq)

        def scores(h):
            pe.wait_ge(k.banks_freed, RING + self.sq.base + 2 * h + 2)
            if h == 0:
                pe.wait_ge(k.rstd_ready, sh.norm_n["pe"])
                k.act_done.wait(pe, "mem.v3")
            if h >= 2:
                k.act_done.wait(pe, f"{n}.exp{h - 2}")
            for half in range(2):
                for c in range(2):
                    ins = pe.matmul(k.bank[4 + h % 2][:, half * T:(half + 1) * T],
                                    self.Q[:, 2 * h + c, half * P:(half + 1) * P], k.memk[:, 2 * h + c, :],
                                    start=c == 0, stop=c == 1)
            k.pe_done.done(ins, f"{n}.s{h}")

        scores(0)
        for h in range(self.HEADS):
            if h + 1 < self.HEADS:
                scores(h + 1)
            k.dve_done.wait(pe, f"{n}.p{h}")
            if h:
                k.act_done.wait(pe, f"{n}.et{h - 1}")
            for slots in range(2):
                for half in range(2):
                    j = 2 * slots + half
                    ins = pe.transpose(k.bank[6][:, j * P:(j + 1) * P],
                                       self.E[:, h % 2, half, slots * P:(slots + 1) * P], k.ident)
            k.pe_done.done(ins, f"{n}.t{h}")
            k.act_done.wait(pe, f"{n}.et{h}")
            if h:
                k.dve_done.wait(pe, f"{n}.ol{h - 1}")
            for c in range(2):
                for slots in range(2):
                    f = h * self.DH + c * P
                    ins = pe.matmul(k.bank[7][:, c * T:(c + 1) * T], k.memv[:, slots, f:f + P],
                                    self.ET[:, h % 2, slots * T:(slots + 1) * T], start=slots == 0, stop=slots == 1)
            k.pe_done.done(ins, f"{n}.o{h}")
        sh.pe_stage(pe, self.so, lambda kg, kc: (self.Oh[:, kc, :], self.Ol[:, kc, :]),
                    lambda kg, kc: k.dve_done.wait(pe, f"{n}.ol{kc // 2}"))

    def act(self, act):
        sh, k, n = self.sh, self.k, self.name
        sh.norm(act, "act")
        sh.act_stage(act, self.sq)
        for h in range(self.HEADS):
            k.dve_done.wait(act, f"{n}.nmax{h}")
            if h >= 2:
                k.pe_done.wait(act, f"{n}.t{h - 2}")
            for half in range(2):
                ins = act.activation(self.E[:, h % 2, half, :], k.bank[4 + h % 2][:, half * T:(half + 1) * T], ACT.Exp,
                                     bias=self.st[:, h, 1, half:half + 1], scale=1.0 / 16,
                                     accum_out=self.st[:, h, 2, half:half + 1])
                k.act_done.done(ins, f"{n}.exp{h}")
            k.pe_done.wait(act, f"{n}.t{h}")
            if h >= 2:
                k.pe_done.wait(act, f"{n}.o{h - 2}")
            k.act_done.done(act.activation(self.ET[:, h % 2, :], k.bank[6][:], ACT.Copy), f"{n}.et{h}")
            k.pe_done.wait(act, f"{n}.o{h}")
            out = self.Oh[:, 2 * h:2 * h + 2, :].rearrange("p c t -> p (c t)")
            k.act_done.done(act.activation(out, k.bank[7][:], ACT.Copy), f"{n}.oh{h}")
        sh.act_resid(act, self.so, self.next_gain)

    def dve(self, dve):
        sh, k, n = self.sh, self.k, self.name
        sh.norm(dve, "dve")
        sh.dve_project(dve, self.sq, lambda i, q: self.Q[:, bass.ds(RING * i + q, 1), :].rearrange("p a t -> p (a t)"))

        def maximum(h):
            k.pe_done.wait(dve, f"{n}.s{h}")
            src = k.bank[4 + h % 2][:].rearrange("p (b m) -> p b m", b=2)
            k.dve_done.done(dve.tensor_reduce(self.st[:, h, 0, :], src, AX.X, ALU.max), f"{n}.max{h}")
            k.dve_done.wait(dve, f"{n}.max{h}")
            k.dve_done.done(dve.tensor_scalar(self.st[:, h, 1, :], self.st[:, h, 0, :], -1.0 / 16, None, ALU.mult), f"{n}.nmax{h}")

        maximum(0)
        for h in range(self.HEADS):
            if h + 1 < self.HEADS:
                maximum(h + 1)
            k.act_done.wait(dve, f"{n}.exp{h}")
            k.dve_done.done(dve.reciprocal(self.st[:, h, 3, :], self.st[:, h, 2, :]), f"{n}.rs{h}")
            k.dve_done.wait(dve, f"{n}.rs{h}")
            for half in range(2):
                e = self.E[:, h % 2, half, :]
                k.dve_done.done(dve.tensor_scalar(e, e, self.st[:, h, 3, half:half + 1], None, ALU.mult), f"{n}.p{h}")
            k.act_done.wait(dve, f"{n}.oh{h}")
            k.dve_done.done(dve.tensor_tensor(self.Ol[:, 2 * h:2 * h + 2, :].rearrange("p c t -> p (c t)"), k.bank[7][:],
                                              self.Oh[:, 2 * h:2 * h + 2, :].rearrange("p c t -> p (c t)").bitcast(F32),
                                              ALU.subtract), f"{n}.ol{h}")
        sh.dve_resid(dve, self.so, 1.0, self.next_gain)

    def pool(self, pool):
        self.sh.pool_stage(pool, self.sq)
        self.sh.pool_stage(pool, self.so)


class GatedMlp:
    G = 16

    def __init__(self, sh, name, nxt):
        self.sh, self.k, self.next_gain = sh, sh.k, nxt
        self.uv, self.so = sh.stage["gmlp_uv"], sh.stage["gmlp_o"]
        k, a = sh.k, sh.k.A0
        self.UV = k.at("gUV", a, [P, 2 * self.G, T])
        self.U, self.V = self.UV[:, :self.G, :], self.UV[:, self.G:, :]
        self.Gh = k.at("gGh", a + 16 * KB, [P, self.G, T], F32R)
        self.VT = k.at("gVT", a + 32 * KB, [P, 2 * self.G, P])
        self.WS = k.at("gWS", a + 48 * KB, [P, self.G, P])
        self.BS = k.at("gBS", a + 56 * KB, [P, self.G, P])
        self.TMP = k.at("gTMP", a + 64 * KB, [P, 4, T])
        self.SQ = k.at("gSQ", a + 68 * KB, [P, 4, T])
        self.Gl = k.at("gGl", a + 64 * KB, [P, self.G - 4, T], F32R)
        self.Gl2 = k.at("gGl2", 36 * KB, [P, 4, T], F32R)
        self.T2 = k.at("gT2", 32 * KB, [P, 2, 2, T])

        self.loads = 32 + k.loads_before
        k.loads_before += 32

    def low(self, g, n):
        return self.Gl[:, g:g + n, :] if g < 12 else self.Gl2[:, g - 12:g - 12 + n, :]

    def pe(self, pe):
        sh, k, G = self.sh, self.k, self.G
        sh.norm(pe, "pe")
        sh.split_n["pe"] += NC
        sh.pe_stage_h(pe, self.uv)
        for j in range(4):
            k.act_done.wait(pe, f"g.sq{j}")
            if j == 0:
                pe.wait_ge(k.rstd_ready, sh.norm_n["pe"])
            for c in range(4):
                ins = pe.matmul(k.bank[4][:, :T], k.ones, self.SQ[:, c, :], start=j == c == 0, stop=j == c == 3)
            k.pe_done.done(ins, f"g.ss{j}")
        for b in range(8):
            k.dve_done.wait(pe, f"g.vn{2 * b + 1}")
            if b >= 4:
                k.act_done.wait(pe, f"g.vt{b - 4}")
            for j in range(4):
                g, chunk = 2 * b + j // 2, j % 2
                ins = pe.transpose(k.bank[b % 4][:, j * P:(j + 1) * P], self.V[:, g, chunk * P:(chunk + 1) * P], k.ident)
            k.pe_done.done(ins, f"g.vt{b}")
        k.dve_done.wait(pe, "g.ws")
        for b in range(8):
            k.act_done.wait(pe, f"g.vt{b}")
            if b >= 4:
                k.dve_done.wait(pe, f"g.sv{b - 4}")
            else:
                k.act_done.wait(pe, "g.std")
            for j in range(4):
                g, chunk = 2 * b + j // 2, j % 2
                ins = pe.matmul(k.bank[4 + b % 4][:, j * P:(j + 1) * P], self.VT[:, 2 * g + chunk, :],
                                self.WS[:, g, :], start=True, stop=True)
            k.pe_done.done(ins, f"g.sv{b}")
        sh.pe_stage(pe, self.so, lambda kg, kc: (self.Gh[:, 8 * kg + kc, :], self.low(8 * kg + kc, 1)[:, 0, :]),
                    lambda kg, kc: k.dve_done.wait(pe, f"g.gl{(8 * kg + kc) // 2}"))

    def act(self, act):
        sh, k, st = self.sh, self.k, self.uv
        act.dma_start(self.WS[:], k.io["ws"]).then_inc(k.mixer_loads, 16)
        act.dma_start(self.BS[:], k.io["bs"].partition_broadcast(P)).then_inc(k.mixer_loads, 16)
        sh.norm(act, "act")

        def follow(i, q):
            act.wait_ge(k.banks_freed, RING + st.base + RING * i + q + 1)
            out = self.UV[:, bass.ds(RING * i + q, 1), :].rearrange("p a t -> p (a t)")
            act.activation(out, self.TMP[:, q, :], ACT.Gelu_apprx_tanh).then_inc(k.gelu_done, 1)
        sh.act_stage(act, st, follow)
        act.wait_ge(k.gelu_done, RING + st.slabs)
        for j in range(4):
            if j:
                k.pe_done.wait(act, f"g.ss{j - 1}")
            k.act_done.done(act.activation(self.SQ[:], self.V[:, 4 * j:4 * j + 4, :], ACT.Square), f"g.sq{j}")
        k.pe_done.wait(act, "g.ss3")
        k.act_done.done(act.activation(k.STD[:], k.bank[4][:, :T], ACT.Sqrt, bias=k.col(C_EPS),
                                       scale=1.0 / (2 * D)), "g.std")
        for b in range(8):
            k.pe_done.wait(act, f"g.vt{b}")
            out = self.VT[:, 4 * b:4 * b + 4, :].rearrange("p a d -> p (a d)")
            k.act_done.done(act.activation(out, k.bank[b % 4][:], ACT.Copy), f"g.vt{b}")
        for b in range(8):
            k.dve_done.wait(act, f"g.usv{b}")
            k.act_done.done(act.activation(self.Gh[:, 2 * b:2 * b + 2, :], self.U[:, 2 * b:2 * b + 2, :], ACT.Copy), f"g.gh{b}")
        sh.act_resid(act, self.so, self.next_gain)

    def dve(self, dve):
        sh, k, st = self.sh, self.k, self.uv
        sh.norm(dve, "dve")
        dve.wait_ge(k.mixer_loads, self.loads)
        causal = bcast(k.mask("causal"), self.G)
        k.dve_done.done(dve.tensor_tensor(self.WS[:], self.WS[:], causal, ALU.mult), "g.ws")
        sh.dve_project(dve, st, lambda i, q: self.TMP[:, q, :],
                       before=lambda i, q: dve.wait_ge(k.gelu_done, RING * i + q + 1))
        k.act_done.wait(dve, "g.std")
        k.dve_done.done(dve.reciprocal(k.R[:], k.STD[:]), "g.r")
        k.dve_done.wait(dve, "g.r")
        for g in range(self.G):
            v = self.V[:, g, :]
            k.dve_done.done(dve.scalar_tensor_tensor(v, v, k.v1("v_norm", g), k.R[:], ALU.mult, ALU.mult), f"g.vn{g}")
        for b in range(8):
            k.pe_done.wait(dve, f"g.sv{b}")
            ps = k.bank[4 + b % 4][:].rearrange("p (g c t) -> p g c t", g=2, c=2)
            bs = self.BS[:, 2 * b:2 * b + 2, :].unsqueeze(2).broadcast_to([P, 2, 2, P])
            tmp = self.T2[:, b % 2, :, :].rearrange("p g (c t) -> p g c t", c=2)
            if b >= 2:
                k.dve_done.wait(dve, f"g.usv{b - 2}")
            k.dve_done.done(dve.tensor_tensor(tmp, ps, bs, ALU.add), f"g.sv{b}")
            u = self.U[:, 2 * b:2 * b + 2, :]
            k.dve_done.wait(dve, f"g.sv{b}")
            k.dve_done.done(dve.tensor_tensor(u, u, self.T2[:, b % 2, :, :], ALU.mult), f"g.usv{b}")
            k.act_done.wait(dve, f"g.gh{b}")
            k.dve_done.wait(dve, f"g.usv{b}")
            k.dve_done.done(dve.tensor_tensor(self.low(2 * b, 2), u,
                                              self.Gh[:, 2 * b:2 * b + 2, :].bitcast(F32), ALU.subtract), f"g.gl{b}")
        sh.dve_resid(dve, self.so, 1.0, self.next_gain)

    def pool(self, pool):
        self.sh.pool_stage(pool, self.uv)
        self.sh.pool_stage(pool, self.so)


class FinalNorm:

    def __init__(self, sh, name, nxt):
        self.sh, self.k, self.next_gain = sh, sh.k, nxt

    def pe(self, pe):
        self.sh.norm(pe, "pe")

    def act(self, act):
        k = self.k
        self.sh.norm(act, "act")
        self.sh.prep_all(act, "act", k.X, self.next_gain, wait=lambda c: act.wait_ge(k.x_scaled, c + 1))

    def dve(self, dve):
        k = self.k
        self.sh.norm(dve, "dve")
        dve.wait_ge(k.rstd_ready, self.sh.norm_n["dve"])
        for c in range(NC):
            dve.scalar_tensor_tensor(k.X[:, c, :], k.X[:, c, :], k.v1("final_norm", c), k.R[:],
                                     ALU.mult, ALU.mult).then_inc(k.x_scaled, 1)
        dve.wait_ge(k.x_scaled, NC)
        self.sh.prep_all(dve, "dve", k.X, self.next_gain)

    def pool(self, pool):
        pass


class Hgrn2:
    H = 8

    def __init__(self, sh, name, nxt):
        self.sh, self.k, self.next_gain = sh, sh.k, nxt
        k, a = sh.k, sh.k.A0

        def big(n, offset, dt=F32):
            return k.at("h" + n, offset, [P, NC, T], dt)
        self.Q, self.CUM, self.K, self.V, self.G = (big(n, a + 8 * KB * j) for j, n in enumerate(("Q", "CUM", "K", "V", "G")))
        self.VT = k.at("hVT", a + 40 * KB, [P, 2, D])
        self.Y = big("Y", a + 48 * KB)
        self.LV = [big("LV0", a + 56 * KB), big("LV1", a + 64 * KB), big("LV2", 16 * KB)]
        self.S = k.at("hS", 24 * KB, [P, 2 * self.H, P])
        self.SX = k.at("hSX", 32 * KB, [P, self.H, P])
        self.C = k.at("hC", 36 * KB, [P, 8, NC])
        self.Oh, self.Ol = big("Oh", a + 8 * KB, F32R), big("Ol", a + 16 * KB, F32R)
        self.LEVELS = [6, 5, 4, 3, 2, 1, 0]

    def pe(self, pe):
        sh, k, H = self.sh, self.k, self.H
        sh.norm(pe, "pe")
        sh.split_n["pe"] += NC
        for x in "qfig":
            sh.pe_stage_h(pe, sh.stage[f"hgrn_{x}"])
        for b in range(4):
            pe.wait_ge(k.banks_freed, RING + sh.stage["hgrn_g"].base)
            if b == 0:
                pe.wait_ge(k.rstd_ready, sh.norm_n["pe"])
            for j in range(4):
                c, half = 2 * b + j // 2, j % 2
                ins = pe.transpose(k.bank[4 + b][:, j * P:(j + 1) * P], self.V[:, c, half * P:(half + 1) * P], k.ident)
            k.pe_done.done(ins, f"h.vt{b}")

        n = 0

        def gram(label, left, right, count):
            nonlocal n
            for b in range(count // 4):
                bank = 4 * (n % 2) + b
                if n >= 2:
                    k.dve_done.wait(pe, f"h.take{n - 2}.{b}")
                elif n == 1:
                    k.act_done.wait(pe, f"h.vt{b}")
                else:
                    pe.wait_ge(k.banks_freed, RING + sh.stage["hgrn_g"].base + NC)
                for j in range(4):
                    ins = pe.matmul(k.bank[bank][:, j * P:(j + 1) * P], left(4 * b + j), right(4 * b + j),
                                    start=True, stop=True)
                k.pe_done.done(ins, f"h.gram{n}.{b}")
            n += 1

        for lv in self.LEVELS:
            a = self.LV[n % 3]
            k.dve_done.wait(pe, f"h.lv{n}")
            half = lambda u: a[:, u // 2, (u % 2) * P:(u % 2 + 1) * P]
            gram(n, half, half, 2 * H)
        gram(n, lambda u: self.K[:, u // 2, (u % 2) * P:(u % 2 + 1) * P],
             lambda u: self.Q[:, u // 2, (u % 2) * P:(u % 2 + 1) * P], 2 * H)
        k.dve_done.wait(pe, f"h.lv{n}")
        a = self.LV[n % 3]
        gram(n, lambda u: a[:, u, :P], lambda u: a[:, u, P:], H)
        last = n - 1
        for b in range(4):
            bank = k.bank[4 + b]
            if b == 0:
                for j in range(4):
                    k.dve_done.wait(pe, f"h.take{last - 1}.{j}")
                for j in range(2):
                    k.dve_done.wait(pe, f"h.take{last}.{j}")
                for j in range(4):
                    k.act_done.wait(pe, f"h.vt{j}")
            for j in range(2):
                h = 2 * b + j
                v0, v1 = self.VT[:, 0, h * P:(h + 1) * P], self.VT[:, 1, h * P:(h + 1) * P]
                o0, o1 = bank[:, j * T:j * T + P], bank[:, j * T + P:(j + 1) * T]
                pe.matmul(o0, v0, self.S[:, 2 * h, :], start=True, stop=True)
                pe.matmul(o1, v0, self.SX[:, h, :], start=True, stop=False)
                ins = pe.matmul(o1, v1, self.S[:, 2 * h + 1, :], start=False, stop=True)
            k.pe_done.done(ins, f"h.o{b}")
        for b in range(4):
            k.act_done.wait(pe, f"h.osq{b}")
            for j in range(2):
                ins = pe.matmul(k.bank[b][:, j * T:(j + 1) * T], k.ones, self.LV[0][:, 2 * b + j, :], start=True, stop=True)
            k.pe_done.done(ins, f"h.oss{b}")
        sh.pe_stage(pe, sh.stage["hgrn_o"], lambda kg, kc: (self.Oh[:, kc, :], self.Ol[:, kc, :]),
                    lambda kg, kc: k.dve_done.wait(pe, "h.ol"))

    def act(self, act):
        sh, k = self.sh, self.k
        d = lambda ins, label: k.act_done.done(ins, label)
        sh.norm(act, "act")
        C = self.C
        k.dve_done.wait(act, "h.lbd")
        d(act.activation(C[:, 2:4, :], C[:, 0:2, :], ACT.Exp), "h.lbe")
        for x in "qfig":
            st = sh.stage[f"hgrn_{x}"]
            if x in "qg":
                dst = self.Q if x == "q" else self.G

                def follow(i, q, st=st, dst=dst):
                    act.wait_ge(k.banks_freed, RING + st.base + RING * i + q + 1)
                    a = dst[:, bass.ds(RING * i + q, 1), :].rearrange("p a t -> p (a t)")
                    act.activation(a, a, ACT.Silu).then_inc(k.proj_act, 1)
                sh.act_stage(act, st, follow)
            else:
                sh.act_stage(act, st)
        for b in range(4):
            k.pe_done.wait(act, f"h.vt{b}")
            dst = self.VT[:, :, 2 * b * P:(2 * b + 2) * P].rearrange("p h (c j) -> p c h j", c=2)
            d(act.activation(dst, k.bank[4 + b][:].rearrange("p (c h j) -> p c h j", c=2, h=2), ACT.Copy), f"h.vt{b}")
        d(act.activation(self.LV[0][:], self.CUM[:], ACT.Sigmoid), "h.sig")
        d(act.activation(self.K[:], self.CUM[:], ACT.Sigmoid, scale=-1.0), "h.nsig")
        k.dve_done.wait(act, "h.f7")
        d(act.activation(self.LV[1][:], self.LV[0][:], ACT.Ln), "h.lnf")
        for n, lv in enumerate(self.LEVELS):
            b = 1 << lv
            v = self.LV[n % 3][:].rearrange("p c (n b) -> p (c n) b", b=2 * b)
            k.dve_done.wait(act, f"h.d{n}")
            d(act.activation(v[:, :, b:], v[:, :, b:], ACT.Exp), f"h.er{n}")
            d(act.activation(v[:, :, :b], v[:, :, :b], ACT.Exp, scale=-1.0), f"h.el{n}")
        n = len(self.LEVELS) + 1
        a = self.LV[n % 3]
        k.dve_done.wait(act, f"h.d{n}")
        d(act.activation(a[:, :, P:], self.CUM[:, :, P:], ACT.Exp), f"h.er{n}")
        d(act.activation(a[:, :, :P], a[:, :, :P], ACT.Exp, scale=-1.0), f"h.el{n}")
        for b in range(4):
            k.pe_done.wait(act, f"h.o{b}")
            sl = slice(2 * b, 2 * b + 2)
            ps = k.bank[4 + b][:].rearrange("p (h t) -> p h t", h=2)
            d(act.activation(self.Y[:, sl, :], ps, ACT.Copy), f"h.y{b}")
            d(act.activation(self.LV[0][:, sl, :], ps, ACT.Square), f"h.osq{b}")
        for b in range(4):
            k.pe_done.wait(act, f"h.oss{b}")
            sl = slice(2 * b, 2 * b + 2)
            ps = k.bank[b][:].rearrange("p (h t) -> p h t", h=2)
            d(act.activation(self.LV[1][:, sl, :], ps, ACT.Sqrt, bias=k.col(C_EPS), scale=1.0 / P), f"h.ostd{b}")
        k.dve_done.wait(act, "h.o32")
        d(act.activation(self.Oh[:], self.Y[:], ACT.Copy), "h.oh")
        sh.act_resid(act, sh.stage["hgrn_o"], self.next_gain)

    def dve(self, dve):
        sh, k, H, C = self.sh, self.k, self.H, self.C

        def d(ins, label):
            k.dve_done.done(ins, label)
            k.dve_done.wait(dve, label)
        sh.norm(dve, "dve")
        l0, l1 = (k.vec[:, COL[n]:COL[n] + NC] for n in ("lb0", "lb1"))
        d(dve.tensor_tensor(C[:, 4, :], l0, l1, ALU.max), "h.lbm")
        d(dve.tensor_tensor(C[:, 0, :], l0, C[:, 4, :], ALU.subtract), "h.lb0")
        d(dve.tensor_tensor(C[:, 1, :], l1, C[:, 4, :], ALU.subtract), "h.lbd")
        k.act_done.wait(dve, "h.lbe")
        d(dve.tensor_tensor(C[:, 4, :], C[:, 2, :], C[:, 3, :], ALU.add), "h.lbs")
        d(dve.reciprocal(C[:, 5, :], C[:, 4, :]), "h.lbr")
        d(dve.tensor_tensor(C[:, 6, :], C[:, 2, :], C[:, 5, :], ALU.mult), "h.lbu")
        d(dve.tensor_scalar(C[:, 6, :], C[:, 6, :], 1.2e-38, None, ALU.max), "h.lb")
        d(dve.tensor_tensor(C[:, 7, :], C[:, 3, :], C[:, 5, :], ALU.mult), "h.olb")
        for x, dst in zip("qfig", (self.Q, self.CUM, self.V, self.G)):
            sh.dve_project(dve, sh.stage[f"hgrn_{x}"],
                           lambda i, q, dst=dst: dst[:, bass.ds(RING * i + q, 1), :].rearrange("p a t -> p (a t)"))
        k.act_done.wait(dve, "h.sig")
        for h in range(H):
            s = self.LV[0][:, h, :]
            k.dve_done.done(dve.tensor_scalar(s, s, C[:, 7, h:h + 1], C[:, 6, h:h + 1], ALU.mult, ALU.add), f"h.f{h}")
        k.act_done.wait(dve, "h.nsig")
        for h in range(H):
            s = self.K[:, h, :]
            k.dve_done.done(dve.tensor_scalar(s, s, C[:, 7, h:h + 1], None, ALU.mult), f"h.k{h}")
        k.act_done.wait(dve, "h.lnf")
        for h in range(H):
            for half in range(2):
                sl = slice(half * P, (half + 1) * P)
                k.dve_done.done(dve.tensor_tensor_scan(self.CUM[:, h, sl], k.ones, self.LV[1][:, h, sl], 0.0,
                                                       ALU.mult, ALU.add), f"h.cum{h}.{half}")
        k.dve_done.wait(dve, f"h.cum{H - 1}.1")
        dve.wait_ge(k.proj_act, 2 * NC)

        def view(t, b):
            return t[:].rearrange("p c (n b) -> p (c n) b", b=2 * b)

        def subtract(n, lv):
            b = 1 << lv
            a, cum = view(self.LV[n % 3], b), view(self.CUM, b)
            if n >= 3:
                k.pe_done.wait(dve, f"h.gram{n - 3}.3")
            ref = cum[:, :, b - 1:b].broadcast_to([P, cum.shape[1], 2 * b])
            k.dve_done.done(dve.tensor_tensor(a, cum, ref, ALU.subtract), f"h.d{n}")

        def multiply(n, lv):
            b = 1 << lv
            a, q, kk = view(self.LV[n % 3], b), view(self.Q, b), view(self.K, b)
            k.act_done.wait(dve, f"h.er{n}")
            k.dve_done.done(dve.tensor_tensor(a[:, :, b:], a[:, :, b:], q[:, :, b:], ALU.mult), f"h.lvr{n}")
            k.act_done.wait(dve, f"h.el{n}")
            k.dve_done.done(dve.tensor_tensor(a[:, :, :b], a[:, :, :b], kk[:, :, :b], ALU.mult), f"h.lv{n}")

        def take(n, name):
            for b in range(4):
                k.pe_done.wait(dve, f"h.gram{n}.{b}")
                ps = k.bank[4 * (n % 2) + b][:].rearrange("p (u t) -> p u t", u=4)
                out, m = self.S[:, 4 * b:4 * b + 4, :], bcast(k.mask(name), 4)
                if n == 0:
                    ins = dve.tensor_tensor(out, ps, m, ALU.mult)
                else:
                    k.dve_done.wait(dve, f"h.take{n - 1}.{b}")
                    ins = dve.copy_predicated(out, m.bitcast(I32), ps)
                k.dve_done.done(ins, f"h.take{n}.{b}")

        L = self.LEVELS
        subtract(0, L[0])
        for n, lv in enumerate(L):
            if n + 1 < len(L):
                subtract(n + 1, L[n + 1])
            multiply(n, lv)
            if n:
                take(n - 1, f"pair{L[n - 1]}")
        n = len(L)
        a = self.LV[(n + 1) % 3]
        k.pe_done.wait(dve, f"h.gram{n - 2}.3")
        ref = self.CUM[:, :, P - 1:P].broadcast_to([P, NC, P])
        k.dve_done.done(dve.tensor_tensor(a[:, :, :P], self.CUM[:, :, :P], ref, ALU.subtract), f"h.d{n + 1}")
        take(n - 1, f"pair{L[-1]}")
        take(n, "identity")
        k.act_done.wait(dve, f"h.el{n + 1}")
        k.dve_done.done(dve.tensor_tensor(a[:, :, P:], a[:, :, P:], self.Q[:, :, P:], ALU.mult), f"h.lvr{n + 1}")
        k.dve_done.done(dve.tensor_tensor(a[:, :, :P], a[:, :, :P], self.K[:, :, :P], ALU.mult), f"h.lv{n + 1}")
        for b in range(2):
            k.pe_done.wait(dve, f"h.gram{n + 1}.{b}")
            ps = k.bank[4 * ((n + 1) % 2) + b][:].rearrange("p (u t) -> p u t", u=4)
            k.dve_done.done(dve.tensor_copy(self.SX[:, 4 * b:4 * b + 4, :], ps), f"h.take{n + 1}.{b}")
        for b in range(4):
            k.act_done.wait(dve, f"h.y{b}")
            sl = slice(2 * b, 2 * b + 2)
            d(dve.scalar_tensor_tensor(self.Y[:, sl, :], self.Y[:, sl, :], k.v1("a_out_gain", 0), self.G[:, sl, :],
                                       ALU.mult, ALU.mult), f"h.yg{b}")
        for b in range(4):
            sl = slice(2 * b, 2 * b + 2)
            k.act_done.wait(dve, f"h.ostd{b}")
            d(dve.reciprocal(self.LV[1][:, sl, :], self.LV[1][:, sl, :]), f"h.or{b}")
        d(dve.tensor_tensor(self.Y[:], self.Y[:], self.LV[1][:], ALU.mult), "h.o32")
        k.act_done.wait(dve, "h.oh")
        k.dve_done.done(dve.tensor_tensor(self.Ol[:], self.Y[:], self.Oh[:].bitcast(F32), ALU.subtract), "h.ol")
        sh.dve_resid(dve, sh.stage["hgrn_o"], 1.0, self.next_gain)

    def pool(self, pool):
        for x in "qfigo":
            self.sh.pool_stage(pool, self.sh.stage[f"hgrn_{x}"])


class DilatedKeys:

    def __init__(self, sh, name, nxt):
        self.sh, self.k, self.next_gain = sh, sh.k, nxt
        k, a = sh.k, sh.k.A0
        nc = k.nc
        self.K = k.at("dK", a, [P, 3 * NC, T])
        self.V = k.at("dV", a + 24 * KB, [P, 3 * NC, T])
        self.SQ = k.at("dSQ", a + 48 * KB, [P, NC, T])
        self.SD = k.at("dSD", a + 56 * KB, [P, NC, T])
        self.VS = k.at("dVS", a + 64 * KB, [P, 4, 2, 2 * P])
        self.BT = k.at("dBT", a + 72 * KB, [BUCKETS + GROUPS, REACH])
        self.BL = k.at("dBL", a + 72 * KB + 1536, [BUCKETS + GROUPS, 48])
        self.BR = k.at("dBR", a + 72 * KB + 1792, [48, REACH])
        k.dil_k = nc.dram_tensor("dil_keys", (P, 3 * NC, T), F32).ap()
        k.dil_v = nc.dram_tensor("dil_values", (P, 2, 3 * D), F32).ap()
        k.dil_b = nc.dram_tensor("dil_bias", (48, REACH), F32).ap()
        self.loads = 32 + k.loads_before
        k.loads_before += 32
        self.stores = 16 * (1 + GROUPS)

    def pe(self, pe):
        sh, k = self.sh, self.k
        sh.norm(pe, "pe")
        sh.split_n["pe"] += NC
        for x in "kv":
            sh.pe_stage_h(pe, sh.stage[f"dil_{x}"])
        v = sh.stage["dil_v"]
        pe.wait_ge(k.mixer_loads, self.loads)
        pe.wait_ge(k.rstd_ready, sh.norm_n["pe"])
        k.pe_done.done(pe.matmul(k.bank[7][:48, :REACH], self.BL[:], self.BT[:], start=True, stop=True), "kv.bias")
        for g in range(GROUPS):
            k.act_done.wait(pe, f"kv.sq{g}")
            for b in range(4):
                if g == 0:
                    pe.wait_ge(k.banks_freed, RING + v.base + v.slabs)
                else:
                    k.act_done.wait(pe, f"kv.std{g - 1}.{b}")
                for j in range(2):
                    ins = pe.matmul(k.bank[b][:, j * T:(j + 1) * T], k.head_ones, self.SQ[:, 2 * b + j, :],
                                    start=True, stop=True)
                k.pe_done.done(ins, f"kv.ss{g}.{b}")
        for b in range(12):
            if b == 3:
                k.act_done.wait(pe, "kv.bias")
            if b >= 4:
                k.dve_done.wait(pe, f"kv.vt{b - 4}")
            for j in range(4):
                c, half = 2 * b + j // 2, j % 2
                ins = pe.transpose(k.bank[4 + b % 4][:, j * P:(j + 1) * P], self.V[:, c, half * P:(half + 1) * P], k.ident)
            k.pe_done.done(ins, f"kv.vt{b}")

    def act(self, act):
        sh, k = self.sh, self.k
        act.dma_start(self.BT[:], k.io["bias_table"]).then_inc(k.mixer_loads, 16)
        act.dma_start(self.BL[:], k.io["bias_rows"]).then_inc(k.mixer_loads, 16)
        sh.norm(act, "act")
        sk, sv = sh.stage["dil_k"], sh.stage["dil_v"]
        sh.act_stage(act, sk)
        sh.act_stage(act, sv)
        k.pe_done.wait(act, "kv.bias")
        k.act_done.done(act.activation(self.BR[:], k.bank[7][:48, :REACH], ACT.Copy), "kv.bias")
        k.act_done.wait(act, "kv.bias")
        act.dma_start(k.dil_b, self.BR[:]).then_inc(k.mixer_stores, 16)
        for g in range(GROUPS):
            if g == 0:
                act.wait_ge(k.banks_freed, RING + sk.base + sk.slabs)
            else:
                k.pe_done.wait(act, f"kv.ss{g - 1}.3")
            k.act_done.done(act.activation(self.SQ[:], self.K[:, NC * g:NC * (g + 1), :], ACT.Square), f"kv.sq{g}")
            if g:
                k.dve_done.wait(act, f"kv.k{g - 1}")
                act.dma_start(k.dil_k[:, NC * (g - 1):NC * g, :], self.K[:, NC * (g - 1):NC * g, :]).then_inc(k.mixer_stores, 16)
            for b in range(4):
                k.pe_done.wait(act, f"kv.ss{g}.{b}")
                k.act_done.done(act.activation(self.SD[:, 2 * b:2 * b + 2, :], k.bank[b][:].rearrange("p (c t) -> p c t", c=2),
                                               ACT.Sqrt, bias=k.col(C_EPS), scale=1.0 / HEAD), f"kv.std{g}.{b}")
        k.dve_done.wait(act, "kv.k2")
        act.dma_start(k.dil_k[:, 2 * NC:, :], self.K[:, 2 * NC:, :]).then_inc(k.mixer_stores, 16)
        for b in range(12):
            k.dve_done.wait(act, f"kv.vt{b}")
            act.dma_start(k.dil_v[:, :, 2 * b * P:(2 * b + 2) * P], self.VS[:, b % 4, :, :]).then_inc(k.values_stored[b % 4], 16)
        sh.prep_all(act, "act", k.X, self.next_gain, square=False,
                    wait=lambda c: act.wait_ge(k.slab_used, sv.base + sv.slabs))
        act.wait_ge(k.mixer_stores, self.stores)
        for q in range(4):
            act.wait_ge(k.values_stored[q], 16 * 3)

    def dve(self, dve):
        sh, k = self.sh, self.k
        sh.norm(dve, "dve")
        for x, dst in (("k", self.K), ("v", self.V)):
            sh.dve_project(dve, sh.stage[f"dil_{x}"],
                           lambda i, q, dst=dst: dst[:, bass.ds(RING * i + q, 1), :].rearrange("p a t -> p (a t)"))
        for g in range(GROUPS):
            for b in range(4):
                k.act_done.wait(dve, f"kv.std{g}.{b}")
                sl = self.SD[:, 2 * b:2 * b + 2, :]
                k.dve_done.done(dve.reciprocal(sl, sl), f"kv.r{g}.{b}")
            k.dve_done.wait(dve, f"kv.r{g}.3")
            kk = self.K[:, NC * g:NC * (g + 1), :]
            k.dve_done.done(dve.scalar_tensor_tensor(kk, kk, k.v1("k_gain", g), self.SD[:], ALU.mult, ALU.mult), f"kv.k{g}")
        for b in range(12):
            k.pe_done.wait(dve, f"kv.vt{b}")
            if b >= 4:
                dve.wait_ge(k.values_stored[b % 4], 16 * (b // 4))
            dst = self.VS[:, b % 4, :, :].rearrange("p h (c j) -> p c h j", c=2)
            k.dve_done.done(dve.tensor_copy(dst, k.bank[4 + b % 4][:].rearrange("p (c h j) -> p c h j", c=2, h=2)), f"kv.vt{b}")
        sh.prep_all(dve, "dve", k.X, self.next_gain, square=False)

    def pool(self, pool):
        for x in "kv":
            self.sh.pool_stage(pool, self.sh.stage[f"dil_{x}"])


class DilatedAttention:
    BLOCKS9 = 9

    def __init__(self, sh, name, nxt):
        self.sh, self.k, self.next_gain = sh, sh.k, nxt
        k, a = sh.k, sh.k.A0
        self.sq, self.so = sh.stage["dil_q"], sh.stage["dil_o"]
        self.Q = k.at("aQ", a, [P, GROUPS, NC, T])
        self.Oh = k.at("aOh", a + 24 * KB, [P, NC, T], F32R)
        self.Ol = k.at("aOl", a + 32 * KB, [P, NC, T], F32R)
        self.OS = k.at("aOS", a + 40 * KB, [P, 2, D])
        self.KP = k.at("aKP", a + 48 * KB, [P, 2, GROUPS, T])
        self.VP = k.at("aVP", a + 54 * KB, [P, 2, 2, GROUPS, P])
        self.B0 = k.at("aB0", a + 60 * KB, [P, 2, 2, GROUPS, P])
        self.B1 = k.at("aB1", a + 66 * KB, [P, 2, 2, GROUPS, T])
        self.S = k.at("aS", 0, [P, 2, 9, P])
        self.QP = k.at("aQP", 9 * KB, [P, 2, GROUPS, T])
        self.PT = k.at("aPT", 16 * KB, [P, 2, 9, P])
        self.T1 = k.at("aT1", 25 * KB, [P, GROUPS, T])
        self.T2 = k.at("aT2", 28 * KB, [P, GROUPS, T])
        self.st = k.at("ast", 31 * KB, [P, 4, 2, 2])
        self.loads = k.loads_before

    def pe(self, pe):
        sh, k = self.sh, self.k
        sh.norm(pe, "pe")
        sh.split_n["pe"] += NC
        sh.pe_stage_h(pe, self.sq)

        def norm_sums(c):
            k.act_done.wait(pe, f"a.sq{c}")
            if c:
                k.act_done.wait(pe, f"a.stdb{c - 1}")
            for g in range(2):
                ins = pe.matmul(k.bank[7][:, g * T:(g + 1) * T], k.head_ones, self.T1[:, g, :], start=True, stop=True)
            k.pe_done.done(ins, f"a.ssa{c}")
            k.act_done.wait(pe, f"a.stda{c}")
            k.pe_done.done(pe.matmul(k.bank[7][:, :T], k.head_ones, self.T1[:, 2, :], start=True, stop=True), f"a.ssb{c}")

        def scores(u):
            c, e = u // 2, u % 2
            pe.wait_ge(k.pair_loaded[c % 2], 112 * (c // 2 + 1))
            k.dve_done.wait(pe, f"a.qp{c}")
            if u:
                k.dve_done.wait(pe, f"a.add{u - 1}")
            for g in range(GROUPS):
                q0, q1 = self.QP[:, e, g, P:], self.QP[:, e, g, :P]
                pe.matmul(k.bank[0][:, g * P:(g + 1) * P], q0, self.KP[:, c % 2, g, :P], start=True, stop=True)
                b, o = 1 + g // 2, (g % 2) * T
                ins = pe.matmul(k.bank[b][:, o:o + T], q1, self.KP[:, c % 2, g, :], start=True, stop=True)
            k.pe_done.done(ins, f"a.s{u}")

        norm_sums(0)
        scores(0)
        for u in range(16):
            c, e = u // 2, u % 2
            if e == 0 and c + 1 < NC:
                norm_sums(c + 1)
            if u + 1 < 16 and e == 0:
                scores(u + 1)
            k.act_done.wait(pe, f"a.exp{u}")
            if u:
                k.act_done.wait(pe, f"a.pta{u - 1}")
                k.act_done.wait(pe, f"a.ptc{u - 1}")
                k.dve_done.wait(pe, f"a.ptb{u - 1}")
            for j in range(9):
                ins = pe.transpose(k.bank[3 + j // 4][:, (j % 4) * P:(j % 4 + 1) * P], self.S[:, u % 2, j, :], k.ident)
            k.pe_done.done(ins, f"a.t{u}")
            if u + 1 < 16 and e == 1:
                scores(u + 1)
            k.act_done.wait(pe, f"a.pta{u}")
            k.act_done.wait(pe, f"a.ptc{u}")
            k.dve_done.wait(pe, f"a.ptb{u}")
            if u:
                k.dve_done.wait(pe, f"a.o{u - 1}")
            f = slice(e * HEAD, (e + 1) * HEAD)
            for half in range(2):
                out = k.bank[6][:, (2 * half + e) * HEAD:(2 * half + e + 1) * HEAD]
                n = GROUPS * (half + 1)
                for j in range(n):
                    g, key_half = (j, 0) if half == 0 else (j // 2, j % 2)
                    ins = pe.matmul(out, self.PT[:, u % 2, 3 * half + j, :], self.VP[:, c % 2, key_half, g, f],
                                    start=j == 0, stop=j == n - 1)
            k.pe_done.done(ins, f"a.o{u}")
        for b in range(4):
            k.dve_done.wait(pe, "a.o15")
            k.act_done.wait(pe, "a.pta15")
            for j in range(4):
                c, half = 2 * b + j // 2, j % 2
                ins = pe.transpose(k.bank[b][:, j * P:(j + 1) * P], self.OS[:, half, c * P:(c + 1) * P], k.ident)
            k.pe_done.done(ins, f"a.ot{b}")
        sh.pe_stage(pe, self.so, lambda kg, kc: (self.Oh[:, kc, :], self.Ol[:, kc, :]),
                    lambda kg, kc: k.dve_done.wait(pe, "a.ol3"))

    def act(self, act):
        sh, k = self.sh, self.k
        sh.norm(act, "act")
        sh.act_stage(act, self.sq)

        def load(c):
            if c >= 2:
                k.pe_done.wait(act, f"a.o{2 * (c - 2) + 1}")
                k.dve_done.wait(act, f"a.add{2 * (c - 2) + 1}")
            q = c % 2
            act.dma_start(self.KP[:, q], k.dil_k.rearrange("p (g c) t -> p g c t", g=GROUPS)[:, :, c, :]).then_inc(k.pair_loaded[q], 16)
            for half in range(2):
                act.dma_start(self.VP[:, q, half], k.dil_v[:, half, :].rearrange("p (g c j) -> p g c j", g=GROUPS, c=NC)[:, :, c, :]).then_inc(k.pair_loaded[q], 16)
            for n, dst, off in ((P, self.B0, P), (T, self.B1, 0)):
                for e in range(2):
                    src = bass.AP(k.dil_b.tensor, (2 * c + e) * REACH + off, [[1, P], [16 * REACH, GROUPS], [1, n]])
                    act.dma_start(dst[:, q, e], src).then_inc(k.pair_loaded[q], 16)

        def square(c):
            if c:
                k.dve_done.wait(act, f"a.qp{c - 1}")
                k.pe_done.wait(act, f"a.ssb{c - 1}")
            k.act_done.done(act.activation(self.T1[:], self.Q[:, :, c, :], ACT.Square), f"a.sq{c}")

        def root(c):
            k.pe_done.wait(act, f"a.ssa{c}")
            k.act_done.done(act.activation(self.T2[:, 0:2, :], k.bank[7][:].rearrange("p (g t) -> p g t", g=2), ACT.Sqrt,
                                           bias=k.col(C_EPS), scale=1.0 / HEAD), f"a.stda{c}")
            k.pe_done.wait(act, f"a.ssb{c}")
            k.act_done.done(act.activation(self.T2[:, 2, :], k.bank[7][:, :T], ACT.Sqrt, bias=k.col(C_EPS),
                                           scale=1.0 / HEAD), f"a.stdb{c}")

        act.wait_ge(k.banks_freed, RING + self.sq.base + self.sq.slabs)
        load(0)
        load(1)
        square(0)
        root(0)
        for u in range(16):
            c, e = u // 2, u % 2
            if e == 0 and c + 1 < NC:
                square(c + 1)
                root(c + 1)
            k.dve_done.wait(act, f"a.nmax{u}")
            for half in range(2):
                s = self.S[:, u % 2, 3 * half:3 + 6 * half, :]
                k.act_done.done(act.activation(s, s, ACT.Exp, bias=self.st[:, 1, e, half:half + 1],
                                               accum_out=self.st[:, 2, e, half:half + 1]), f"a.exp{u}")
            k.pe_done.wait(act, f"a.t{u}")
            if u >= 2:
                k.pe_done.wait(act, f"a.o{u - 2}")
            k.act_done.done(act.activation(self.PT[:, u % 2, 0:4, :], k.bank[3][:].rearrange("p (a t) -> p a t", a=4), ACT.Copy), f"a.pta{u}")
            k.act_done.done(act.activation(self.PT[:, u % 2, 8, :], k.bank[5][:, :P], ACT.Copy), f"a.ptc{u}")
            if e == 1 and c + 2 < NC:
                load(c + 2)
        for b in range(4):
            k.pe_done.wait(act, f"a.ot{b}")
            k.act_done.done(act.activation(self.out(self.Oh, b), self.reversed(b), ACT.Copy), f"a.oh{b}")
        sh.act_resid(act, self.so, self.next_gain)

    def reversed(self, b):
        return self.k.bank[b][:].rearrange("p (a t) -> p a t", a=4)[:, :, ::-1]

    def out(self, t, b):
        return t[:, 2 * b:2 * b + 2, :].rearrange("p c (h t) -> p (c h) t", h=2)

    def dve(self, dve):
        sh, k = self.sh, self.k
        sh.norm(dve, "dve")
        Qf = self.Q[:].rearrange("p g c t -> p (g c) t")
        sh.dve_project(dve, self.sq, lambda i, q: Qf[:, bass.ds(RING * i + q, 1), :].rearrange("p a t -> p (a t)"))
        d = lambda ins, label: k.dve_done.done(ins, label)

        def queries(c):
            k.act_done.wait(dve, f"a.stdb{c}")
            d(dve.reciprocal(self.T2[:], self.T2[:]), f"a.qr{c}")
            k.dve_done.wait(dve, f"a.qr{c}")
            k.pe_done.wait(dve, f"a.ssb{c}")
            for g in range(GROUPS):
                d(dve.scalar_tensor_tensor(self.T1[:, g, :], self.Q[:, g, c, :], k.v1("q_gain", g), self.T2[:, g, :],
                                           ALU.mult, ALU.mult), f"a.qn{c}")
            k.dve_done.wait(dve, f"a.qn{c}")
            if c:
                k.pe_done.wait(dve, f"a.s{2 * c - 1}")
            for e, m in enumerate((LOW, HIGH)):
                d(dve.tensor_scalar(self.QP[:, e], self.T1[:, :, ::-1], k.col(m), HEAD ** -0.5, ALU.mult, ALU.mult), f"a.qp{c}")

        def add_bias(u):
            c, e = u // 2, u % 2
            dve.wait_ge(k.pair_loaded[c % 2], 112 * (c // 2 + 1))
            k.pe_done.wait(dve, f"a.s{u}")
            if u >= 2:
                k.pe_done.wait(dve, f"a.t{u - 2}")
            s = self.S[:, u % 2]
            bank = lambda b, n: k.bank[b][:, :n * P].rearrange("p (a t) -> p a t", a=n)
            b1 = self.B1[:, c % 2, e].rearrange("p g (h t) -> p (g h) t", h=2)
            d(dve.tensor_tensor(s[:, 0:3, :], bank(0, 3), self.B0[:, c % 2, e], ALU.add), f"a.add0{u}")
            d(dve.tensor_tensor(s[:, 3:7, :], bank(1, 4), b1[:, 0:4, :], ALU.add), f"a.add1{u}")
            d(dve.tensor_tensor(s[:, 7:9, :], bank(2, 2), b1[:, 4:6, :], ALU.add), f"a.add{u}")
            k.dve_done.wait(dve, f"a.add{u}")
            for half in range(2):
                d(dve.tensor_reduce(self.st[:, 0, e, half:half + 1], s[:, 3 * half:3 + 6 * half, :], AX.XY, ALU.max), f"a.max{u}")
            k.dve_done.wait(dve, f"a.max{u}")
            d(dve.tensor_scalar(self.st[:, 1, e, :], self.st[:, 0, e, :], -1.0, None, ALU.mult), f"a.nmax{u}")

        queries(0)
        add_bias(0)
        for u in range(16):
            c, e = u // 2, u % 2
            if e == 0:
                add_bias(u + 1)
                if c + 1 < NC:
                    queries(c + 1)
            k.pe_done.wait(dve, f"a.t{u}")
            if u >= 2:
                k.pe_done.wait(dve, f"a.o{u - 2}")
            d(dve.tensor_copy(self.PT[:, u % 2, 4:8, :], k.bank[4][:].rearrange("p (a t) -> p a t", a=4)), f"a.ptb{u}")
            k.act_done.wait(dve, f"a.exp{u}")
            d(dve.reciprocal(self.st[:, 3, e, :], self.st[:, 2, e, :]), f"a.rs{u}")
            k.dve_done.wait(dve, f"a.rs{u}")
            k.pe_done.wait(dve, f"a.o{u}")
            for half in range(2):
                d(dve.tensor_scalar(self.OS[:, half, c * P + e * HEAD:c * P + (e + 1) * HEAD],
                                    k.bank[6][:, (2 * half + e) * HEAD:(2 * half + e + 1) * HEAD],
                                    self.st[:, 3, e, half:half + 1], None, ALU.mult), f"a.o{u}")
            if e == 1 and u + 1 < 16:
                add_bias(u + 1)
        for b in range(4):
            k.act_done.wait(dve, f"a.oh{b}")
            d(dve.tensor_tensor(self.out(self.Ol, b), self.reversed(b), self.out(self.Oh, b).bitcast(F32), ALU.subtract), f"a.ol{b}")
        sh.dve_resid(dve, self.so, 1.0, self.next_gain)

    def pool(self, pool):
        self.sh.pool_stage(pool, self.sq)
        self.sh.pool_stage(pool, self.so)


class Rwkv7:
    DECAY = math.exp(-0.5)
    LEVELS = 5

    def __init__(self, sh, name, nxt):
        self.sh, self.k, self.next_gain = sh, sh.k, nxt
        k = sh.k
        self.st = {x: sh.stage[f"rwkv_{x}"] for x in "rkvo"}

        def big(n, kb, dt=F32):
            return k.at("r" + n, kb * KB, [P, NC, T], dt)
        self.H, self.DX = big("H", 0), big("DX", 8)
        self.split = {"r": (big("Sah", 16, F32R), big("Sal", 24, F32R)), "v": (big("Sbh", 32, F32R), big("Sbl", 40, F32R))}
        self.split["k"] = self.split["r"]
        self.XR, self.XW, self.XA = big("XR", 64), big("XW", 80), big("XA", 48)
        self.XG, self.XK, self.XV = big("XG", 104), big("XK", 56), big("XV", 64)
        self.R, self.K, self.V, self.SIG, self.A, self.G = (big(n, kb) for n, kb in
            (("R", 72), ("K", 80), ("V", 48), ("SIG", 88), ("A", 96), ("G", 56)))
        self.W1 = k.at("rW1", 112 * KB, [P, NC, LORA_W])
        self.A1 = k.at("rA1", 114 * KB, [P, NC, LORA_A])
        self.G1 = k.at("rG1", 96 * KB, [P, NC, LORA_G])
        self.LT = k.at("rLT", 116 * KB, [P, 2, T])
        self.LG = k.at("rLG", 112 * KB, [P, 2, T])
        self.W2 = k.at("rW2", 32 * KB, [P, D])
        self.A2 = k.at("rA2", 36 * KB, [P, D])
        self.G2 = k.at("rG2", 40 * KB, [P, 2, D])
        self.KN, self.TA, self.SQ = big("KN", 104), big("TA", 0), big("SQ", 8)
        self.CS, self.PP, self.BV, self.PI = big("CS", 16), big("PP", 24), big("BV", 64), big("PI", 72)
        self.TOH = k.at("rTOH", 32 * KB, [16, NC, P])
        self.S16 = k.at("rS16", 36 * KB, [16, T])
        self.AR = k.at("rAR", 0, [P, NC, 2, 2, P])
        self.BK = k.at("rBK", 16 * KB, [P, NC, 2, 2, T])
        s = 72
        self.LN = [k.at(f"rLN{z}", (s + 18 * z) * KB, [P, 2, 2, 2, P]) for z in range(2)]
        self.MQ = [k.at(f"rMQ{z}", (s + 18 * z + 4) * KB, [P, 2, 2, 2, P]) for z in range(2)]
        self.D = [k.at(f"rD{z}", (s + 18 * z + 8) * KB, [P, 4, P]) for z in range(2)]
        self.DT = [k.at(f"rDT{z}", (s + 18 * z + 10) * KB, [P, 4, P]) for z in range(2)]
        self.AX = [k.at(f"rAX{z}", (s + 18 * z + 12) * KB, [P, 2, 4, HEAD]) for z in range(2)]
        self.VT = [k.at(f"rVT{z}", (s + 18 * z + 14) * KB, [P, 2, P]) for z in range(2)]
        self.BKT = [k.at(f"rBKT{z}", (s + 18 * z + 15) * KB, [P, 3, 2, P]) for z in range(2)]
        self.E = [k.at(f"rE{lv}", (108 + 2 * lv) * KB, [P, 4, P]) for lv in range(self.LEVELS)]
        self.LOWER = k.at("rLOWER", 118 * KB, [P, self.LEVELS, 64])
        self.PT = k.at("rPT", 119 * KB + 256, [P, NC, 4])
        self.YC, self.YSQ = big("YC", 72), big("YSQ", 80)
        self.TOH2 = k.at("rTOH2", 88 * KB, [16, NC, P])
        self.S16b = k.at("rS16b", 92 * KB, [16, T])
        self.Oh, self.Ol = big("Oh", 96, F32R), big("Ol", 104, F32R)
        self.loads = [k.loads_before + 16 * n for n in (8, 9, 10)]
        k.loads_before += 16 * 10

    def pe(self, pe):
        sh, k, st = self.sh, self.k, self.st
        sh.norm(pe, "pe")

        def project(x):
            hi, lo = self.split[x]
            sh.pe_stage(pe, st[x], lambda kg, kc: (hi[:, kc, :], lo[:, kc, :]),
                        lambda kg, kc: k.dve_done.wait(pe, f"r.{x}lo"))
        project("r")
        pe.wait_ge(k.mixer_loads, self.loads[0])
        pe.wait_ge(k.rstd_ready, sh.norm_n["pe"])
        for x, w, bank, cols, src in (("w", self.W1, 5, slice(0, 64), self.XW), ("a", self.A1, 6, slice(0, 64), self.XA),
                                      ("g", self.G1, 7, slice(0, 128), self.XG), ("h", self.G1, 4, slice(128, 160), self.XG)):
            if x != "h":
                k.dve_done.wait(pe, f"r.x{x}1")
            n = cols.stop - cols.start
            for c in range(NC):
                ins = pe.matmul(k.bank[bank][:n, :T], w[:, c, cols], src[:, c, :], start=c == 0, stop=c == NC - 1)
            k.pe_done.done(ins, f"r.l1{x}")
        for n in range(12):
            kind, pair = "wag"[n // 4], n % 4
            k.act_done.wait(pe, "r.t" + kind)
            k.act_done.wait(pe, f"r.l2{n - 4}" if n >= 4 else "r.tg")
            for j in range(2):
                c = 2 * pair + j
                out, f = k.bank[4 + n % 4][:, j * T:(j + 1) * T], slice(c * P, (c + 1) * P)
                if kind == "g":
                    pe.matmul(out, self.G2[:, 0, f], self.LG[:, 0, :], start=True, stop=False)
                    ins = pe.matmul(out, self.G2[:32, 1, f], self.LG[:32, 1, :], start=False, stop=True)
                else:
                    w, t = (self.W2, 0) if kind == "w" else (self.A2, 1)
                    ins = pe.matmul(out, w[:64, f], self.LT[:64, t, :], start=True, stop=True)
            k.pe_done.done(ins, f"r.l2{n}")
        project("k")
        project("v")

        k.act_done.wait(pe, "r.sq")
        k.act_done.wait(pe, "r.l28")
        for c in range(NC):
            ins = pe.matmul(k.bank[4][:16, :T], k.sel[:, 16 * c:16 * (c + 1)], self.SQ[:, c, :], start=c == 0, stop=c == NC - 1)
        k.pe_done.done(ins, "r.ss")
        k.dve_done.wait(pe, "r.bp")
        pe.wait_ge(k.banks_freed, RING + st["v"].base + NC)
        for b in range(4):
            for j in range(2):
                ins = pe.matmul(k.bank[b][:, j * T:(j + 1) * T], k.head_ones, self.BV[:, 2 * b + j, :], start=True, stop=True)
            k.pe_done.done(ins, f"r.bs{b}")
        k.dve_done.wait(pe, "r.rn")
        pe.wait_ge(k.mixer_loads, self.loads[1])
        for b in range(4):
            if b:
                k.act_done.wait(pe, f"r.l2{8 + b}")
            for j in range(2):
                ins = pe.matmul(k.bank[4 + b][:, j * T:(j + 1) * T], self.TOH[:, 2 * b + j, :], self.S16[:], start=True, stop=True)
            k.pe_done.done(ins, f"r.rb{b}")

        for c in range(-1, NC + 1):
            after = self.pe_after(pe, c - 1) if c >= 1 else {}
            before = self.pe_before(pe, c + 1) if c + 1 < NC else {}
            if c == -1:
                for step in ("l", "g1", "t", "g2"):
                    before[step]()
                continue
            inv = self.pe_invert(pe, c) if c < NC else {}
            for step in ("e1", "x1", "c1", "w", "e2", "gt", "u", "c2", "ht", "e3", "y", "c3", "l", "e4", "g1", "c4",
                         "t", "e5", "g2", "c5"):
                for part in (inv, after, before):
                    if step in part:
                        part[step]()

        for j in (1, 2):
            for c in range(NC):
                k.dve_done.wait(pe, f"r.u{c}" if j == 1 else f"r.z1{c}")
                if j == 1:
                    k.pool_done.wait(pe, f"r.gti{c}")
                    k.act_done.wait(pe, "r.y7")
                    k.dve_done.wait(pe, "r.ht7")
                k.pe_done.done(pe.matmul(k.bank[c][:, :P], self.gti(c, j), self.z(c, j - 1), start=True, stop=True), f"r.z{j}{c}")
        for c in range(NC):
            k.dve_done.wait(pe, f"r.z2{c}")
            k.dve_done.wait(pe, f"r.ht{c}")
            for j in (1, 2, 3):
                ins = pe.matmul(k.bank[c][:, T + (j - 1) * 64:T + j * 64], self.z(c, j - 1),
                                self.AR[:, c, j // 2, 1, (j % 2) * 64:(j % 2 + 1) * 64], start=True, stop=True)
            k.pe_done.done(ins, f"r.ys{c}")

        for b in range(4):
            k.dve_done.wait(pe, f"r.y{2 * b + 1}")
            for j in range(2):
                ins = pe.matmul(k.bank[b][:, j * T:(j + 1) * T], k.head_ones, self.AR[:, 2 * b + j, :, 0, :], start=True, stop=True)
            k.pe_done.done(ins, f"r.mean{b}")
        for c in range(NC):
            if c % 2 == 0:
                k.act_done.wait(pe, f"r.ysq{c // 2}")
            ins = pe.matmul(k.bank[4][:16, :T], k.sel[:, 16 * c:16 * (c + 1)], self.YSQ[:, c, :], start=c == 0, stop=c == NC - 1)
        k.pe_done.done(ins, "r.yss")
        k.dve_done.wait(pe, "r.yr")
        pe.wait_ge(k.mixer_loads, self.loads[2])
        for b in range(4):
            for j in range(2):
                ins = pe.matmul(k.bank[4 + b][:, j * T:(j + 1) * T], self.TOH2[:, 2 * b + j, :], self.S16b[:], start=True, stop=True)
            k.pe_done.done(ins, f"r.yb{b}")
        if sh.memory:
            k.dve_done.wait(pe, "r.yn3")
            sh.memory.pe(pe)
        sh.pe_stage(pe, st["o"], lambda kg, kc: (self.Oh[:, kc, :], self.Ol[:, kc, :]),
                    lambda kg, kc: k.dve_done.wait(pe, f"r.ol{kc // 2}"))

    def gti(self, c, j):
        return self.BK[:, c, 0, 0, (j - 1) * P:j * P]

    def z(self, c, j):
        return self.BK[:, c, 1, j // 2, (j % 2) * P:(j % 2 + 1) * P]

    def pe_before(self, pe, c):
        k, z, AR, BK = self.k, c % 2, self.AR, self.BK

        def freed(steps, label, first_steps, first_label):
            if c >= 2:
                steps.wait(pe, f"{label}{c - 2}")
            elif c == 1:
                first_steps.wait(pe, f"{first_label}0")

        def l():
            if c == 0:
                k.act_done.wait(pe, "r.bk1")
                k.dve_done.wait(pe, "r.bv")
            freed(k.act_done, "r.x1", k.act_done, "r.g2b")
            for u in range(4):
                hf, e = u // 2, u % 2
                ins = pe.matmul(k.bank[2][:, u * P:(u + 1) * P], AR[:, c, hf, 0, :], BK[:, c, 0, e, hf * P:(hf + 1) * P],
                                start=True, stop=True)
            k.pe_done.done(ins, f"r.l{c}")

        def gram(kind, hf, bank, label):
            for e in range(2):
                ins = pe.matmul(k.bank[bank][:, e * T:(e + 1) * T], BK[:, c, kind, e, hf * P:(hf + 1) * P],
                                AR[:, c, hf, :, :].rearrange("p k t -> p (k t)"), start=True, stop=True)
            k.pe_done.done(ins, label)

        def g1():
            freed(k.act_done, "r.w", k.dve_done, "r.g1a")
            gram(0, 0, 3, f"r.g1a{c}")
            freed(k.dve_done, "r.gt", k.dve_done, "r.g1b")
            gram(0, 1, 4, f"r.g1b{c}")

        def t():
            freed(k.dve_done, "r.u", k.act_done, "r.t1")
            for hf in range(2):
                pe.transpose(k.bank[5][:, hf * P:(hf + 1) * P], AR[:, c, hf, 0, :], k.ident)
                ins = pe.transpose(k.bank[5][:, (2 + hf) * P:(3 + hf) * P], self.V[:, c, hf * P:(hf + 1) * P], k.ident)
            k.pe_done.done(ins, f"r.t1{c}")
            freed(k.dve_done, "r.ht", k.act_done, "r.t2")
            for kind in range(2):
                for hf in range(2):
                    for e in range(2):
                        o = (2 * kind + hf) * P + e * HEAD
                        ins = pe.matmul(k.bank[6][:, o:o + HEAD], BK[:, c, kind, e, hf * P:(hf + 1) * P],
                                        k.ident[:, e * HEAD:(e + 1) * HEAD], start=True, stop=True)
            k.pe_done.done(ins, f"r.t2{c}")

        def g2():
            freed(k.act_done, "r.y", k.act_done, "r.g2a")
            gram(1, 0, 7, f"r.g2a{c}")
            k.dve_done.wait(pe, f"r.l{c}")
            gram(1, 1, 2, f"r.g2b{c}")
        return {"l": l, "g1": g1, "t": t, "g2": g2}

    def cols(self, t, u, b, side):
        return t[:, u, :].rearrange("p (n b) -> p n b", b=2 * b)[:, :, side * b:(side + 1) * b]

    def pe_invert(self, pe, c):
        k, z = self.k, c % 2
        D, DT, LN = self.D[z], self.DT[z], self.LN[z]
        steps = {}
        for lv in range(1, self.LEVELS + 1):
            def e(lv=lv):
                if lv == 1:
                    k.pool_done.wait(pe, f"r.dt{c}")
                    if c:
                        k.dve_done.wait(pe, f"r.ct5{c - 1}")
                    else:
                        k.dve_done.wait(pe, "r.bv")
                else:
                    k.dve_done.wait(pe, f"r.ct{lv - 1}{c}")
                for u in range(4):
                    ins = pe.matmul(k.bank[0][:, u * 64:(u + 1) * 64], LN[:, u // 2, u % 2, 0, :],
                                    self.cols(D, u, 1 << lv, 0), start=True, stop=True)
                k.pe_done.done(ins, f"r.e{lv}{c}")

            def cc(lv=lv):
                k.dve_done.wait(pe, f"r.e{lv}{c}")
                E = self.E[lv - 1]
                for u in range(4):
                    pe.matmul(k.bank[1][:, u * 64:(u + 1) * 64], DT[:, u, :], self.cols(E, u, 1 << lv, 0), start=True, stop=True)
                    ins = pe.matmul(k.bank[1][:, T + u * 64:T + (u + 1) * 64], E[:, u, :], self.cols(DT, u, 1 << lv, 1),
                                    start=True, stop=True)
                k.pe_done.done(ins, f"r.c{lv}{c}")
            steps[f"e{lv}"], steps[f"c{lv}"] = e, cc
        return steps

    def pe_after(self, pe, c):
        k, z = self.k, c % 2
        AX, VT, BKT, LN, MQ = self.AX[z], self.VT[z], self.BKT[z], self.LN[z], self.MQ[z]
        nxt = c + 1 < NC
        half_of = {0: (0, 0), 1: (0, 2), 2: (1, 1)}

        def x1():
            if nxt:
                k.act_done.wait(pe, f"r.g2b{c + 1}")
            else:
                k.act_done.wait(pe, f"r.x1{c - 1}")
            k.pool_done.wait(pe, f"r.mq{c}")
            k.act_done.wait(pe, f"r.t1{c}")
            for u in range(4):
                hf, e = u // 2, u % 2
                ins = pe.matmul(k.bank[2][:, u * 64:(u + 1) * 64], MQ[:, hf, e, 0, :], VT[:, hf, e * 64:(e + 1) * 64],
                                start=True, stop=True)
            k.pe_done.done(ins, f"r.x1{c}")

        def w():
            if nxt:
                k.dve_done.wait(pe, f"r.g1a{c + 1}")
            else:
                k.act_done.wait(pe, f"r.w{c - 1}")
            k.act_done.wait(pe, f"r.x1{c}")
            k.dve_done.wait(pe, f"r.ct5{c}")
            for u in range(4):
                hf, e = u // 2, u % 2
                ins = pe.matmul(k.bank[3][:, u * P:(u + 1) * P], self.DT[z][:, u, :],
                                AX[:, :, u, :], start=True, stop=True)
            k.pe_done.done(ins, f"r.w{c}")

        def gt():
            k.dve_done.wait(pe, f"r.g1b{c + 1}" if nxt else f"r.gt{c - 1}")
            k.act_done.wait(pe, f"r.w{c}")
            k.act_done.wait(pe, f"r.t2{c}")
            for j in (1, 2):
                hf, n = half_of[j]
                ins = pe.matmul(k.bank[4][:, (j - 1) * P:j * P], AX[:, 0, 2 * hf:2 * hf + 2, :].rearrange("p e f -> p (e f)"), BKT[:, n, 0, :], start=True, stop=True)
            k.pe_done.done(ins, f"r.gt{c}")

        def u_():
            if nxt:
                k.act_done.wait(pe, f"r.t1{c + 1}")
            else:
                k.dve_done.wait(pe, f"r.u{c - 1}")
            for j in range(3):
                hf, n = half_of[j]
                out = k.bank[5][:, j * P:(j + 1) * P]
                pe.matmul(out, BKT[:, n, 0, :], AX[:, 1, 2 * hf:2 * hf + 2, :], start=True, stop=False)
                ins = pe.matmul(out, BKT[:, n, 1, :], VT[:, hf, :], start=False, stop=True)
            k.pe_done.done(ins, f"r.u{c}")

        def ht():
            if nxt:
                k.act_done.wait(pe, f"r.t2{c + 1}")
            else:
                k.dve_done.wait(pe, f"r.ht{c - 1}")
            for hf in range(2):
                for e in range(2):
                    ins = pe.matmul(k.bank[6][e * 64:(e + 1) * 64, hf * P:(hf + 1) * P], AX[:, 0, 2 * hf + e, :],
                                    LN[:, hf, e, 1, :], start=True, stop=True, skip_group_check=True)
            k.pe_done.done(ins, f"r.ht{c}")

        def y():
            if nxt:
                k.act_done.wait(pe, f"r.g2a{c + 1}")
            else:
                k.act_done.wait(pe, f"r.y{c - 1}")
            for hf in range(2):
                for e in range(2):
                    out = k.bank[7][e * 64:(e + 1) * 64, hf * P:(hf + 1) * P]
                    pe.matmul(out, AX[:, 1, 2 * hf + e, :], LN[:, hf, e, 1, :], start=True, stop=False, skip_group_check=True)
                    ins = pe.matmul(out, VT[:, hf, e * 64:(e + 1) * 64], MQ[:, hf, e, 1, :], start=False, stop=True,
                                    skip_group_check=True)
            k.pe_done.done(ins, f"r.y{c}")
        return {"x1": x1, "w": w, "gt": gt, "u": u_, "ht": ht, "y": y}

    def act(self, act):
        sh, k, st = self.sh, self.k, self.st
        d = lambda ins, label: k.act_done.done(ins, label)
        load = lambda dst, src: act.dma_start(dst, k.io[src]).then_inc(k.mixer_loads, 16)
        load(self.W1[:], "lora_w1")
        load(self.A1[:], "lora_a1")
        load(self.G1[:], "lora_g1")
        load(self.LOWER[:], "lower")
        load(self.W2[:64], "lora_w2")
        load(self.A2[:64], "lora_a2")
        load(self.G2[:, 0, :], "lora_g2a")
        load(self.G2[:32, 1, :], "lora_g2b")
        sh.norm(act, "act")

        def split(x, src):
            for half in range(2):
                sl = slice(4 * half, 4 * half + 4)
                k.dve_done.wait(act, f"r.x{x}{half}")
                d(act.activation(self.split[x][0][:, sl, :], src[:, sl, :], ACT.Copy), f"r.{x}hi{half}")
        split("r", self.XR)
        sh.act_stage(act, st["r"])
        k.pe_done.wait(act, "r.l1w")
        d(act.activation(self.LT[:64, 0, :], k.bank[5][:64, :T], ACT.Tanh), "r.tw")
        k.pe_done.wait(act, "r.l1a")
        d(act.activation(self.LT[:64, 1, :], k.bank[6][:64, :T], ACT.Copy), "r.ta")
        k.pe_done.wait(act, "r.l1h")
        d(act.activation(self.LG[:, 0, :], k.bank[7][:, :T], ACT.Sigmoid), "r.tg0")
        d(act.activation(self.LG[:32, 1, :], k.bank[4][:32, :T], ACT.Sigmoid), "r.tg")
        split("k", self.XK)
        for n in range(12):
            kind, pair = "wag"[n // 4], n % 4
            k.pe_done.wait(act, f"r.l2{n}")
            if kind == "g":
                if pair == 0:
                    k.dve_done.wait(act, "r.klo")
                d(act.activation(self.G[:, 2 * pair:2 * pair + 2, :], k.bank[4 + n % 4][:].rearrange("p (c t) -> p c t", c=2),
                                 ACT.Copy), f"r.l2{n}")
            else:
                dst, b = (self.SIG, "w0") if kind == "w" else (self.A, "a0")
                for j in range(2):
                    c = 2 * pair + j
                    d(act.activation(dst[:, c, :], k.bank[4 + n % 4][:, j * T:(j + 1) * T], ACT.Sigmoid, bias=k.v1(b, c)), f"r.l2{n}")
        split("v", self.XV)
        sh.act_stage(act, st["k"])
        for c in range(NC):
            k.dve_done.wait(act, f"r.kk{c}")
            d(act.activation(self.SQ[:, c, :], self.KN[:, c, :], ACT.Square), "r.sq")
        sh.act_stage(act, st["v"])
        act.wait_ge(k.slab_used, st["v"].base + NC)
        load(self.TOH[:], "to_heads")
        k.pe_done.wait(act, "r.ss")
        d(act.activation(self.S16[:], k.bank[4][:16, :T], ACT.Sqrt), "r.n16")
        k.dve_done.wait(act, "r.cs")
        d(act.activation(self.PP[:], self.CS[:], ACT.Exp, scale=-self.DECAY), "r.p")
        k.act_done.wait(act, "r.p")
        d(act.activation(self.PT[:], self.PP[:, :, CHUNK - 1::CHUNK], ACT.Copy), "r.pt")
        k.pool_done.wait(act, "r.dd")
        d(act.activation(self.SIG[:], self.SIG[:], ACT.Exp, scale=-self.DECAY), "r.pprev")
        k.dve_done.wait(act, "r.R")
        d(act.activation(self.PI[:], self.CS[:], ACT.Exp, scale=self.DECAY), "r.pinv")
        for kind, src, label in ((0, self.A, "r.B"), (1, self.K, "r.K")):
            k.dve_done.wait(act, label)
            for e, m in enumerate((LOW, HIGH)):
                d(act.activation(self.BK[:, :, kind, e, :], src[:], ACT.Copy, scale=k.col(m)), f"r.bk{kind}")
        for c in range(-1, NC + 1):
            if c >= 1:
                self.act_after(act, c - 1)
            if c + 1 < NC:
                self.act_before(act, c + 1)
        k.pe_done.wait(act, "r.ys7")
        if sh.memory:
            act.dma_start(sh.memory.M[:], k.io["mem"]).then_inc(k.mem_loaded, 16)
        load(self.TOH2[:], "to_heads")
        for b in range(4):
            k.dve_done.wait(act, f"r.yc{b}")
            d(act.activation(self.YSQ[:, 2 * b:2 * b + 2, :], self.YC[:, 2 * b:2 * b + 2, :], ACT.Square), f"r.ysq{b}")
        k.pe_done.wait(act, "r.yss")
        d(act.activation(self.S16b[:], k.bank[4][:16, :T], ACT.Sqrt, bias=k.cols[:16, C_GN_EPS:C_GN_EPS + 1], scale=1.0 / HEAD), "r.ystd")
        for b in range(4):
            k.dve_done.wait(act, f"r.yn{b}")
            for c in (2 * b, 2 * b + 1):
                d(act.activation(self.YC[:, c, :], self.YC[:, c, :], ACT.Identity, bias=k.v1("ln_b", c), scale=k.v1("ln_w", c)), f"r.yl{b}")
            if b:
                k.pool_done.wait(act, f"r.yg{b - 1}")
                d(act.activation(self.Oh[:, 2 * b - 2:2 * b, :], self.YC[:, 2 * b - 2:2 * b, :], ACT.Copy), f"r.oh{b - 1}")
        k.pool_done.wait(act, "r.yg3")
        d(act.activation(self.Oh[:, 6:8, :], self.YC[:, 6:8, :], ACT.Copy), "r.oh3")
        if sh.memory:
            sh.memory.act(act)
        sh.act_resid(act, st["o"], self.next_gain)

    def act_before(self, act, c):
        k, z = self.k, c % 2
        d = lambda ins, label: k.act_done.done(ins, label)
        k.pe_done.wait(act, f"r.t1{c}")
        d(act.activation(self.AX[z][:, 0], k.bank[5][:, :T].rearrange("p (u f) -> p u f", u=4), ACT.Copy), f"r.t1{c}")
        d(act.activation(self.VT[z][:], k.bank[5][:, T:].rearrange("p (h f) -> p h f", h=2), ACT.Copy), f"r.t1{c}")
        k.pe_done.wait(act, f"r.t2{c}")
        src = k.bank[6][:].rearrange("p (k h f) -> p h k f", k=2, h=2)
        d(act.activation(self.BKT[z][:, 0:2, :, :], src, ACT.Copy, scale=k.col(LOW)), f"r.t2{c}")
        d(act.activation(self.BKT[z][:, 2, :, :], src[:, 0, :, :], ACT.Copy, scale=k.col(HIGH)), f"r.t2{c}")
        for hf, bank in ((0, 7), (1, 2)):
            k.pe_done.wait(act, f"r.g2{'ab'[hf]}{c}")
            d(act.activation(self.MQ[z][:, hf].rearrange("p e k t -> p (e k t)"), k.bank[bank][:], ACT.Copy), f"r.g2{'ab'[hf]}{c}")

    def act_after(self, act, c):
        k, z = self.k, c % 2
        d = lambda ins, label: k.act_done.done(ins, label)
        k.pe_done.wait(act, f"r.x1{c}")
        d(act.activation(self.AX[z][:, 1], k.bank[2][:, :T].rearrange("p (u f) -> p u f", u=4), ACT.Copy), f"r.x1{c}")
        k.pe_done.wait(act, f"r.w{c}")
        d(act.activation(self.AX[z][:].rearrange("p k u f -> p u k f"), k.bank[3][:].rearrange("p (u k f) -> p u k f", u=4, k=2), ACT.Copy), f"r.w{c}")
        k.pe_done.wait(act, f"r.y{c}")
        d(act.activation(self.AR[:, c, :, 0, :], k.bank[7][:, :T].rearrange("p (h t) -> p h t", h=2), ACT.Copy), f"r.y{c}")

    def dve(self, dve):
        sh, k, st = self.sh, self.k, self.st

        def d(ins, label):
            k.dve_done.done(ins, label)

        def dw(ins, label):
            k.dve_done.done(ins, label)
            k.dve_done.wait(dve, label)
        sh.norm(dve, "dve")
        dve.wait_ge(k.rstd_ready, sh.norm_n["dve"])
        for c in range(NC):
            d(dve.scalar_tensor_tensor(self.H[:, c, :], k.X[:, c, :], k.v1("mix_norm0", c), k.R[:], ALU.mult, ALU.mult), "r.h")
        k.dve_done.wait(dve, "r.h")
        d(dve.tensor_tensor(self.DX[:, :, 1:], self.H[:, :, :-1], self.H[:, :, 1:], ALU.subtract), "r.dx1")
        dw(dve.tensor_scalar(self.DX[:, :, 0:1], self.H[:, :, 0:1], -1.0, None, ALU.mult), "r.dx")

        def mixed(x, j, dst):
            for c in range(NC):
                d(dve.scalar_tensor_tensor(dst[:, c, :], self.DX[:, c, :], k.v1(f"mu{j}", c), self.H[:, c, :], ALU.mult, ALU.add),
                  f"r.x{x}{c // 4}")

        def low(x, src):
            for half in range(2):
                sl = slice(4 * half, 4 * half + 4)
                k.act_done.wait(dve, f"r.{x}hi{half}")
                d(dve.tensor_tensor(self.split[x][1][:, sl, :], src[:, sl, :], self.split[x][0][:, sl, :].bitcast(F32), ALU.subtract), f"r.{x}lo")
        flat = lambda t: (lambda i, q: t[:, bass.ds(RING * i + q, 1), :].rearrange("p a t -> p (a t)"))
        mixed("r", 0, self.XR)
        mixed("w", 1, self.XW)
        low("r", self.XR)
        mixed("a", 4, self.XA)
        mixed("g", 5, self.XG)
        sh.dve_project(dve, st["r"], flat(self.R), scaled=False)
        mixed("k", 2, self.XK)
        mixed("v", 3, self.XV)
        low("k", self.XK)
        k.act_done.wait(dve, "r.vhi0")
        low("v", self.XV)
        sh.dve_project(dve, st["k"], flat(self.K), scaled=False)
        dve.wait_ge(k.banks_freed, RING + st["k"].base + NC)
        for c in range(NC):
            d(dve.tensor_scalar(self.KN[:, c, :], self.K[:, c, :], k.v1("k_k", c), None, ALU.mult), f"r.kk{c}")
        k.act_done.wait(dve, "r.l27")
        for c in range(NC):
            d(dve.tensor_scalar(self.TA[:, c, :], self.A[:, c, :], 1.0, k.v1("k_a", c), ALU.subtract, ALU.mult), "r.ta")
        k.dve_done.wait(dve, "r.ta")
        dw(dve.scalar_tensor_tensor(self.K[:], self.TA[:], 1.0, self.K[:], ALU.add, ALU.mult), "r.kp")
        sh.dve_project(dve, st["v"], flat(self.V), scaled=False)
        for c in range(NC):
            for half in range(2):
                sl = slice(half * P, (half + 1) * P)
                d(dve.tensor_tensor_scan(self.CS[:, c, sl], k.mask("reset"), self.SIG[:, c, sl], 0.0, ALU.mult, ALU.add), "r.cs")
        for c in range(NC):
            d(dve.scalar_tensor_tensor(self.BV[:, c, :], self.R[:, c, :], k.v1("r_k", c), self.K[:, c, :], ALU.mult, ALU.mult), "r.bp")
        k.act_done.wait(dve, "r.n16")
        dw(dve.tensor_scalar(self.S16[:], self.S16[:], 1e-12, None, ALU.max), "r.m16")
        d(dve.reciprocal(self.S16[:], self.S16[:]), "r.rn")
        halves = lambda t: t.rearrange("p c (h t) -> p c h t", h=2)
        k.act_done.wait(dve, "r.p")
        d(dve.tensor_tensor(self.AR[:, :, :, 1, :], halves(self.R[:]), halves(self.PP[:]), ALU.mult), "r.R")
        for b in range(4):
            k.pe_done.wait(dve, f"r.rb{b}")
            sl = slice(2 * b, 2 * b + 2)
            ps = k.bank[4 + b][:].rearrange("p (c t) -> p c t", c=2)
            d(dve.tensor_tensor(self.KN[:, sl, :], self.KN[:, sl, :], ps, ALU.mult), "r.kn")
        k.dve_done.wait(dve, "r.kn")
        dw(dve.tensor_tensor(self.A[:], self.KN[:], self.A[:], ALU.mult), "r.b")
        k.act_done.wait(dve, "r.pprev")
        d(dve.scalar_tensor_tensor(self.AR[:, :, :, 0, :], halves(self.KN[:]), -1.0, halves(self.SIG[:]), ALU.mult, ALU.mult), "r.A")
        k.act_done.wait(dve, "r.pinv")
        d(dve.tensor_tensor(self.A[:], self.A[:], self.PI[:], ALU.mult), "r.B")
        d(dve.tensor_tensor(self.K[:], self.K[:], self.PI[:], ALU.mult), "r.K")
        for b in range(4):
            k.pe_done.wait(dve, f"r.bs{b}")
            sl = slice(2 * b, 2 * b + 2)
            ps = k.bank[b][:].rearrange("p (c t) -> p c t", c=2)
            d(dve.tensor_tensor(self.BV[:, sl, :], ps, self.V[:, sl, :], ALU.mult), "r.bv")
        k.act_done.wait(dve, "r.bk1")
        for lv in range(self.LEVELS):
            d(dve.memset(self.E[lv][:], 0.0), "r.zero")
        k.dve_done.wait(dve, "r.zero")
        dve.wait_ge(k.mixer_loads, self.loads[0])

        for c in range(-1, NC + 1):
            after = self.dve_after(dve, c - 1) if c >= 1 else {}
            before = self.dve_before(dve, c + 1) if c + 1 < NC else {}
            inv = self.dve_invert(dve, c) if 0 <= c < NC else {}
            for step in ("e1", "c1", "e2", "gt", "u", "c2", "ht", "e3", "c3", "l", "e4", "g1", "c4", "e5", "c5"):
                for part in (inv, after, before):
                    if step in part:
                        part[step]()

        for j in (1, 2):
            for c in range(NC):
                k.pe_done.wait(dve, f"r.z{j}{c}")
                zj = self.z(c, j)
                d(dve.scalar_tensor_tensor(zj, k.bank[c][:, :P], self.PT[:, c, j:j + 1], zj, ALU.mult, ALU.add), f"r.z{j}{c}")
        for c in range(NC):
            k.pe_done.wait(dve, f"r.ys{c}")
            y1, y2 = self.AR[:, c, 0, 0, 64:], self.AR[:, c, 1, 0, :]
            d(dve.tensor_tensor(y1, y1, k.bank[c][:, T:T + 64], ALU.add), f"r.y{c}")
            d(dve.tensor_tensor(y2, y2, k.bank[c][:, T + 64:T + 192], ALU.add), f"r.y{c}")
        for b in range(4):
            k.pe_done.wait(dve, f"r.mean{b}")
            sl = slice(2 * b, 2 * b + 2)
            ps = k.bank[b][:].rearrange("p (c h t) -> p c h t", c=2, h=2)
            d(dve.scalar_tensor_tensor(halves(self.YC[:, sl, :]), ps, -1.0 / HEAD, self.AR[:, sl, :, 0, :], ALU.mult, ALU.add), f"r.yc{b}")
        k.act_done.wait(dve, "r.ystd")
        d(dve.reciprocal(self.S16b[:], self.S16b[:]), "r.yr")
        for b in range(4):
            k.pe_done.wait(dve, f"r.yb{b}")
            sl = slice(2 * b, 2 * b + 2)
            ps = k.bank[4 + b][:].rearrange("p (c t) -> p c t", c=2)
            d(dve.tensor_tensor(self.YC[:, sl, :], self.YC[:, sl, :], ps, ALU.mult), f"r.yn{b}")
            if b:
                self.dve_bonus(dve, b - 1)
        self.dve_bonus(dve, 3)
        for b in range(4):
            k.act_done.wait(dve, f"r.oh{b}")
            sl = slice(2 * b, 2 * b + 2)
            d(dve.tensor_tensor(self.Ol[:, sl, :], self.YC[:, sl, :], self.Oh[:, sl, :].bitcast(F32), ALU.subtract), f"r.ol{b}")
        if sh.memory:
            sh.memory.dve(dve)
        sh.dve_resid(dve, st["o"], 1.0, self.next_gain)

    def dve_bonus(self, dve, b):
        k, sl = self.k, slice(2 * b, 2 * b + 2)
        k.act_done.wait(dve, f"r.yl{b}")
        k.dve_done.done(dve.tensor_tensor(self.YC[:, sl, :], self.YC[:, sl, :], self.BV[:, sl, :], ALU.add), f"r.yv{b}")

    def dve_before(self, dve, c):
        k, z = self.k, c % 2

        def l():
            k.pe_done.wait(dve, f"r.l{c}")
            k.dve_done.done(dve.tensor_tensor(self.D[z][:], k.bank[2][:].rearrange("p (u t) -> p u t", u=4),
                                              bcast(k.mask("pair0_lower"), 4), ALU.mult), f"r.l{c}")

        def g1():
            m = k.mask("strict", 2).unsqueeze(1).broadcast_to([P, 2, 2, P])
            for hf in range(2):
                label = f"r.g1{'ab'[hf]}{c}"
                k.pe_done.wait(dve, label)
                ps = k.bank[3 + hf][:].rearrange("p (e k t) -> p e k t", e=2, k=2)
                k.dve_done.done(dve.tensor_tensor(self.LN[z][:, hf], ps, m, ALU.mult), label)
        return {"l": l, "g1": g1}

    def dve_invert(self, dve, c):
        k, z = self.k, c % 2
        steps = {}

        def side(t, b, s):
            return t[:].rearrange("p u (n b) -> p u n b", b=2 * b)[:, :, :, s * b:(s + 1) * b]

        for lv in range(1, self.LEVELS + 1):
            b = 1 << lv

            def e(lv=lv, b=b):
                k.pe_done.wait(dve, f"r.e{lv}{c}")
                ps = k.bank[0][:, :T].rearrange("p (u n b) -> p u n b", u=4, b=b)
                m = self.LOWER[:, lv - 1, :].rearrange("p (n b) -> p n b", b=b).unsqueeze(1).broadcast_to([P, 4, 64 // b, b])
                k.dve_done.done(dve.tensor_tensor(side(self.E[lv - 1], b, 0), ps, m, ALU.mult), f"r.e{lv}{c}")

            def cc(lv=lv, b=b):
                k.pe_done.wait(dve, f"r.c{lv}{c}")
                for t, s, label in ((self.D[z], 0, "r.cd"), (self.DT[z], 1, "r.ct")):
                    ps = k.bank[1][:, s * T:(s + 1) * T].rearrange("p (u n b) -> p u n b", u=4, b=b)
                    v = side(t, b, s)
                    k.dve_done.done(dve.tensor_tensor(v, v, ps, ALU.add), f"{label}{lv}{c}")
            steps[f"e{lv}"], steps[f"c{lv}"] = e, cc
        return steps

    def dve_after(self, dve, c):
        k = self.k

        def gt():
            k.pe_done.wait(dve, f"r.gt{c}")
            dst = self.BK[:, c, 0, 0, :].rearrange("p (j t) -> p j t", j=2)
            k.dve_done.done(dve.tensor_tensor(dst, k.bank[4][:, :T].rearrange("p (j t) -> p j t", j=2),
                                              bcast(k.head_ones, 2), ALU.mult), f"r.gt{c}")

        def u():
            k.pe_done.wait(dve, f"r.u{c}")
            for j in range(3):
                k.dve_done.done(dve.scalar_tensor_tensor(self.z(c, j), k.bank[5][:, j * P:(j + 1) * P], self.PT[:, c, j:j + 1],
                                                         k.head_ones, ALU.mult, ALU.mult), f"r.u{c}")

        def ht():
            k.pe_done.wait(dve, f"r.ht{c}")
            r = self.AR[:, c, :, 1, :]
            k.dve_done.done(dve.tensor_tensor(r, r, k.bank[6][:, :T].rearrange("p (h t) -> p h t", h=2), ALU.add), f"r.ht{c}")
        return {"gt": gt, "u": u, "ht": ht}

    def pool(self, pool):
        sh, k, st = self.sh, self.k, self.st
        d = lambda ins, label: k.pool_done.done(ins, label)
        for x in "rkv":
            sh.pool_stage(pool, st[x])
        k.dve_done.wait(pool, "r.cs")
        d(pool.tensor_tensor(self.SIG[:], self.CS[:], self.SIG[:], ALU.subtract), "r.dd")
        ident4 = bcast(k.ident, 4)
        for c in range(-1, NC + 1):
            if c + 1 < NC:
                n, z = c + 1, (c + 1) % 2
                k.dve_done.wait(pool, f"r.l{n}")
                d(pool.tensor_tensor(self.D[z][:], self.D[z][:], ident4, ALU.add), f"r.d{n}")
                for hf in range(2):
                    k.dve_done.wait(pool, f"r.g1{'ab'[hf]}{n}")
                    d(pool.tensor_tensor(self.DT[z][:, 2 * hf:2 * hf + 2, :], self.LN[z][:, hf, :, 0, :],
                                         bcast(k.mask("pair0"), 2), ALU.mult), f"r.dm{n}")
                k.pool_done.wait(pool, f"r.dm{n}")
                d(pool.tensor_tensor(self.DT[z][:], self.DT[z][:], ident4, ALU.add), f"r.dt{n}")
                m = k.mask("strict", 2).unsqueeze(1).broadcast_to([P, 2, 2, P])
                for hf in range(2):
                    k.act_done.wait(pool, f"r.g2{'ab'[hf]}{n}")
                    d(pool.tensor_tensor(self.MQ[z][:, hf], self.MQ[z][:, hf], m, ALU.mult), f"r.mq{n}")
            if c >= 1:
                self.pool_after(pool, c - 1)
        for b in range(4):
            k.dve_done.wait(pool, f"r.yv{b}")
            sl = slice(2 * b, 2 * b + 2)
            d(pool.tensor_tensor(self.YC[:, sl, :], self.YC[:, sl, :], self.G[:, sl, :], ALU.mult), f"r.yg{b}")
        if sh.memory:
            sh.memory.pool(pool)
        sh.pool_stage(pool, st["o"])

    def pool_after(self, pool, c):
        k = self.k
        k.dve_done.wait(pool, f"r.gt{c}")
        g = self.BK[:, c, 0, 0, :].rearrange("p (j t) -> p j t", j=2)
        k.pool_done.done(pool.tensor_tensor(g, g, bcast(k.ident, 2), ALU.add), f"r.gti{c}")


def make_blocks(sh, blocks):
    out, n_ffn = [], 0
    flow = [b for b in blocks if b != "mem"]
    for n, b in enumerate(flow):
        nxt = flow[n + 1] if n + 1 < len(flow) else None
        gain = "final_norm" if nxt == "final" else GAIN_OF.get(nxt)
        if b.startswith("ffn"):
            out.append(FeedForward(sh, b, n_ffn, gain, own_norm=n == 0 or flow[n - 1] != "kv"))
            n_ffn += 1
        else:
            out.append(MIXERS[b.rstrip("01")](sh, b, gain))
    return out


MIXERS = {"rwkv": Rwkv7, "xattn": CrossAttention, "gmlp": GatedMlp, "final": FinalNorm, "hgrn": Hgrn2, "kv": DilatedKeys, "dil": DilatedAttention}


def program(nc, io, blocks, counts):
    with ExitStack() as ctx:
        k = Resources(nc, ctx, io, counts)
        sh = Shared(k, blocks)
        first = GAIN_OF[[b for b in blocks if b != "mem"][0]]
        st0 = sh.stages[0]
        memory = Memory(sh) if "mem" in blocks else None
        sh.memory = memory
        body = make_blocks(sh, blocks)
        prelude_mem = "mem" in blocks and "rwkv" not in blocks
        block = ctx.enter_context(nc.Block())

        @block.sync
        def _(sp):
            for dst, src in ((k.vec, "vec"), (k.cols, "cols"), (k.masks, "masks"), (k.sel, "sel"), (k.X, "x")):
                sp.dma_start(dst[:], io[src]).then_inc(k.loaded, 16)
            if prelude_mem:
                sp.dma_start(memory.M[:], io["mem"]).then_inc(k.mem_loaded, 16)
            for st in sh.stages:
                sh.sp_stage(sp, st)
            sp.wait_ge(k.banks_freed, RING + sh.n_slabs)
            for c in range(0, NC, 2):
                sp.dma_start(io["out"][:, c:c + 2, :], k.X[:, c:c + 2, :]).then_inc(k.out_stored, 16)
            sp.wait_ge(k.out_stored, 16 * (NC // 2))

        @block.gpsimd
        def _(pool):
            for q in range(RING):
                sh.pool_lo(pool, q, q, st0.width)
            if prelude_mem:
                memory.pool(pool)
            for b in body:
                b.pool(pool)

        @block.scalar
        def _(act):
            act.wait_ge(k.loaded, 16 * 5)
            for q in range(RING):
                sh.act_hi(act, q, q, st0.width, 0)
            if prelude_mem:
                memory.act(act)
            sh.prep_all(act, "act", k.X, first, split=first not in UNSPLIT)
            for b in body:
                b.act(act)

        @block.vector
        def _(dve):
            dve.sem_inc(k.banks_freed, RING)
            dve.sem_inc(k.silu_done, 2)
            dve.sem_inc(k.a_ready, 2)
            dve.sem_inc(k.al_ready, 2)
            dve.sem_inc(k.gelu_done, RING)
            for q in range(RING):
                sh.dve_lo(dve, q, q, st0.width)
            dve.wait_ge(k.loaded, 16 * 5)
            if prelude_mem:
                memory.dve(dve)
            sh.prep_all(dve, "dve", k.X, first, split=first not in UNSPLIT)
            for b in body:
                b.dve(dve)

        @block.tensor
        def _(pe):
            pe.wait_ge(k.loaded, 16 * 5)
            if prelude_mem:
                memory.pe(pe)
            for b in body:
                b.pe(pe)


def by_feature(a):
    return np.ascontiguousarray(a.reshape(T, -1, P).transpose(2, 1, 0))


def column(a):
    return a.reshape(-1, P).T


def slabs(w, group, tiles=None):
    k, n = w.shape
    s = w.reshape(k // (P * group), group, P, n // P, P).transpose(3, 0, 2, 1, 4)
    if tiles is not None:
        s = s[tiles]
    return s.reshape(-1, P, group * P)


def lay_out(a, blocks):
    a = {n: np.asarray(v) for n, v in a.items()}
    v = {"mem_norm": a["mem_norm"], "final_norm": a["final_norm"], "kv_norm": a["kv_norm_2"],
         "w0": a["rwkv_w0"][0], "a0": a["rwkv_a0"][0], "k_k": a["rwkv_k_k"][0], "k_a": a["rwkv_k_a"][0],
         "r_k": a["rwkv_r_k"][0].reshape(-1), "ln_w": a["rwkv_ln_w"][0], "ln_b": a["rwkv_ln_b"][0],
         "lb0": a["a_lb_logits_2"][0], "lb1": a["a_lb_logits_2"][1], "v_norm": a["gmlp_v_norm"][0],
         "a_out_gain": a["a_out_gain_2"][0], "k_gain": np.tile(a["k_gain_2"], (1, 2)).reshape(-1),
         "q_gain": np.tile(a["b_q_gain_2"][0], (1, 2)).reshape(-1)}
    for layer in range(2):
        for n in ("ffn1_norm", "mix_norm", "xattn_norm", "ffn2_norm"):
            v[f"{n}{layer}"] = a[n][layer]
        for j in range(3):
            v[f"norm_gain{layer}{j}"] = a["norm_gain_2"][layer, j]
    for j in range(6):
        v[f"mu{j}"] = a["rwkv_mu"][0, j]
    m = square_masks()
    out = {
        "vec": np.concatenate([column(v[n]) for n, _ in VECTORS], 1),
        "cols": column_masks(),
        "masks": np.stack([m[n] for n in MASKS], 1).astype(np.float32),
        "x": by_feature(a["x"][0]), "mem": by_feature(a["mem"][0]),
    }
    rkv = a["rwkv_w_rkv"][0]
    hg = a["a_w_in_2"][0]
    w = {"mem_kv": a["mem_w_kv"], "rwkv_o": a["rwkv_w_o"][0], "gmlp_uv": a["gmlp_w_uv"][0],
         "gmlp_o": a["gmlp_w_o"][0], "hgrn_o": a["a_w_out_2"][0], "dil_q": a["b_w_q_2"][0],
         "dil_o": a["b_w_o_2"][0], "dil_k": a["w_kv_2"][:, :3 * D], "dil_v": a["w_kv_2"][:, 3 * D:]}
    for j, x in enumerate("rkv"):
        w[f"rwkv_{x}"] = rkv[:, j * D:(j + 1) * D]
    for j, x in enumerate("qfig"):
        w[f"hgrn_{x}"] = hg[:, j * D:(j + 1) * D]
    for layer in range(2):
        w[f"xattn{layer}_q"], w[f"xattn{layer}_o"] = a["xattn_wq"][layer], a["xattn_wo"][layer]
    ffn = [(a["ffn1_w_in"][0], a["ffn1_w_out"][0]), (a["ffn2_w_in"][0], a["ffn2_w_out"][0]),
           (a["ffn1_w_in"][1], a["ffn1_w_out"][1]), (a["ffn2_w_in"][1], a["ffn2_w_out"][1])]
    ffn += [(a["ffn_w_in_2"][layer, j], a["ffn_w_out_2"][layer, j]) for layer in range(2) for j in range(2)]
    gate_up = np.arange(2 * FC).reshape(2, FC).T.reshape(-1)
    w8, w11 = [], []
    for st in plan(blocks)[0]:
        if st.name.startswith("ffn_in"):
            w8.append(slabs(ffn[int(st.name[-1])][0], 8, gate_up))
        elif st.name.startswith("ffn_out"):
            w11.append(slabs(ffn[int(st.name[-1])][1], WIDE))
        else:
            w8.append(slabs(w[st.name], 8))
    out["w8"], out["w11"] = np.concatenate(w8), np.concatenate(w11)
    extra_layout(out, a)
    return {n: np.ascontiguousarray(x) for n, x in out.items()}


def extra_layout(out, a):
    out["ws"] = a["gmlp_w_s"][0].transpose(2, 0, 1)
    out["bs"] = a["gmlp_b_s"][0].reshape(-1)
    out["bias_table"], pick = bias_constants()
    out["bias_rows"] = np.concatenate([a["rel_bias_2"], pick])
    for x in "wag":
        w1 = a[f"rwkv_{x}1"][0]
        out[f"lora_{x}1"] = w1.reshape(NC, P, -1).transpose(1, 0, 2)
    out["lora_w2"], out["lora_a2"] = a["rwkv_w2"][0], a["rwkv_a2"][0]
    out["lora_g2a"], out["lora_g2b"] = a["rwkv_g2"][0][:P], a["rwkv_g2"][0][P:]
    m = square_masks()
    out["lower"] = np.stack([m[f"pair{lv}"].T[:, np.arange(P) % (2 << lv) < (1 << lv)] for lv in range(1, 6)], 1).astype(np.float32)
    feature = np.arange(D) // HEAD
    out["to_heads"] = (np.arange(16)[:, None] == feature[None]).reshape(16, NC, P).astype(np.float32)
    out["sel"] = (feature.reshape(NC, P, 1) == np.arange(16)).transpose(1, 0, 2).reshape(P, NC * 16).astype(np.float32)


def kernel(**inputs):
    import concourse.bacc as bacc
    from concourse.bass_utils import run_bass_kernel_spmd

    arrays = lay_out(inputs, BLOCKS)
    counts = {}
    for _ in range(2):
        nc = bacc.Bacc("TRN2", target_bir_lowering=False, num_devices=1)
        io = {n: nc.dram_tensor(f"in_{n}", x.shape, F32, kind="ExternalInput").ap() for n, x in arrays.items()}
        io["out"] = nc.dram_tensor("out_x", (P, NC, T), F32, kind="ExternalOutput").ap()
        program(nc, io, BLOCKS, counts)
    r = run_bass_kernel_spmd(nc, [{f"in_{n}": x for n, x in arrays.items()}], core_ids=[0])
    return r.results[0]["out_x"].transpose(2, 1, 0).reshape(1, T, D)
```

```python
from contextlib import ExitStack
import math

import numpy as np
import concourse.bass as bass
from concourse import mybir

F32 = mybir.dt.float32
F32R = mybir.dt.float32r
I32 = mybir.dt.int32
ALU = mybir.AluOpType
ACT = mybir.ActivationFunctionType
AX = mybir.AxisListType

P = 128
T = 256
D = 1024
NC = D // P
F = 2816
FC = F // P
RING = 4
WIDE = FC // 2
EPS = 1e-6
KB = 1024
POOL_TILES = {8: 5, 11: 7}


class Steps:

    def __init__(self, sem, counts):
        self.sem, self.counts, self.n = sem, counts, 0

    def done(self, ins, label):
        ins.then_inc(self.sem, 1)
        self.n += 1
        self.counts[label] = self.n

    def wait(self, eng, label):
        eng.wait_ge(self.sem, self.counts.get(label, 1))


class Stage:

    def __init__(self, name, tiles, per_tile, width):
        self.name, self.tiles, self.per_tile, self.width = name, tiles, per_tile, width
        self.slabs = tiles * per_tile
        self.iters = self.slabs // RING
        assert self.slabs % RING == 0


def pack_columns(names_and_widths):
    at, out = 0, {}
    for name, width in names_and_widths:
        out[name] = at
        at += width // P
    return out, at


VECTORS = (
    [("mem_norm", D), ("final_norm", D), ("kv_norm", D)]
    + [(f"{n}{l}", D) for l in range(2) for n in ("ffn1_norm", "mix_norm", "xattn_norm", "ffn2_norm")]
    + [(f"norm_gain{l}{j}", D) for l in range(2) for j in range(3)]
    + [(f"mu{j}", D) for j in range(6)]
    + [(n, D) for n in ("w0", "a0", "k_k", "k_a", "r_k", "ln_w", "ln_b", "lb0", "lb1")]
    + [("v_norm", 2 * D), ("a_out_gain", P), ("k_gain", 3 * P), ("q_gain", 3 * P)]
)
COL, N_COLS = pack_columns(VECTORS)

LORA_W, LORA_A, LORA_G = 64, 64, 160
CHUNK = 64
HEAD = 64
GROUPS = 3
WINDOWS, DILATIONS = (128, 512, 2048), (1, 4, 16)
BUCKETS, MAX_DISTANCE = 32, 2048
REACH = 3 * P
NEG = -1e30


def square_masks():
    r, c = np.arange(P)[:, None], np.arange(P)[None, :]
    same = r // CHUNK == c // CHUNK
    m = {"identity": r == c, "ones": r + c >= 0, "head_ones": same,
         "strict": same & (r < c), "incl": same & (r <= c), "causal": r <= c}
    for lv in range(6):
        b = 1 << lv
        m[f"pair{lv}"] = (r // (2 * b) == c // (2 * b)) & (r % (2 * b) < b) & (c % (2 * b) >= b)
    m["pair0_lower"] = m["pair0"].T
    m["reset"] = (r >= 0) & (c % CHUNK > 0)
    m["pair6"] = (r < CHUNK) & (c >= CHUNK)
    return m


def column_masks():
    low = (np.arange(P) < CHUNK).astype(np.float32)
    cols = [low, 1 - low, -low, low - 1, np.full(P, EPS), np.full(P, 64e-5), np.ones(P),
            low * HEAD ** -0.5, (1 - low) * HEAD ** -0.5]
    cols += [np.full(P, j == 7) for j in range(15)]
    return np.stack(cols, 1).astype(np.float32)


LOW, HIGH, NEG_LOW, NEG_HIGH, C_EPS, C_GN_EPS, C_ONE, LOW_SCALED, HIGH_SCALED, ONE_HOT = range(10)
MASKS = ["identity", "ones", "head_ones", "strict", "incl", "causal"] + [f"pair{lv}" for lv in range(7)] + ["pair0_lower", "reset"]


def bias_constants():
    dist = T - 1 - np.arange(REACH)
    d = np.maximum(dist, 0)
    exact = BUCKETS // 2
    large = exact + (np.log(np.maximum(d, 1) / exact) / math.log(MAX_DISTANCE / exact) * (BUCKETS - exact)).astype(np.int32)
    bucket = np.where(d < exact, d, np.minimum(large, BUCKETS - 1))
    table = np.zeros((BUCKETS + GROUPS, REACH), np.float32)
    table[bucket, np.arange(REACH)] = 1.0
    table[:BUCKETS, dist < 0] = 0.0
    for g in range(GROUPS):
        ok = (dist >= 0) & (dist <= WINDOWS[g]) & (dist % DILATIONS[g] == 0)
        table[BUCKETS + g] = np.where(ok, 0.0, NEG)
    pick = np.kron(np.eye(GROUPS), np.ones((1, 16))).astype(np.float32)
    return table, pick


def plan(blocks):
    st = []
    for b in blocks:
        if b.startswith("ffn"):
            st.append(Stage(f"ffn_in{b[3]}", 2 * FC, 1, 8))
            st.append(Stage(f"ffn_out{b[3]}", NC, 2, WIDE))
        elif b == "mem":
            st.append(Stage("mem_kv", 2 * NC, 1, 8))
        elif b == "rwkv":
            st.extend(Stage(f"rwkv_{x}", NC, 1, 8) for x in "rkv")
            if "mem" in blocks:
                st.append(Stage("mem_kv", 2 * NC, 1, 8))
            st.append(Stage("rwkv_o", NC, 1, 8))
        elif b.startswith("xattn"):
            st.extend(Stage(f"{b}_{x}", NC, 1, 8) for x in "qo")
        elif b == "gmlp":
            st.append(Stage("gmlp_uv", 4 * NC, 1, 8))
            st.append(Stage("gmlp_o", NC, 2, 8))
        elif b == "hgrn":
            st.extend(Stage(f"hgrn_{x}", NC, 1, 8) for x in "qfigo")
        elif b == "kv":
            st.extend(Stage(f"dil_{x}{g}", NC, 1, 8) for x in "kv" for g in range(GROUPS))
        elif b == "dil":
            st.extend(Stage(f"dil_q{g}", NC, 1, 8) for g in range(GROUPS))
            st.append(Stage("dil_o", NC, 1, 8))
    seen, out = set(), []
    for s in st:
        if s.name not in seen:
            seen.add(s.name)
            out.append(s)
    base, row = 0, {8: 0, WIDE: 0}
    for s in out:
        s.base, s.row = base, row[s.width]
        base += s.slabs
        row[s.width] += s.slabs
    for s, nxt in zip(out, out[1:] + [None]):
        s.ahead = nxt.width if nxt else 0
    return out, base, row


BLOCKS = ["ffn0", "rwkv", "mem", "xattn0", "ffn1", "ffn2", "gmlp", "xattn1", "ffn3", "final",
          "ffn4", "hgrn", "ffn5", "kv", "ffn6", "dil", "ffn7"]
GAIN_OF = {"ffn0": "ffn1_norm0", "rwkv": "mix_norm0", "xattn0": "xattn_norm0", "ffn1": "ffn2_norm0",
           "ffn2": "ffn1_norm1", "gmlp": "mix_norm1", "xattn1": "xattn_norm1", "ffn3": "ffn2_norm1",
           "ffn4": "norm_gain00", "hgrn": "norm_gain01", "ffn5": "norm_gain02", "kv": "kv_norm",
           "ffn6": "norm_gain10", "dil": "norm_gain11", "ffn7": "norm_gain12"}

UNSPLIT = ("final_norm", "mix_norm0")


def run(eng, stage, body, between=None):
    if between:
        assert stage.iters == 2
        body(0, stage.width)
        between()
        body(1, stage.ahead)
        return
    full = stage.iters if stage.ahead == stage.width else stage.iters - 1
    if full > 1:
        with eng.Fori(0, full) as i:
            body(i, stage.width)
    elif full == 1:
        body(0, stage.width)
    if full < stage.iters:
        body(stage.iters - 1, stage.ahead)


def bcast(ap, n):
    return ap.unsqueeze(1).broadcast_to([P, n, ap.shape[-1]])


class Resources:

    def __init__(self, nc, ctx, io, counts):
        self.nc, self.io = nc, io

        def sb(name, shape, dt=F32):
            return ctx.enter_context(nc.sbuf_tensor(name, shape, dt))

        def sem(name):
            return ctx.enter_context(nc.semaphore(name))

        self.raw = sb("raw", [P, RING, WIDE * P])
        self.hi = sb("hi", [P, RING, WIDE * P], F32R)
        self.lo = sb("lo", [P, RING, WIDE * P], F32R)
        self.X = sb("X", [P, NC, T])
        self.R = sb("R", [P, T])
        self.STD = sb("STD", [P, T])
        self.SQSUM = sb("SQSUM", [P, T])
        self.SQ = sb("SQ", [P, 2, T])
        self.vec = sb("vec", [P, N_COLS])
        self.cols = sb("cols", [P, ONE_HOT + 15])
        self.masks = sb("masks", [P, len(MASKS), P])
        self.sel = sb("sel", [P, NC * 16])
        self.base = -(-nc.sbuf_base // 64) * 64
        self.room = nc.sbuf_usable_end - self.base
        self.arena = sb("arena", [P, (self.room - 128) // 4])
        self.limit = self.room - 128

        self.Hh = self.at("Hh", 0, [P, NC, T], F32R)
        self.Hl = self.at("Hl", 8 * KB, [P, NC, T], F32R)
        self.memk = self.at("memk", 16 * KB, [P, NC, T])
        self.memv = self.at("memv", 24 * KB, [P, 2, D])
        self.gate = self.at("gate", 32 * KB, [P, 2, T])
        self.sgate = self.at("sgate", 34 * KB, [P, 2, T])
        self.up = self.at("up", 36 * KB, [P, 2, T])
        self.act32 = self.at("act32", 38 * KB, [P, 2, T])
        self.A0 = 40 * KB
        self.Ah = self.at("Ah", self.A0, [P, FC, T], F32R)
        self.Al = self.at("Al", self.A0 + 22 * KB, [P, FC, T], F32R)

        self.bank = [ctx.enter_context(nc.psum_tensor(f"bank{b}", [P, 512], F32)) for b in range(8)]

        self.ident, self.ones, self.head_ones = self.mask("identity"), self.mask("ones"), self.mask("head_ones")

        self.landed = [sem(f"slab_landed{q}") for q in range(RING)]
        self.hi_ready = sem("hi_ready")
        self.lo_pool = sem("lo_ready_pool")
        self.lo_dve = sem("lo_ready_dve")
        self.slab_used = sem("slab_used")
        self.banks_freed = sem("banks_freed")
        self.h_hi, self.h_lo = sem("h_hi_ready"), sem("h_lo_ready")
        self.sq_ready, self.sq_added = sem("square_ready"), sem("square_added")
        self.ss_ready, self.std_ready, self.rstd_ready = sem("sumsq_ready"), sem("std_ready"), sem("rstd_ready")
        self.gate_scaled, self.silu_done = sem("gate_scaled"), sem("silu_done")
        self.a_ready, self.ah_ready, self.al_ready = sem("a_ready"), sem("ah_ready"), sem("al_ready")
        self.gelu_done = sem("gelu_done")
        self.proj_act = sem("projection_activated")
        self.loaded = sem("small_loads")
        self.x_loaded = [sem(f"x_half{h}_loaded") for h in range(2)]
        self.mem_loaded = sem("mem_loaded")
        self.x_scaled = sem("x_scaled")
        self.mixer_loads = sem("mixer_loads")
        self.mixer_stores = sem("mixer_stores")
        self.values_stored = [sem(f"values_stored{q}") for q in range(4)]
        self.pair_loaded = [sem(f"pair_loaded{q}") for q in range(2)]
        self.values_loaded = [sem(f"values_loaded{q}") for q in range(2)]
        self.out_stored = sem("out_stored")
        self.pe_done = Steps(sem("mixer_products"), counts.setdefault("mixer_products", {}))
        self.act_done = Steps(sem("mixer_activations"), counts.setdefault("mixer_activations", {}))
        self.dve_done = Steps(sem("mixer_vectors"), counts.setdefault("mixer_vectors", {}))
        self.pool_done = Steps(sem("mixer_pool"), counts.setdefault("mixer_pool", {}))

        self.loads_before = 0

    def at(self, name, offset, shape, dt=F32):
        size = 4 * int(np.prod(shape[1:]))
        assert offset + size <= self.limit, (name, offset, size, self.limit)
        return self.nc.alloc_sbuf_tensor_at(name, shape, dt, offset=self.base + offset)

    def mask(self, name, n=1):
        i = MASKS.index(name)
        return self.masks[:, i, :] if n == 1 else self.masks[:, i:i + n, :]

    def v1(self, name, c):
        return self.vec[:, COL[name] + c:COL[name] + c + 1]

    def col(self, i):
        return self.cols[:, i:i + 1]


class Shared:

    def __init__(self, k, blocks):
        self.k, self.blocks = k, blocks
        self.stages, self.n_slabs, self.rows = plan(blocks)
        self.stage = {s.name: s for s in self.stages}
        self.split_n = {"act": 0, "dve": 0, "pe": 0}
        self.square_n = {"act": 0, "dve": 0, "pe": 0}
        self.norm_n = {"act": 0, "dve": 0, "pe": 0}

    def act_hi(self, act, s, q, width, turn):
        k, w = self.k, width * P
        if not width:
            return
        act.wait_ge(k.landed[q], 16 * (turn + 1))
        if not (isinstance(s, int) and s < RING):
            act.wait_ge(k.slab_used, s - (RING - 1))
        act.activation(k.hi[:, q, :w], k.raw[:, q, :w], ACT.Copy).then_inc(k.hi_ready, 1)

    def dve_lo(self, dve, s, q, width):
        k = self.k
        if not width:
            return
        a, w = POOL_TILES[width] * P, width * P
        dve.wait_ge(k.hi_ready, s + 1)
        dve.tensor_tensor(k.lo[:, q, a:w], k.raw[:, q, a:w], k.hi[:, q, a:w].bitcast(F32),
                          ALU.subtract).then_inc(k.lo_dve, 1)

    def pool_lo(self, pool, s, q, width):
        k = self.k
        if not width:
            return
        a = POOL_TILES[width] * P
        pool.wait_ge(k.hi_ready, s + 1)
        pool.tensor_tensor(k.lo[:, q, :a], k.raw[:, q, :a], k.hi[:, q, :a].bitcast(F32),
                           ALU.subtract).then_inc(k.lo_pool, 1)

    def sp_stage(self, sp, st):
        k = self.k
        src, w = (k.io["w8"], 8 * P) if st.width == 8 else (k.io["w11"], WIDE * P)

        def body(i, _):
            for q in range(RING):
                s = st.base + RING * i + q
                if not (isinstance(s, int) and s < RING):
                    sp.wait_ge(k.lo_pool, s - (RING - 1))
                    sp.wait_ge(k.lo_dve, s - (RING - 1))
                sp.dma_start(k.raw[:, q, :w], src[bass.ds(st.row + RING * i + q, 1), :, :].rearrange(
                    "a p w -> p (a w)")).then_inc(k.landed[q], 16)

        first = 1 if st.base == 0 else 0
        if first:
            body(0, 0)
        if st.iters - first > 1:
            with sp.Fori(first, st.iters) as i:
                body(i, 0)
        elif st.iters > first:
            body(first, 0)

    def pool_stage(self, pool, st):
        def body(i, ahead):
            for q in range(RING):
                self.pool_lo(pool, st.base + RING * i + q + RING, q, ahead)
        run(pool, st, body)

    def act_stage(self, act, st, follow=None):
        k = self.k

        def body(i, ahead):
            for q in range(RING):
                if follow:
                    follow(i, q)
                self.act_hi(act, st.base + RING * i + q + RING, q, ahead, st.base // RING + i + 1)
        run(act, st, body)

    def pe_stage(self, pe, st, moving, ready, between=None, after_first=None):
        k = self.k

        def body(i, after_first=None):
            for q in range(RING):
                if q == 1 and after_first:
                    after_first()
                s, kg = st.base + RING * i + q, q % st.per_tile
                pe.wait_ge(k.lo_pool, s + 1)
                pe.wait_ge(k.lo_dve, s + 1)
                if kg == 0:
                    pe.wait_ge(k.banks_freed, s + 1)
                out = k.bank[q - kg][:, :T]
                for kc in range(st.width):
                    if q < st.per_tile:
                        ready(kg, kc)
                    xh, xl = moving(kg, kc)
                    wh, wl = (w[:, q, kc * P:(kc + 1) * P] for w in (k.hi, k.lo))
                    first, last = kg == kc == 0, kg == st.per_tile - 1 and kc == st.width - 1
                    pe.matmul(out, wh, xh, start=first, stop=False)
                    pe.matmul(out, wh, xl, start=False, stop=False)
                    mm = pe.matmul(out, wl, xh, start=False, stop=last)
                mm.then_inc(k.slab_used, 1)
        if between:
            assert st.iters == 2
            body(0)
            between()
            body(1)
        elif after_first:
            body(0, after_first)
            with pe.Fori(1, st.iters) as i:
                body(i)
        else:
            with pe.Fori(0, st.iters) as i:
                body(i)

    def pe_first_stage(self, pe, st):
        self.split_n["pe"] += NC
        self.pe_stage_h(pe, st, lambda: self.norm(pe, "pe"))

    def pe_stage_h(self, pe, st, after_first=None):
        k, n = self.k, self.split_n["pe"] - NC
        self.pe_stage(pe, st, lambda kg, kc: (k.Hh[:, kc, :], k.Hl[:, kc, :]),
                      lambda kg, kc: pe.wait_ge(k.h_lo, n + kc + 1), after_first=after_first)

    def dve_project(self, dve, st, dest, scaled=True, before=None, between=None):
        k = self.k
        if scaled:
            dve.wait_ge(k.rstd_ready, self.norm_n["dve"])

        def body(i, ahead):
            for q in range(RING):
                s = st.base + RING * i + q
                dve.wait_ge(k.slab_used, s + 1)
                if before:
                    before(i, q)
                if scaled:
                    ins = dve.tensor_tensor(dest(i, q), k.bank[q][:, :T], k.R[:], ALU.mult)
                else:
                    ins = dve.tensor_copy(dest(i, q), k.bank[q][:, :T])
                ins.then_inc(k.banks_freed, 1)
                self.dve_lo(dve, s + RING, q, ahead)
        run(dve, st, body, between)

    def prep(self, eng, e, src, gain, c, split=True, square=True, wait=None):
        k = self.k
        ns, nq = self.split_n[e] + c, self.square_n[e] + c
        if e == "act":
            if wait:
                wait(c)
            if split:
                eng.activation(k.Hh[:, c, :], src[:, c, :], ACT.Copy, scale=k.v1(gain, c)).then_inc(k.h_hi, 1)
            if square:
                if nq >= 2:
                    eng.wait_ge(k.sq_added, nq - 1)
                eng.activation(k.SQ[:, c % 2, :], src[:, c, :], ACT.Square).then_inc(k.sq_ready, 1)
        else:
            if split:
                eng.wait_ge(k.h_hi, ns + 1)
                eng.scalar_tensor_tensor(k.Hl[:, c, :], src[:, c, :], k.v1(gain, c),
                                         k.Hh[:, c, :].bitcast(F32), ALU.mult, ALU.subtract).then_inc(k.h_lo, 1)
            if square:
                eng.wait_ge(k.sq_ready, nq + 1)
                if c == 0:
                    if self.norm_n["dve"]:
                        eng.wait_ge(k.ss_ready, self.norm_n["dve"])
                    ins = eng.tensor_copy(k.SQSUM[:], k.SQ[:, 0, :])
                else:
                    eng.wait_ge(k.sq_added, nq)
                    ins = eng.tensor_tensor(k.SQSUM[:], k.SQSUM[:], k.SQ[:, c % 2, :], ALU.add)
                ins.then_inc(k.sq_added, 1)

    def prep_all(self, eng, e, src, gain, split=True, square=True, wait=None):
        for c in range(NC):
            self.prep(eng, e, src, gain, c, split, square, wait)
        self.prepped(e, split, square)

    def prepped(self, e, split=True, square=True):
        self.split_n[e] += NC * split
        self.square_n[e] += NC * square

    def act_resid(self, act, st, gain):
        k, split = self.k, gain not in UNSPLIT
        for c in range(NC):
            s = st.base + c * st.per_tile
            if gain:
                self.prep(act, "act", k.X, gain, c, split,
                          wait=lambda _: act.wait_ge(k.banks_freed, RING + s + st.per_tile))
            for kg in range(st.per_tile):
                w = st.width if s + kg + RING < st.base + st.slabs else st.ahead
                self.act_hi(act, s + kg + RING, (s + kg) % RING, w, (s + kg) // RING + 1)
        if gain:
            self.prepped("act", split)

    def dve_resid(self, dve, st, coef, gain):
        k, split = self.k, gain not in UNSPLIT
        for c in range(NC):
            s = st.base + c * st.per_tile
            dve.wait_ge(k.slab_used, s + st.per_tile)
            dve.scalar_tensor_tensor(k.X[:, c, :], k.bank[s % RING][:, :T], coef, k.X[:, c, :],
                                     ALU.mult, ALU.add).then_inc(k.banks_freed, st.per_tile)
            if gain:
                dve.wait_ge(k.banks_freed, RING + s + st.per_tile)
                self.prep(dve, "dve", k.X, gain, c, split)
            for kg in range(st.per_tile):
                w = st.width if s + kg + RING < st.base + st.slabs else st.ahead
                self.dve_lo(dve, s + kg + RING, (s + kg) % RING, w)
        if gain:
            self.prepped("dve", split)

    def norm(self, eng, e):
        k, n = self.k, self.norm_n[e]
        if e == "pe":
            self.square_n["pe"] += NC
            eng.wait_ge(k.sq_added, self.square_n["pe"])
            eng.matmul(k.bank[4][:, :T], k.ones, k.SQSUM[:], start=True, stop=True).then_inc(k.ss_ready, 1)
        elif e == "act":
            eng.wait_ge(k.ss_ready, n + 1)
            if n:
                eng.wait_ge(k.rstd_ready, n)
            eng.activation(k.STD[:], k.bank[4][:, :T], ACT.Sqrt, bias=k.col(C_EPS), scale=1.0 / D).then_inc(k.std_ready, 1)
        else:
            eng.wait_ge(k.std_ready, n + 1)
            eng.reciprocal(k.R[:], k.STD[:]).then_inc(k.rstd_ready, 1)
        self.norm_n[e] += 1


class FeedForward:

    def __init__(self, sh, name, order, nxt, own_norm=True):
        self.sh, self.k, self.n, self.next_gain, self.own_norm = sh, sh.k, order, nxt, own_norm
        self.st_in, self.st_out = sh.stage[f"ffn_in{name[3]}"], sh.stage[f"ffn_out{name[3]}"]

    def pe(self, pe):
        sh, k = self.sh, self.k
        if self.own_norm:
            sh.pe_first_stage(pe, self.st_in)
        else:
            sh.split_n["pe"] += NC
            sh.pe_stage_h(pe, self.st_in)
        done = 2 + FC * self.n
        sh.pe_stage(pe, self.st_out,
                    lambda kg, kc: (k.Ah[:, kg * WIDE + kc, :], k.Al[:, kg * WIDE + kc, :]),
                    lambda kg, kc: pe.wait_ge(k.al_ready, done + WIDE * (kg + 1)) if kc == 0 else None)

    def act(self, act):
        sh, k, st = self.sh, self.k, self.st_in
        if self.own_norm:
            sh.norm(act, "act")

        def body(i, ahead):
            for j in range(2):
                m, s = 2 * i + j, st.base + RING * i + 2 * j
                g = FC * self.n + m
                turn = st.base // RING + i + 1
                act.wait_ge(k.gate_scaled, g + 1)
                act.wait_ge(k.a_ready, g + 1)
                act.activation(k.sgate[:, j, :], k.gate[:, j, :], ACT.Silu).then_inc(k.silu_done, 1)
                sh.act_hi(act, s + RING, 2 * j, ahead, turn)
                act.wait_ge(k.a_ready, g + 3)
                act.activation(k.Ah[:, bass.ds(m, 1), :].rearrange("p a t -> p (a t)"), k.act32[:, j, :],
                               ACT.Copy).then_inc(k.ah_ready, 1)
                sh.act_hi(act, s + 1 + RING, 2 * j + 1, ahead, turn)
        run(act, st, body)
        sh.act_resid(act, self.st_out, self.next_gain)

    def dve(self, dve):
        sh, k, st = self.sh, self.k, self.st_in
        if self.own_norm:
            sh.norm(dve, "dve")
        dve.wait_ge(k.rstd_ready, sh.norm_n["dve"])

        def body(i, ahead):
            for j in range(2):
                m, s = 2 * i + j, st.base + RING * i + 2 * j
                g = FC * self.n + m
                dve.wait_ge(k.slab_used, s + 1)
                dve.wait_ge(k.silu_done, g + 1)
                dve.tensor_tensor(k.gate[:, j, :], k.bank[2 * j][:, :T], k.R[:], ALU.mult).then_inc(k.gate_scaled, 1)
                dve.wait_ge(k.slab_used, s + 2)
                dve.wait_ge(k.a_ready, g + 1)
                dve.tensor_tensor(k.up[:, j, :], k.bank[2 * j + 1][:, :T], k.R[:], ALU.mult).then_inc(k.banks_freed, 2)
                sh.dve_lo(dve, s + RING, 2 * j, ahead)
                dve.wait_ge(k.silu_done, g + 3)
                dve.wait_ge(k.banks_freed, RING + s + 2)
                dve.wait_ge(k.al_ready, g + 1)
                dve.tensor_tensor(k.act32[:, j, :], k.sgate[:, j, :], k.up[:, j, :], ALU.mult).then_inc(k.a_ready, 1)
                dve.wait_ge(k.ah_ready, g + 1)
                dve.wait_ge(k.a_ready, g + 3)
                dve.tensor_tensor(k.Al[:, bass.ds(m, 1), :].rearrange("p a t -> p (a t)"), k.act32[:, j, :],
                                  k.Ah[:, bass.ds(m, 1), :].rearrange("p a t -> p (a t)").bitcast(F32),
                                  ALU.subtract).then_inc(k.al_ready, 1)
                sh.dve_lo(dve, s + 1 + RING, 2 * j + 1, ahead)
        run(dve, st, body)
        sh.dve_resid(dve, self.st_out, 0.5, self.next_gain)

    def stage_list(self):
        return [self.st_in, self.st_out]

    def pool(self, pool):
        for st in self.stage_list():
            self.sh.pool_stage(pool, st)


class Memory:

    def __init__(self, sh):
        self.sh, self.k, self.st = sh, sh.k, sh.stage["mem_kv"]
        k = sh.k
        self.M = k.at("mem_x", k.A0, [P, NC, T])
        self.VT = k.at("mem_vt", k.A0 + 8 * KB, [P, NC, T])

    def pe(self, pe):
        self.pe_project(pe)
        self.pe_values(pe)

    def act(self, act):
        self.act_start(act)
        self.act_finish(act)

    def dve(self, dve):
        self.dve_start(dve)
        self.dve_finish(dve)

    def pe_project(self, pe):
        sh = self.sh
        sh.pe_first_stage(pe, self.st)

    def pe_values(self, pe):
        k = self.k
        for b in range(4):
            pe.wait_ge(k.banks_freed, RING + self.st.base + NC + 2 * b + 2)
            for j in range(4):
                c, half = 2 * b + j // 2, j % 2
                ins = pe.transpose(k.bank[4 + b][:, j * P:(j + 1) * P], self.VT[:, c, half * P:(half + 1) * P], k.ident)
            k.pe_done.done(ins, f"mem.vt{b}")

    def act_start(self, act):
        sh, k = self.sh, self.k
        sh.prep_all(act, "act", self.M, "mem_norm", wait=lambda _: act.wait_ge(k.mem_loaded, 16))
        sh.norm(act, "act")

    def act_finish(self, act):
        sh, k = self.sh, self.k
        sh.act_stage(act, self.st)
        for b in range(4):
            k.pe_done.wait(act, f"mem.vt{b}")
            src = k.bank[4 + b][:].rearrange("p (c h j) -> p c h j", c=2, h=2)
            dst = k.memv[:, :, 2 * b * P:(2 * b + 2) * P].rearrange("p h (c j) -> p c h j", c=2)
            k.act_done.done(act.activation(dst, src, ACT.Copy), f"mem.v{b}")

    def dve_start(self, dve):
        sh, k = self.sh, self.k
        dve.wait_ge(k.mem_loaded, 16)
        sh.prep_all(dve, "dve", self.M, "mem_norm")
        sh.norm(dve, "dve")

    def dve_finish(self, dve):
        sh, k = self.sh, self.k
        dve.wait_ge(k.rstd_ready, sh.norm_n["dve"])
        for s in range(self.st.slabs):
            at, q = self.st.base + s, s % RING
            out = (k.memk if s < NC else self.VT)[:, s % NC, :]
            dve.wait_ge(k.slab_used, at + 1)
            dve.tensor_tensor(out, k.bank[q][:, :T], k.R[:], ALU.mult).then_inc(k.banks_freed, 1)
            sh.dve_lo(dve, at + RING, q, self.st.width if s + RING < self.st.slabs else self.st.ahead)

    def pool(self, pool):
        self.sh.pool_stage(pool, self.st)


class CrossAttention:
    HEADS, DH = 4, 256

    def __init__(self, sh, name, nxt):
        self.sh, self.k, self.name, self.next_gain = sh, sh.k, name, nxt
        self.sq, self.so = sh.stage[f"{name}_q"], sh.stage[f"{name}_o"]
        k = sh.k
        a, n = k.A0, name
        self.Q = k.at(n + "Q", a, [P, NC, T])
        self.Oh = k.at(n + "Oh", a + 8 * KB, [P, NC, T], F32R)
        self.Ol = k.at(n + "Ol", a + 16 * KB, [P, NC, T], F32R)
        self.E = k.at(n + "E", a + 24 * KB, [P, 2, 2, T])
        self.ET = k.at(n + "ET", a + 28 * KB, [P, 2, 2 * T])
        self.st = k.at(n + "st", a + 32 * KB, [P, 4, 4, 2])

    def pe(self, pe):
        sh, k, n = self.sh, self.k, self.name
        sh.pe_first_stage(pe, self.sq)

        def scores(h):
            pe.wait_ge(k.banks_freed, RING + self.sq.base + 2 * h + 2)
            if h == 0:
                pe.wait_ge(k.rstd_ready, sh.norm_n["pe"])
                k.act_done.wait(pe, "mem.v3")
            if h >= 2:
                k.act_done.wait(pe, f"{n}.exp{h - 2}")
            for half in range(2):
                for c in range(2):
                    ins = pe.matmul(k.bank[4 + h % 2][:, half * T:(half + 1) * T],
                                    self.Q[:, 2 * h + c, half * P:(half + 1) * P], k.memk[:, 2 * h + c, :],
                                    start=c == 0, stop=c == 1)
            k.pe_done.done(ins, f"{n}.s{h}")

        def output(h):
            k.act_done.wait(pe, f"{n}.et{h}")
            if h:
                k.dve_done.wait(pe, f"{n}.ol{h - 1}")
            for c in range(2):
                for slots in range(2):
                    f = h * self.DH + c * P
                    ins = pe.matmul(k.bank[7][:, c * T:(c + 1) * T], k.memv[:, slots, f:f + P],
                                    self.ET[:, h % 2, slots * T:(slots + 1) * T], start=slots == 0, stop=slots == 1)
            k.pe_done.done(ins, f"{n}.o{h}")

        scores(0)
        for h in range(self.HEADS):
            if h + 1 < self.HEADS:
                scores(h + 1)
            if h:
                output(h - 1)
            k.dve_done.wait(pe, f"{n}.p{h}")
            if h:
                k.act_done.wait(pe, f"{n}.et{h - 1}")
            for slots in range(2):
                for half in range(2):
                    j = 2 * slots + half
                    ins = pe.transpose(k.bank[6][:, j * P:(j + 1) * P],
                                       self.E[:, h % 2, half, slots * P:(slots + 1) * P], k.ident)
            k.pe_done.done(ins, f"{n}.t{h}")
        output(self.HEADS - 1)
        sh.pe_stage(pe, self.so, lambda kg, kc: (self.Oh[:, kc, :], self.Ol[:, kc, :]),
                    lambda kg, kc: k.dve_done.wait(pe, f"{n}.ol{kc // 2}"))

    def act(self, act):
        sh, k, n = self.sh, self.k, self.name
        sh.norm(act, "act")
        sh.act_stage(act, self.sq)

        def exponentials(h):
            k.dve_done.wait(act, f"{n}.nmax{h}")
            if h >= 2:
                k.pe_done.wait(act, f"{n}.t{h - 2}")
            for half in range(2):
                ins = act.activation(self.E[:, h % 2, half, :], k.bank[4 + h % 2][:, half * T:(half + 1) * T], ACT.Exp,
                                     bias=self.st[:, h, 1, half:half + 1], scale=1.0 / 16,
                                     accum_out=self.st[:, h, 2, half:half + 1])
                k.act_done.done(ins, f"{n}.exp{h}")

        exponentials(0)
        for h in range(self.HEADS):
            if h + 1 < self.HEADS:
                exponentials(h + 1)
            k.pe_done.wait(act, f"{n}.t{h}")
            if h >= 2:
                k.pe_done.wait(act, f"{n}.o{h - 2}")
            k.act_done.done(act.activation(self.ET[:, h % 2, :], k.bank[6][:], ACT.Copy), f"{n}.et{h}")
            k.pe_done.wait(act, f"{n}.o{h}")
            out = self.Oh[:, 2 * h:2 * h + 2, :].rearrange("p c t -> p (c t)")
            k.act_done.done(act.activation(out, k.bank[7][:], ACT.Copy), f"{n}.oh{h}")
        sh.act_resid(act, self.so, self.next_gain)

    def dve(self, dve):
        sh, k, n = self.sh, self.k, self.name
        sh.norm(dve, "dve")
        sh.dve_project(dve, self.sq, lambda i, q: self.Q[:, bass.ds(RING * i + q, 1), :].rearrange("p a t -> p (a t)"))

        def maximum(h):
            k.pe_done.wait(dve, f"{n}.s{h}")
            src = k.bank[4 + h % 2][:].rearrange("p (b m) -> p b m", b=2)
            k.dve_done.done(dve.tensor_reduce(self.st[:, h, 0, :], src, AX.X, ALU.max), f"{n}.max{h}")
            k.dve_done.wait(dve, f"{n}.max{h}")
            k.dve_done.done(dve.tensor_scalar(self.st[:, h, 1, :], self.st[:, h, 0, :], -1.0 / 16, None, ALU.mult), f"{n}.nmax{h}")

        def low(h):
            k.act_done.wait(dve, f"{n}.oh{h}")
            k.dve_done.done(dve.tensor_tensor(self.Ol[:, 2 * h:2 * h + 2, :].rearrange("p c t -> p (c t)"), k.bank[7][:],
                                              self.Oh[:, 2 * h:2 * h + 2, :].rearrange("p c t -> p (c t)").bitcast(F32),
                                              ALU.subtract), f"{n}.ol{h}")

        maximum(0)
        for h in range(self.HEADS):
            if h + 1 < self.HEADS:
                maximum(h + 1)
            k.act_done.wait(dve, f"{n}.exp{h}")
            k.dve_done.done(dve.reciprocal(self.st[:, h, 3, :], self.st[:, h, 2, :]), f"{n}.rs{h}")
            k.dve_done.wait(dve, f"{n}.rs{h}")
            for half in range(2):
                e = self.E[:, h % 2, half, :]
                k.dve_done.done(dve.tensor_scalar(e, e, self.st[:, h, 3, half:half + 1], None, ALU.mult), f"{n}.p{h}")
            if h:
                low(h - 1)
        low(self.HEADS - 1)
        sh.dve_resid(dve, self.so, 1.0, self.next_gain)

    def pool(self, pool):
        self.sh.pool_stage(pool, self.sq)
        self.sh.pool_stage(pool, self.so)


class GatedMlp:
    G = 16

    def __init__(self, sh, name, nxt):
        self.sh, self.k, self.next_gain = sh, sh.k, nxt
        self.uv, self.so = sh.stage["gmlp_uv"], sh.stage["gmlp_o"]
        k, a = sh.k, sh.k.A0
        self.UV = k.at("gUV", a, [P, 2 * self.G, T])
        self.U, self.V = self.UV[:, :self.G, :], self.UV[:, self.G:, :]
        self.Gh = k.at("gGh", a + 16 * KB, [P, self.G, T], F32R)
        self.VT = k.at("gVT", a + 32 * KB, [P, 2 * self.G, P])
        self.WS = k.at("gWS", a + 48 * KB, [P, self.G, P])
        self.BS = k.at("gBS", a + 56 * KB, [P, self.G, P])
        self.TMP = k.at("gTMP", a + 64 * KB, [P, 4, T])
        self.SQ = k.at("gSQ", a + 68 * KB, [P, 4, T])
        self.Gl = k.at("gGl", a + 64 * KB, [P, self.G - 4, T], F32R)
        self.Gl2 = k.at("gGl2", 36 * KB, [P, 4, T], F32R)
        self.T2 = k.at("gT2", 32 * KB, [P, 2, 2, T])

        self.loads = 32 + k.loads_before
        k.loads_before += 32

    def low(self, g, n):
        return self.Gl[:, g:g + n, :] if g < 12 else self.Gl2[:, g - 12:g - 12 + n, :]

    def pe(self, pe):
        sh, k, G = self.sh, self.k, self.G
        sh.pe_first_stage(pe, self.uv)
        for j in range(4):
            k.act_done.wait(pe, f"g.sq{j}")
            if j == 0:
                pe.wait_ge(k.rstd_ready, sh.norm_n["pe"])
            for c in range(4):
                ins = pe.matmul(k.bank[4][:, :T], k.ones, self.SQ[:, c, :], start=j == c == 0, stop=j == c == 3)
            k.pe_done.done(ins, f"g.ss{j}")
        for b in range(8):
            k.dve_done.wait(pe, f"g.vn{2 * b + 1}")
            if b >= 4:
                k.act_done.wait(pe, f"g.vt{b - 4}")
            for j in range(4):
                g, chunk = 2 * b + j // 2, j % 2
                ins = pe.transpose(k.bank[b % 4][:, j * P:(j + 1) * P], self.V[:, g, chunk * P:(chunk + 1) * P], k.ident)
            k.pe_done.done(ins, f"g.vt{b}")
        k.dve_done.wait(pe, "g.ws")
        for b in range(8):
            k.act_done.wait(pe, f"g.vt{b}")
            if b >= 4:
                k.dve_done.wait(pe, f"g.sv{b - 4}")
            else:
                k.act_done.wait(pe, "g.std")
            for j in range(4):
                g, chunk = 2 * b + j // 2, j % 2
                ins = pe.matmul(k.bank[4 + b % 4][:, j * P:(j + 1) * P], self.VT[:, 2 * g + chunk, :],
                                self.WS[:, g, :], start=True, stop=True)
            k.pe_done.done(ins, f"g.sv{b}")
        sh.pe_stage(pe, self.so, lambda kg, kc: (self.Gh[:, 8 * kg + kc, :], self.low(8 * kg + kc, 1)[:, 0, :]),
                    lambda kg, kc: k.dve_done.wait(pe, f"g.gl{(8 * kg + kc) // 2}"))

    def act(self, act):
        sh, k, st = self.sh, self.k, self.uv
        act.dma_start(self.WS[:], k.io["ws"]).then_inc(k.mixer_loads, 16)
        act.dma_start(self.BS[:], k.io["bs"].partition_broadcast(P)).then_inc(k.mixer_loads, 16)
        sh.norm(act, "act")

        def follow(i, q):
            act.wait_ge(k.banks_freed, RING + st.base + RING * i + q + 1)
            out = self.UV[:, bass.ds(RING * i + q, 1), :].rearrange("p a t -> p (a t)")
            act.activation(out, self.TMP[:, q, :], ACT.Gelu_apprx_tanh).then_inc(k.gelu_done, 1)
        sh.act_stage(act, st, follow)
        act.wait_ge(k.gelu_done, RING + st.slabs)
        for j in range(4):
            if j:
                k.pe_done.wait(act, f"g.ss{j - 1}")
            k.act_done.done(act.activation(self.SQ[:], self.V[:, 4 * j:4 * j + 4, :], ACT.Square), f"g.sq{j}")
        k.pe_done.wait(act, "g.ss3")
        k.act_done.done(act.activation(k.STD[:], k.bank[4][:, :T], ACT.Sqrt, bias=k.col(C_EPS),
                                       scale=1.0 / (2 * D)), "g.std")
        for b in range(8):
            k.pe_done.wait(act, f"g.vt{b}")
            out = self.VT[:, 4 * b:4 * b + 4, :].rearrange("p a d -> p (a d)")
            k.act_done.done(act.activation(out, k.bank[b % 4][:], ACT.Copy), f"g.vt{b}")
        for b in range(8):
            k.dve_done.wait(act, f"g.usv{b}")
            k.act_done.done(act.activation(self.Gh[:, 2 * b:2 * b + 2, :], self.U[:, 2 * b:2 * b + 2, :], ACT.Copy), f"g.gh{b}")
        sh.act_resid(act, self.so, self.next_gain)

    def dve(self, dve):
        sh, k, st = self.sh, self.k, self.uv
        sh.norm(dve, "dve")
        dve.wait_ge(k.mixer_loads, self.loads)
        causal = bcast(k.mask("causal"), self.G)
        k.dve_done.done(dve.tensor_tensor(self.WS[:], self.WS[:], causal, ALU.mult), "g.ws")
        sh.dve_project(dve, st, lambda i, q: self.TMP[:, q, :],
                       before=lambda i, q: dve.wait_ge(k.gelu_done, RING * i + q + 1))
        k.act_done.wait(dve, "g.std")
        k.dve_done.done(dve.reciprocal(k.R[:], k.STD[:]), "g.r")
        k.dve_done.wait(dve, "g.r")
        for g in range(self.G):
            v = self.V[:, g, :]
            k.dve_done.done(dve.scalar_tensor_tensor(v, v, k.v1("v_norm", g), k.R[:], ALU.mult, ALU.mult), f"g.vn{g}")
        for b in range(8):
            k.pe_done.wait(dve, f"g.sv{b}")
            ps = k.bank[4 + b % 4][:].rearrange("p (g c t) -> p g c t", g=2, c=2)
            bs = self.BS[:, 2 * b:2 * b + 2, :].unsqueeze(2).broadcast_to([P, 2, 2, P])
            tmp = self.T2[:, b % 2, :, :].rearrange("p g (c t) -> p g c t", c=2)
            if b >= 2:
                k.dve_done.wait(dve, f"g.usv{b - 2}")
            k.dve_done.done(dve.tensor_tensor(tmp, ps, bs, ALU.add), f"g.sv{b}")
            u = self.U[:, 2 * b:2 * b + 2, :]
            k.dve_done.wait(dve, f"g.sv{b}")
            k.dve_done.done(dve.tensor_tensor(u, u, self.T2[:, b % 2, :, :], ALU.mult), f"g.usv{b}")
            k.act_done.wait(dve, f"g.gh{b}")
            k.dve_done.wait(dve, f"g.usv{b}")
            k.dve_done.done(dve.tensor_tensor(self.low(2 * b, 2), u,
                                              self.Gh[:, 2 * b:2 * b + 2, :].bitcast(F32), ALU.subtract), f"g.gl{b}")
        sh.dve_resid(dve, self.so, 1.0, self.next_gain)

    def pool(self, pool):
        self.sh.pool_stage(pool, self.uv)
        self.sh.pool_stage(pool, self.so)


class FinalNorm:

    def __init__(self, sh, name, nxt):
        self.sh, self.k, self.next_gain = sh, sh.k, nxt

    def pe(self, pe):
        self.sh.norm(pe, "pe")

    def act(self, act):
        k = self.k
        self.sh.norm(act, "act")
        self.sh.prep_all(act, "act", k.X, self.next_gain, wait=lambda c: act.wait_ge(k.x_scaled, c + 1))

    def dve(self, dve):
        k = self.k
        self.sh.norm(dve, "dve")
        dve.wait_ge(k.rstd_ready, self.sh.norm_n["dve"])
        for c in range(NC):
            dve.scalar_tensor_tensor(k.X[:, c, :], k.X[:, c, :], k.v1("final_norm", c), k.R[:],
                                     ALU.mult, ALU.mult).then_inc(k.x_scaled, 1)
        dve.wait_ge(k.x_scaled, NC)
        self.sh.prep_all(dve, "dve", k.X, self.next_gain)

    def pool(self, pool):
        pass


class Hgrn2:
    H = 8

    def __init__(self, sh, name, nxt):
        self.sh, self.k, self.next_gain = sh, sh.k, nxt
        k, a = sh.k, sh.k.A0

        def big(n, offset, dt=F32):
            return k.at("h" + n, offset, [P, NC, T], dt)
        self.Q, self.CUM, self.K, self.V, self.G = (big(n, a + 8 * KB * j) for j, n in enumerate(("Q", "CUM", "K", "V", "G")))
        self.VT = k.at("hVT", a + 40 * KB, [P, 2, D])
        self.Y = big("Y", a + 48 * KB)
        self.LV = [big("LV0", a + 56 * KB), big("LV1", a + 64 * KB), big("LV2", 16 * KB)]
        self.S = k.at("hS", 24 * KB, [P, 2 * self.H, P])
        self.SX = k.at("hSX", 32 * KB, [P, self.H, P])
        self.S8 = k.at("hS8", 37 * KB, [self.H, T])
        self.C = k.at("hC", 36 * KB, [P, 8, NC])
        self.Oh, self.Ol = big("Oh", a + 8 * KB, F32R), big("Ol", a + 16 * KB, F32R)
        self.LEVELS = [6, 5, 4, 3, 2, 1, 0]

    def pe(self, pe):
        sh, k, H = self.sh, self.k, self.H
        sh.pe_first_stage(pe, sh.stage["hgrn_q"])
        for x in "fig":
            sh.pe_stage_h(pe, sh.stage[f"hgrn_{x}"])
        for b in range(4):
            pe.wait_ge(k.banks_freed, RING + sh.stage["hgrn_g"].base)
            if b == 0:
                pe.wait_ge(k.rstd_ready, sh.norm_n["pe"])
            for j in range(4):
                c, half = 2 * b + j // 2, j % 2
                ins = pe.transpose(k.bank[4 + b][:, j * P:(j + 1) * P], self.V[:, c, half * P:(half + 1) * P], k.ident)
            k.pe_done.done(ins, f"h.vt{b}")

        n = 0

        def gram(label, left, right, count):
            nonlocal n
            for b in range(count // 4):
                bank = 4 * (n % 2) + b
                if n >= 2:
                    k.dve_done.wait(pe, f"h.take{n - 2}.{b}")
                elif n == 1:
                    k.act_done.wait(pe, f"h.vt{b}")
                else:
                    pe.wait_ge(k.banks_freed, RING + sh.stage["hgrn_g"].base + NC)
                for j in range(4):
                    ins = pe.matmul(k.bank[bank][:, j * P:(j + 1) * P], left(4 * b + j), right(4 * b + j),
                                    start=True, stop=True)
                k.pe_done.done(ins, f"h.gram{n}.{b}")
            n += 1

        for lv in self.LEVELS:
            a = self.LV[n % 3]
            k.dve_done.wait(pe, f"h.lv{n}")
            half = lambda u: a[:, u // 2, (u % 2) * P:(u % 2 + 1) * P]
            gram(n, half, half, 2 * H)
        gram(n, lambda u: self.K[:, u // 2, (u % 2) * P:(u % 2 + 1) * P],
             lambda u: self.Q[:, u // 2, (u % 2) * P:(u % 2 + 1) * P], 2 * H)
        k.dve_done.wait(pe, f"h.lv{n}")
        a = self.LV[n % 3]
        gram(n, lambda u: a[:, u, :P], lambda u: a[:, u, P:], H)
        last = n - 1
        for b in range(4):
            bank = k.bank[4 + b]
            if b == 0:
                for j in range(4):
                    k.dve_done.wait(pe, f"h.take{last - 1}.{j}")
                for j in range(2):
                    k.dve_done.wait(pe, f"h.take{last}.{j}")
                for j in range(4):
                    k.act_done.wait(pe, f"h.vt{j}")
            for j in range(2):
                h = 2 * b + j
                v0, v1 = self.VT[:, 0, h * P:(h + 1) * P], self.VT[:, 1, h * P:(h + 1) * P]
                o0, o1 = bank[:, j * T:j * T + P], bank[:, j * T + P:(j + 1) * T]
                pe.matmul(o0, v0, self.S[:, 2 * h, :], start=True, stop=True)
                pe.matmul(o1, v0, self.SX[:, h, :], start=True, stop=False)
                ins = pe.matmul(o1, v1, self.S[:, 2 * h + 1, :], start=False, stop=True)
            k.pe_done.done(ins, f"h.o{b}")
        for h in range(H):
            k.act_done.wait(pe, f"h.osq{h // 2}")
            one = k.cols[:, ONE_HOT + 7 - h:ONE_HOT + 15 - h]
            ins = pe.matmul(k.bank[0][:H, :T], one, self.LV[0][:, h, :], start=h == 0, stop=h == H - 1)
        k.pe_done.done(ins, "h.oss")
        k.dve_done.wait(pe, "h.or")
        for b in range(4):
            for j in range(2):
                h = 2 * b + j
                ins = pe.matmul(k.bank[b][:, j * T:(j + 1) * T], k.masks[:H, 0, h:h + 1].broadcast_to([H, P]), self.S8[:],
                                start=True, stop=True)
            k.pe_done.done(ins, f"h.back{b}")
        sh.pe_stage(pe, sh.stage["hgrn_o"], lambda kg, kc: (self.Oh[:, kc, :], self.Ol[:, kc, :]),
                    lambda kg, kc: k.dve_done.wait(pe, f"h.ol{kc // 2}"))

    def act(self, act):
        sh, k, H = self.sh, self.k, self.H
        d = lambda ins, label: k.act_done.done(ins, label)
        sh.norm(act, "act")
        C = self.C
        k.dve_done.wait(act, "h.lbd")
        d(act.activation(C[:, 2:4, :], C[:, 0:2, :], ACT.Exp), "h.lbe")
        def project(x, dst=None):
            st = sh.stage[f"hgrn_{x}"]

            def silu(i, q):
                act.wait_ge(k.banks_freed, RING + st.base + RING * i + q + 1)
                a = dst[:, bass.ds(RING * i + q, 1), :].rearrange("p a t -> p (a t)")
                act.activation(a, a, ACT.Silu).then_inc(k.proj_act, 1)
            sh.act_stage(act, st, silu if dst else None)

        def decays(n):
            b = 1 << self.LEVELS[n]
            v = self.LV[n % 3][:].rearrange("p c (n b) -> p (c n) b", b=2 * b)
            k.dve_done.wait(act, f"h.d{n}")
            d(act.activation(v[:, :, b:], v[:, :, b:], ACT.Exp), f"h.er{n}")
            d(act.activation(v[:, :, :b], v[:, :, :b], ACT.Exp, scale=-1.0), f"h.el{n}")
        project("q", self.Q)
        project("f")
        act.wait_ge(k.banks_freed, RING + sh.stage["hgrn_f"].base + NC)
        d(act.activation(self.LV[1][:], self.CUM[:], ACT.Sigmoid), "h.sig")
        d(act.activation(self.K[:], self.CUM[:], ACT.Sigmoid, scale=-1.0), "h.nsig")
        project("i")
        k.dve_done.wait(act, "h.f7")
        d(act.activation(self.LV[1][:], self.LV[1][:], ACT.Ln), "h.lnf")
        decays(0)
        project("g", self.G)
        for b in range(4):
            k.pe_done.wait(act, f"h.vt{b}")
            dst = self.VT[:, :, 2 * b * P:(2 * b + 2) * P].rearrange("p h (c j) -> p c h j", c=2)
            d(act.activation(dst, k.bank[4 + b][:].rearrange("p (c h j) -> p c h j", c=2, h=2), ACT.Copy), f"h.vt{b}")
        for n in range(1, len(self.LEVELS)):
            decays(n)
        n = len(self.LEVELS) + 1
        a = self.LV[n % 3]
        k.dve_done.wait(act, f"h.d{n}")
        d(act.activation(a[:, :, P:], self.CUM[:, :, P:], ACT.Exp), f"h.er{n}")
        d(act.activation(a[:, :, :P], a[:, :, :P], ACT.Exp, scale=-1.0), f"h.el{n}")
        for b in range(4):
            k.pe_done.wait(act, f"h.o{b}")
            sl = slice(2 * b, 2 * b + 2)
            ps = k.bank[4 + b][:].rearrange("p (h t) -> p h t", h=2)
            d(act.activation(self.Y[:, sl, :], ps, ACT.Copy), f"h.y{b}")
            d(act.activation(self.LV[0][:, sl, :], ps, ACT.Square), f"h.osq{b}")
        k.pe_done.wait(act, "h.oss")
        d(act.activation(self.S8[:], k.bank[0][:H, :T], ACT.Sqrt, bias=k.cols[:H, C_EPS:C_EPS + 1], scale=1.0 / P), "h.ostd")
        for b in range(4):
            k.dve_done.wait(act, f"h.o32{b}")
            sl = slice(2 * b, 2 * b + 2)
            d(act.activation(self.Oh[:, sl, :], self.Y[:, sl, :], ACT.Copy), f"h.oh{b}")
        sh.act_resid(act, sh.stage["hgrn_o"], self.next_gain)

    def dve(self, dve):
        sh, k, H, C = self.sh, self.k, self.H, self.C

        def d(ins, label):
            k.dve_done.done(ins, label)
            k.dve_done.wait(dve, label)
        sh.norm(dve, "dve")
        l0, l1 = (k.vec[:, COL[n]:COL[n] + NC] for n in ("lb0", "lb1"))
        d(dve.tensor_tensor(C[:, 4, :], l0, l1, ALU.max), "h.lbm")
        d(dve.tensor_tensor(C[:, 0, :], l0, C[:, 4, :], ALU.subtract), "h.lb0")
        d(dve.tensor_tensor(C[:, 1, :], l1, C[:, 4, :], ALU.subtract), "h.lbd")
        k.act_done.wait(dve, "h.lbe")
        d(dve.tensor_tensor(C[:, 4, :], C[:, 2, :], C[:, 3, :], ALU.add), "h.lbs")
        d(dve.reciprocal(C[:, 5, :], C[:, 4, :]), "h.lbr")
        d(dve.tensor_tensor(C[:, 6, :], C[:, 2, :], C[:, 5, :], ALU.mult), "h.lbu")
        d(dve.tensor_scalar(C[:, 6, :], C[:, 6, :], 1.2e-38, None, ALU.max), "h.lb")
        d(dve.tensor_tensor(C[:, 7, :], C[:, 3, :], C[:, 5, :], ALU.mult), "h.olb")
        def project(x, dst):
            sh.dve_project(dve, sh.stage[f"hgrn_{x}"],
                           lambda i, q: dst[:, bass.ds(RING * i + q, 1), :].rearrange("p a t -> p (a t)"))

        def view(t, b):
            return t[:].rearrange("p c (n b) -> p (c n) b", b=2 * b)

        def subtract(n, lv):
            b = 1 << lv
            a, cum = view(self.LV[n % 3], b), view(self.CUM, b)
            if n >= 3:
                k.pe_done.wait(dve, f"h.gram{n - 3}.3")
            ref = cum[:, :, b - 1:b].broadcast_to([P, cum.shape[1], 2 * b])
            k.dve_done.done(dve.tensor_tensor(a, cum, ref, ALU.subtract), f"h.d{n}")

        def multiply(n, lv):
            b = 1 << lv
            a, q, kk = view(self.LV[n % 3], b), view(self.Q, b), view(self.K, b)
            k.act_done.wait(dve, f"h.er{n}")
            k.dve_done.done(dve.tensor_tensor(a[:, :, b:], a[:, :, b:], q[:, :, b:], ALU.mult), f"h.lvr{n}")
            k.act_done.wait(dve, f"h.el{n}")
            k.dve_done.done(dve.tensor_tensor(a[:, :, :b], a[:, :, :b], kk[:, :, :b], ALU.mult), f"h.lv{n}")

        def take(n, name):
            for b in range(4):
                k.pe_done.wait(dve, f"h.gram{n}.{b}")
                ps = k.bank[4 * (n % 2) + b][:].rearrange("p (u t) -> p u t", u=4)
                out, m = self.S[:, 4 * b:4 * b + 4, :], bcast(k.mask(name), 4)
                if n == 0:
                    ins = dve.tensor_tensor(out, ps, m, ALU.mult)
                else:
                    k.dve_done.wait(dve, f"h.take{n - 1}.{b}")
                    ins = dve.copy_predicated(out, m.bitcast(I32), ps)
                k.dve_done.done(ins, f"h.take{n}.{b}")

        L = self.LEVELS
        project("q", self.Q)
        project("f", self.CUM)
        k.act_done.wait(dve, "h.sig")
        for h in range(H):
            s = self.LV[1][:, h, :]
            k.dve_done.done(dve.tensor_scalar(s, s, C[:, 7, h:h + 1], C[:, 6, h:h + 1], ALU.mult, ALU.add), f"h.f{h}")
        k.act_done.wait(dve, "h.nsig")
        for h in range(H):
            s = self.K[:, h, :]
            k.dve_done.done(dve.tensor_scalar(s, s, C[:, 7, h:h + 1], None, ALU.mult), f"h.k{h}")
        project("i", self.V)
        k.act_done.wait(dve, "h.lnf")
        for h in range(H):
            for half in range(2):
                sl = slice(half * P, (half + 1) * P)
                k.dve_done.done(dve.tensor_tensor_scan(self.CUM[:, h, sl], k.ones, self.LV[1][:, h, sl], 0.0,
                                                       ALU.mult, ALU.add), f"h.cum{h}.{half}")
        k.dve_done.wait(dve, f"h.cum{H - 1}.1")
        subtract(0, L[0])
        project("g", self.G)
        dve.wait_ge(k.proj_act, NC)
        for n, lv in enumerate(L):
            if n + 1 < len(L):
                subtract(n + 1, L[n + 1])
            multiply(n, lv)
            if n:
                take(n - 1, f"pair{L[n - 1]}")
        n = len(L)
        a = self.LV[(n + 1) % 3]
        k.pe_done.wait(dve, f"h.gram{n - 2}.3")
        ref = self.CUM[:, :, P - 1:P].broadcast_to([P, NC, P])
        k.dve_done.done(dve.tensor_tensor(a[:, :, :P], self.CUM[:, :, :P], ref, ALU.subtract), f"h.d{n + 1}")
        take(n - 1, f"pair{L[-1]}")
        take(n, "identity")
        k.act_done.wait(dve, f"h.el{n + 1}")
        k.dve_done.done(dve.tensor_tensor(a[:, :, P:], a[:, :, P:], self.Q[:, :, P:], ALU.mult), f"h.lvr{n + 1}")
        k.dve_done.done(dve.tensor_tensor(a[:, :, :P], a[:, :, :P], self.K[:, :, :P], ALU.mult), f"h.lv{n + 1}")
        for b in range(2):
            k.pe_done.wait(dve, f"h.gram{n + 1}.{b}")
            ps = k.bank[4 * ((n + 1) % 2) + b][:].rearrange("p (u t) -> p u t", u=4)
            k.dve_done.done(dve.tensor_copy(self.SX[:, 4 * b:4 * b + 4, :], ps), f"h.take{n + 1}.{b}")
        dve.wait_ge(k.proj_act, 2 * NC)
        for b in range(4):
            k.act_done.wait(dve, f"h.y{b}")
            sl = slice(2 * b, 2 * b + 2)
            d(dve.scalar_tensor_tensor(self.Y[:, sl, :], self.Y[:, sl, :], k.v1("a_out_gain", 0), self.G[:, sl, :],
                                       ALU.mult, ALU.mult), f"h.yg{b}")
        k.act_done.wait(dve, "h.ostd")
        k.dve_done.done(dve.reciprocal(self.S8[:], self.S8[:]), "h.or")
        for b in range(5):
            if b < 4:
                k.pe_done.wait(dve, f"h.back{b}")
                sl = slice(2 * b, 2 * b + 2)
                k.dve_done.done(dve.tensor_tensor(self.Y[:, sl, :], self.Y[:, sl, :], k.bank[b][:].rearrange("p (h t) -> p h t", h=2),
                                                  ALU.mult), f"h.o32{b}")
            if b:
                k.act_done.wait(dve, f"h.oh{b - 1}")
                sl = slice(2 * b - 2, 2 * b)
                k.dve_done.done(dve.tensor_tensor(self.Ol[:, sl, :], self.Y[:, sl, :], self.Oh[:, sl, :].bitcast(F32), ALU.subtract),
                                f"h.ol{b - 1}")
        sh.dve_resid(dve, sh.stage["hgrn_o"], 1.0, self.next_gain)

    def pool(self, pool):
        for x in "qfigo":
            self.sh.pool_stage(pool, self.sh.stage[f"hgrn_{x}"])


class HeadNorm:

    def __init__(self, k, name, X, gain, SQ, TOH, S16):
        self.k, self.p, self.X, self.gain, self.SQ, self.TOH, self.S16 = k, name, X, gain, SQ, TOH, S16

    def pe_sums(self, pe, g):
        k, p = self.k, self.p
        k.act_done.wait(pe, f"{p}.sq{g}")
        if g:
            k.act_done.wait(pe, f"{p}.root{g - 1}")
        for c in range(NC):
            ins = pe.matmul(k.bank[4][:16, :T], k.sel[:, 16 * c:16 * (c + 1)], self.SQ[:, c, :], start=c == 0, stop=c == NC - 1)
        k.pe_done.done(ins, f"{p}.ss{g}")

    def pe_back(self, pe, g):
        k, p = self.k, self.p
        k.dve_done.wait(pe, f"{p}.r{g}")
        for b, bank in enumerate((5, 6, 7, 5)):
            if b == 3:
                k.dve_done.wait(pe, f"{p}.n{g}.0")
            elif g:
                k.dve_done.wait(pe, f"{p}.n{g - 1}.{3 if b == 0 else b}")
            for j in range(2):
                ins = pe.matmul(k.bank[bank][:, j * T:(j + 1) * T], self.TOH[:, 2 * b + j, :], self.S16[:, g, :], start=True, stop=True)
            k.pe_done.done(ins, f"{p}.back{g}.{b}")

    def act_square(self, act, g, stage):
        k, p = self.k, self.p
        act.wait_ge(k.banks_freed, RING + stage.base + stage.slabs)
        if g:
            k.pe_done.wait(act, f"{p}.ss{g - 1}")
        k.act_done.done(act.activation(self.SQ[:], self.X[:, NC * g:NC * (g + 1), :], ACT.Square), f"{p}.sq{g}")

    def act_root(self, act, g):
        k, p = self.k, self.p
        k.pe_done.wait(act, f"{p}.ss{g}")
        k.act_done.done(act.activation(self.S16[:, g, :], k.bank[4][:16, :T], ACT.Sqrt, bias=k.cols[:16, C_EPS:C_EPS + 1],
                                       scale=1.0 / HEAD), f"{p}.root{g}")

    def dve_reciprocal(self, dve, g):
        k, p = self.k, self.p
        k.act_done.wait(dve, f"{p}.root{g}")
        k.dve_done.done(dve.reciprocal(self.S16[:, g, :], self.S16[:, g, :]), f"{p}.r{g}")

    def dve_scale(self, dve, g):
        k, p = self.k, self.p
        for b, bank in enumerate((5, 6, 7, 5)):
            k.pe_done.wait(dve, f"{p}.back{g}.{b}")
            x = self.X[:, NC * g + 2 * b:NC * g + 2 * b + 2, :]
            k.dve_done.done(dve.scalar_tensor_tensor(x, k.bank[bank][:].rearrange("p (c t) -> p c t", c=2), k.v1(self.gain, g), x,
                                                     ALU.mult, ALU.mult), f"{p}.n{g}.{b}")


class DilatedKeys:

    def __init__(self, sh, name, nxt):
        self.sh, self.k, self.next_gain = sh, sh.k, nxt
        k, a = sh.k, sh.k.A0
        nc = k.nc
        self.K = k.at("dK", a, [P, 3 * NC, T])
        self.V = k.at("dV", a + 24 * KB, [P, 3 * NC, T])
        self.TOH = k.at("dTOH", a + 56 * KB, [16, NC, P])
        self.norm = HeadNorm(k, "kv", self.K, "k_gain", k.at("dSQ", a + 48 * KB, [P, NC, T]), self.TOH,
                             k.at("dS16", a + 60 * KB, [16, GROUPS, T]))
        self.VS = k.at("dVS", a + 64 * KB, [P, 4, 2, 2 * P])
        self.BT = k.at("dBT", 16 * KB, [BUCKETS + GROUPS, REACH])
        self.BL = k.at("dBL", 18 * KB, [BUCKETS + GROUPS, 48])
        self.BR = k.at("dBR", 20 * KB, [48, REACH])
        k.dil_k = nc.dram_tensor("dil_keys", (P, 3 * NC, T), F32).ap()
        k.dil_v = nc.dram_tensor("dil_values", (P, 2, 3 * D), F32).ap()
        k.dil_b = nc.dram_tensor("dil_bias", (48, REACH), F32).ap()
        self.loads = 48 + k.loads_before
        k.loads_before += 48
        self.stores = 16 * (1 + GROUPS)

    def stage(self, x, g):
        return self.sh.stage[f"dil_{x}{g}"]

    def pe(self, pe):
        sh, k, norm = self.sh, self.k, self.norm
        project = lambda x, g: sh.pe_stage_h(pe, self.stage(x, g))
        sh.pe_first_stage(pe, self.stage("k", 0))
        project("k", 1)
        pe.wait_ge(k.rstd_ready, sh.norm_n["pe"])
        pe.wait_ge(k.mixer_loads, self.loads)
        norm.pe_sums(pe, 0)
        k.pe_done.done(pe.matmul(k.bank[7][:48, :REACH], self.BL[:], self.BT[:], start=True, stop=True), "kv.bias")
        project("k", 2)
        norm.pe_sums(pe, 1)
        k.act_done.wait(pe, "kv.bias")
        norm.pe_back(pe, 0)
        project("v", 0)
        norm.pe_sums(pe, 2)
        norm.pe_back(pe, 1)
        project("v", 1)
        norm.pe_back(pe, 2)

        def transposes(b0, b1):
            for b in range(b0, b1):
                if b == 0:
                    k.act_done.wait(pe, "kv.root2")
                    k.dve_done.wait(pe, "kv.n2.3")
                    pe.wait_ge(k.banks_freed, RING + self.stage("v", 1).base + NC)
                if b == 8:
                    pe.wait_ge(k.banks_freed, RING + self.stage("v", 2).base + NC)
                if b >= 4:
                    k.dve_done.wait(pe, f"kv.vt{b - 4}")
                for j in range(4):
                    c, half = 2 * b + j // 2, j % 2
                    ins = pe.transpose(k.bank[4 + b % 4][:, j * P:(j + 1) * P], self.V[:, c, half * P:(half + 1) * P], k.ident)
                k.pe_done.done(ins, f"kv.vt{b}")
        transposes(0, 8)
        project("v", 2)
        transposes(8, 12)

    def act(self, act):
        sh, k, norm = self.sh, self.k, self.norm
        act.dma_start(self.BT[:], k.io["bias_table"]).then_inc(k.mixer_loads, 16)
        act.dma_start(self.BL[:], k.io["bias_rows"]).then_inc(k.mixer_loads, 16)
        act.dma_start(self.TOH[:], k.io["to_heads"]).then_inc(k.mixer_loads, 16)
        sh.norm(act, "act")
        split = lambda x, g: sh.act_stage(act, self.stage(x, g))

        def store_keys(g):
            k.dve_done.wait(act, f"kv.n{g}.3")
            sl = slice(NC * g, NC * (g + 1))
            act.dma_start(k.dil_k[:, sl, :], self.K[:, sl, :]).then_inc(k.mixer_stores, 16)

        def store_values(b0, b1):
            for b in range(b0, b1):
                k.dve_done.wait(act, f"kv.vt{b}")
                act.dma_start(k.dil_v[:, :, 2 * b * P:(2 * b + 2) * P], self.VS[:, b % 4, :, :]).then_inc(k.values_stored[b % 4], 16)
        split("k", 0)
        norm.act_square(act, 0, self.stage("k", 0))
        split("k", 1)
        norm.act_root(act, 0)
        k.pe_done.wait(act, "kv.bias")
        k.act_done.done(act.activation(self.BR[:], k.bank[7][:48, :REACH], ACT.Copy), "kv.bias")
        norm.act_square(act, 1, self.stage("k", 1))
        split("k", 2)
        norm.act_root(act, 1)
        norm.act_square(act, 2, self.stage("k", 2))
        act.dma_start(k.dil_b, self.BR[:]).then_inc(k.mixer_stores, 16)
        split("v", 0)
        norm.act_root(act, 2)
        store_keys(0)
        split("v", 1)
        store_keys(1)
        store_values(0, 8)
        split("v", 2)
        store_keys(2)
        last = self.stage("v", 2)
        sh.prep_all(act, "act", k.X, self.next_gain, square=False,
                    wait=lambda c: act.wait_ge(k.slab_used, last.base + last.slabs))
        store_values(8, 12)
        act.wait_ge(k.mixer_stores, self.stores)
        for q in range(4):
            act.wait_ge(k.values_stored[q], 16 * 3)

    def dve(self, dve):
        sh, k, norm = self.sh, self.k, self.norm
        sh.norm(dve, "dve")

        def project(x, g):
            dst = self.K if x == "k" else self.V
            sh.dve_project(dve, self.stage(x, g),
                           lambda i, q: dst[:, bass.ds(NC * g + RING * i + q, 1), :].rearrange("p a t -> p (a t)"))

        def values(b0, b1):
            for b in range(b0, b1):
                k.pe_done.wait(dve, f"kv.vt{b}")
                if b >= 4:
                    dve.wait_ge(k.values_stored[b % 4], 16 * (b // 4))
                dst = self.VS[:, b % 4, :, :].rearrange("p h (c j) -> p c h j", c=2)
                k.dve_done.done(dve.tensor_copy(dst, k.bank[4 + b % 4][:].rearrange("p (c h j) -> p c h j", c=2, h=2)), f"kv.vt{b}")
        project("k", 0)
        project("k", 1)
        norm.dve_reciprocal(dve, 0)
        project("k", 2)
        norm.dve_scale(dve, 0)
        norm.dve_reciprocal(dve, 1)
        project("v", 0)
        norm.dve_scale(dve, 1)
        norm.dve_reciprocal(dve, 2)
        project("v", 1)
        norm.dve_scale(dve, 2)
        values(0, 8)
        project("v", 2)
        sh.prep_all(dve, "dve", k.X, self.next_gain, square=False)
        values(8, 12)

    def pool(self, pool):
        for x in "kv":
            for g in range(GROUPS):
                self.sh.pool_stage(pool, self.stage(x, g))


class DilatedAttention:

    def __init__(self, sh, name, nxt):
        self.sh, self.k, self.next_gain = sh, sh.k, nxt
        k, a = sh.k, sh.k.A0
        self.sq, self.so = [sh.stage[f"dil_q{g}"] for g in range(GROUPS)], sh.stage["dil_o"]
        self.Q = k.at("aQ", a, [P, GROUPS * NC, T])
        self.TOH = k.at("aTOH", a + 32 * KB, [16, NC, P])
        self.norm = HeadNorm(k, "q", self.Q, "q_gain", k.at("aSQ", a + 24 * KB, [P, NC, T]), self.TOH,
                             k.at("aS16", a + 36 * KB, [16, GROUPS, T]))
        self.Oh = k.at("aOh", a + 24 * KB, [P, NC, T], F32R)
        self.Ol = k.at("aOl", a + 32 * KB, [P, NC, T], F32R)
        self.OS = k.at("aOS", a + 40 * KB, [P, 2, D])
        self.KP = k.at("aKP", a + 48 * KB, [P, 2, GROUPS, T])
        self.VP = k.at("aVP", a + 54 * KB, [P, 2, 2, GROUPS, P])
        self.B0 = k.at("aB0", a + 60 * KB, [P, 2, 2, GROUPS, P])
        self.B1 = k.at("aB1", a + 66 * KB, [P, 2, 2, GROUPS, T])
        self.S = k.at("aS", 0, [P, 2, 9, P])
        self.PT = k.at("aPT", 16 * KB, [P, 2, 9, P])
        self.QP = [k.at(f"aQP{z}", (9, 25)[z] * KB, [P, 2, GROUPS, T]) for z in range(2)]
        self.st = k.at("ast", 31 * KB, [P, 4, 2, 2])
        self.loads = 16 + k.loads_before
        k.loads_before += 16

    def pe(self, pe):
        sh, k, norm = self.sh, self.k, self.norm
        sh.pe_first_stage(pe, self.sq[0])
        sh.pe_stage_h(pe, self.sq[1])
        pe.wait_ge(k.rstd_ready, sh.norm_n["pe"])
        norm.pe_sums(pe, 0)
        sh.pe_stage_h(pe, self.sq[2])
        norm.pe_sums(pe, 1)
        pe.wait_ge(k.mixer_loads, self.loads)
        norm.pe_back(pe, 0)
        norm.pe_sums(pe, 2)
        norm.pe_back(pe, 1)
        norm.pe_back(pe, 2)

        def scores(u):
            c, e = u // 2, u % 2
            pe.wait_ge(k.pair_loaded[c % 2], 80 * (c // 2 + 1))
            k.act_done.wait(pe, f"a.qp{c}")
            if u:
                k.dve_done.wait(pe, f"a.add{u - 1}")
            else:
                pe.wait_ge(k.banks_freed, RING + self.sq[2].base + NC)
            for g in range(GROUPS):
                q0, q1 = self.QP[c % 2][:, e, g, P:], self.QP[c % 2][:, e, g, :P]
                pe.matmul(k.bank[0][:, g * P:(g + 1) * P], q0, self.KP[:, c % 2, g, :P], start=True, stop=True)
                b, o = 1 + g // 2, (g % 2) * T
                ins = pe.matmul(k.bank[b][:, o:o + T], q1, self.KP[:, c % 2, g, :], start=True, stop=True)
            k.pe_done.done(ins, f"a.s{u}")

        def output(u):
            c, e = u // 2, u % 2
            pe.wait_ge(k.values_loaded[c % 2], 32 * (c // 2 + 1))
            k.act_done.wait(pe, f"a.pt{u}")
            if u >= 2:
                k.dve_done.wait(pe, f"a.o{u - 2}")
            f = slice(e * HEAD, (e + 1) * HEAD)
            for half in range(2):
                out = k.bank[6 + u % 2][:, half * HEAD:(half + 1) * HEAD]
                n = GROUPS * (half + 1)
                for j in range(n):
                    g, key_half = (j, 0) if half == 0 else (j // 2, j % 2)
                    ins = pe.matmul(out, self.PT[:, u % 2, 3 * half + j, :], self.VP[:, c % 2, key_half, g, f],
                                    start=j == 0, stop=j == n - 1)
            k.pe_done.done(ins, f"a.o{u}")

        scores(0)
        for u in range(16):
            if u + 1 < 16:
                scores(u + 1)
            k.act_done.wait(pe, f"a.exp{u}")
            if u:
                k.act_done.wait(pe, f"a.pt{u - 1}")
            else:
                k.dve_done.wait(pe, "q.n2.3")
            for j in range(9):
                ins = pe.transpose(k.bank[3 + j // 4][:, (j % 4) * P:(j % 4 + 1) * P], self.S[:, u % 2, j, :], k.ident)
            k.pe_done.done(ins, f"a.t{u}")
            if u:
                output(u - 1)
        output(15)
        for b in range(4):
            k.dve_done.wait(pe, "a.o15")
            k.act_done.wait(pe, "a.pt15")
            for j in range(4):
                c, half = 2 * b + j // 2, j % 2
                ins = pe.transpose(k.bank[b][:, j * P:(j + 1) * P], self.OS[:, half, c * P:(c + 1) * P], k.ident)
            k.pe_done.done(ins, f"a.ot{b}")
        sh.pe_stage(pe, self.so, lambda kg, kc: (self.Oh[:, kc, :], self.Ol[:, kc, :]),
                    lambda kg, kc: k.dve_done.wait(pe, f"a.ol{kc // 2}"))

    def act(self, act):
        sh, k, norm = self.sh, self.k, self.norm
        act.dma_start(self.TOH[:], k.io["to_heads"]).then_inc(k.mixer_loads, 16)
        sh.norm(act, "act")

        def load(c):
            if c >= 2:
                k.pe_done.wait(act, f"a.s{2 * (c - 2) + 1}")
                k.dve_done.wait(act, f"a.add{2 * (c - 2) + 1}")
            q = c % 2
            act.dma_start(self.KP[:, q], k.dil_k.rearrange("p (g c) t -> p g c t", g=GROUPS)[:, :, c, :]).then_inc(k.pair_loaded[q], 16)
            for n, dst, off in ((P, self.B0, P), (T, self.B1, 0)):
                for e in range(2):
                    src = bass.AP(k.dil_b.tensor, (2 * c + e) * REACH + off, [[1, P], [16 * REACH, GROUPS], [1, n]])
                    act.dma_start(dst[:, q, e], src).then_inc(k.pair_loaded[q], 16)

        def load_values(c):
            if c >= 2:
                k.pe_done.wait(act, f"a.o{2 * (c - 2) + 1}")
            q = c % 2
            for half in range(2):
                src = k.dil_v[:, half, :].rearrange("p (g c j) -> p g c j", g=GROUPS, c=NC)[:, :, c, :]
                act.dma_start(self.VP[:, q, half], src).then_inc(k.values_loaded[q], 16)

        def queries(c):
            if c >= 2:
                k.pe_done.wait(act, f"a.s{2 * (c - 2) + 1}")
            src = self.Q[:].rearrange("p (g c) t -> p g c t", g=GROUPS)[:, :, c, ::-1]
            for e, m in enumerate((LOW_SCALED, HIGH_SCALED)):
                k.act_done.done(act.activation(self.QP[c % 2][:, e], src, ACT.Copy, scale=k.col(m)), f"a.qp{c}")

        for c in range(2):
            load(c)
            load_values(c)
        sh.act_stage(act, self.sq[0])
        norm.act_square(act, 0, self.sq[0])
        sh.act_stage(act, self.sq[1])
        norm.act_root(act, 0)
        norm.act_square(act, 1, self.sq[1])
        sh.act_stage(act, self.sq[2])
        norm.act_root(act, 1)
        norm.act_square(act, 2, self.sq[2])
        norm.act_root(act, 2)
        k.dve_done.wait(act, "q.n2.3")
        queries(0)
        queries(1)
        for u in range(16):
            c, e = u // 2, u % 2
            k.dve_done.wait(act, f"a.nmax{u}")
            if u >= 2:
                k.dve_done.wait(act, f"a.rs{u - 2}")
            for half in range(2):
                s = self.S[:, u % 2, 3 * half:3 + 6 * half, :]
                k.act_done.done(act.activation(s, s, ACT.Exp, bias=self.st[:, 1, e, half:half + 1],
                                               accum_out=self.st[:, 2, e, half:half + 1]), f"a.exp{u}")
            if e == 0 and c >= 1 and c + 1 < NC:
                load(c + 1)
                queries(c + 1)
            k.pe_done.wait(act, f"a.t{u}")
            if u >= 2:
                k.pe_done.wait(act, f"a.o{u - 2}")
            for b, n in ((0, 4), (1, 4), (2, 1)):
                k.act_done.done(act.activation(self.PT[:, u % 2, 4 * b:4 * b + n, :],
                                               k.bank[3 + b][:, :n * P].rearrange("p (a t) -> p a t", a=n), ACT.Copy), f"a.pt{u}")
            if e == 1 and c >= 1 and c + 1 < NC:
                load_values(c + 1)
        for b in range(4):
            k.pe_done.wait(act, f"a.ot{b}")
            k.act_done.done(act.activation(self.out(self.Oh, b), self.reversed(b), ACT.Copy), f"a.oh{b}")
        sh.act_resid(act, self.so, self.next_gain)

    def reversed(self, b):
        return self.k.bank[b][:].rearrange("p (a t) -> p a t", a=4)[:, :, ::-1]

    def out(self, t, b):
        return t[:, 2 * b:2 * b + 2, :].rearrange("p c (h t) -> p (c h) t", h=2)

    def dve(self, dve):
        sh, k, norm = self.sh, self.k, self.norm
        sh.norm(dve, "dve")
        d = lambda ins, label: k.dve_done.done(ins, label)

        def project(g):
            sh.dve_project(dve, self.sq[g], lambda i, q: self.Q[:, bass.ds(NC * g + RING * i + q, 1), :].rearrange("p a t -> p (a t)"))

        def add_bias(u):
            c, e = u // 2, u % 2
            dve.wait_ge(k.pair_loaded[c % 2], 80 * (c // 2 + 1))
            k.pe_done.wait(dve, f"a.s{u}")
            if u >= 2:
                k.pe_done.wait(dve, f"a.t{u - 2}")
            s = self.S[:, u % 2]
            bank = lambda b, n: k.bank[b][:, :n * P].rearrange("p (a t) -> p a t", a=n)
            b1 = self.B1[:, c % 2, e].rearrange("p g (h t) -> p (g h) t", h=2)
            d(dve.tensor_tensor(s[:, 0:3, :], bank(0, 3), self.B0[:, c % 2, e], ALU.add), f"a.add0{u}")
            d(dve.tensor_tensor(s[:, 3:7, :], bank(1, 4), b1[:, 0:4, :], ALU.add), f"a.add1{u}")
            d(dve.tensor_tensor(s[:, 7:9, :], bank(2, 2), b1[:, 4:6, :], ALU.add), f"a.add{u}")
            k.dve_done.wait(dve, f"a.add{u}")
            for half in range(2):
                d(dve.tensor_reduce(self.st[:, 0, e, half:half + 1], s[:, 3 * half:3 + 6 * half, :], AX.XY, ALU.max), f"a.max{u}")
            k.dve_done.wait(dve, f"a.max{u}")
            d(dve.tensor_scalar(self.st[:, 1, e, :], self.st[:, 0, e, :], -1.0, None, ALU.mult), f"a.nmax{u}")

        def normalize(u):
            c, e = u // 2, u % 2
            k.act_done.wait(dve, f"a.exp{u}")
            d(dve.reciprocal(self.st[:, 3, e, :], self.st[:, 2, e, :]), f"a.rs{u}")
            k.dve_done.wait(dve, f"a.rs{u}")
            k.pe_done.wait(dve, f"a.o{u}")
            for half in range(2):
                d(dve.tensor_scalar(self.OS[:, half, c * P + e * HEAD:c * P + (e + 1) * HEAD],
                                    k.bank[6 + u % 2][:, half * HEAD:(half + 1) * HEAD],
                                    self.st[:, 3, e, half:half + 1], None, ALU.mult), f"a.o{u}")
        project(0)
        project(1)
        norm.dve_reciprocal(dve, 0)
        project(2)
        norm.dve_scale(dve, 0)
        norm.dve_reciprocal(dve, 1)
        norm.dve_scale(dve, 1)
        norm.dve_reciprocal(dve, 2)
        norm.dve_scale(dve, 2)
        add_bias(0)
        for u in range(16):
            if u + 1 < 16:
                add_bias(u + 1)
            if u:
                normalize(u - 1)
        normalize(15)
        for b in range(4):
            k.act_done.wait(dve, f"a.oh{b}")
            d(dve.tensor_tensor(self.out(self.Ol, b), self.reversed(b), self.out(self.Oh, b).bitcast(F32), ALU.subtract), f"a.ol{b}")
        sh.dve_resid(dve, self.so, 1.0, self.next_gain)

    def pool(self, pool):
        for st in self.sq + [self.so]:
            self.sh.pool_stage(pool, st)


class Rwkv7:
    DECAY = math.exp(-0.5)
    LEVELS = 5

    def __init__(self, sh, name, nxt):
        self.sh, self.k, self.next_gain = sh, sh.k, nxt
        k = sh.k
        self.st = {x: sh.stage[f"rwkv_{x}"] for x in "rkvo"}

        def big(n, kb, dt=F32):
            return k.at("r" + n, kb * KB, [P, NC, T], dt)
        self.H, self.DX = big("H", 0), big("DX", 8)
        self.split = {"r": (big("Sah", 16, F32R), big("Sal", 24, F32R)), "v": (big("Sbh", 32, F32R), big("Sbl", 40, F32R))}
        self.split["k"] = self.split["r"]
        self.XR, self.XW, self.XA = big("XR", 64), big("XW", 80), big("XA", 48)
        self.XG, self.XK, self.XV = big("XG", 104), big("XK", 56), big("XV", 64)
        self.R, self.K, self.V, self.SIG, self.A, self.G = (big(n, kb) for n, kb in
            (("R", 72), ("K", 80), ("V", 48), ("SIG", 88), ("A", 96), ("G", 56)))
        self.W1 = k.at("rW1", 112 * KB, [P, NC, LORA_W])
        self.A1 = k.at("rA1", 114 * KB, [P, NC, LORA_A])
        self.G1 = k.at("rG1", 96 * KB, [P, NC, LORA_G])
        self.LT = k.at("rLT", 116 * KB, [P, 2, T])
        self.LG = k.at("rLG", 112 * KB, [P, 2, T])
        self.W2 = k.at("rW2", 32 * KB, [P, D])
        self.A2 = k.at("rA2", 36 * KB, [P, D])
        self.G2 = k.at("rG2", 40 * KB, [P, 2, D])
        self.KN, self.TA, self.SQ = big("KN", 104), big("TA", 0), big("SQ", 8)
        self.CS, self.PP, self.BV, self.PI = big("CS", 16), big("PP", 24), big("BV", 64), big("PI", 72)
        self.TOH = k.at("rTOH", 112 * KB, [16, NC, P])
        self.S16 = k.at("rS16", 116 * KB, [16, T])
        self.AR = k.at("rAR", 0, [P, NC, 2, 2, P])
        self.BK = k.at("rBK", 16 * KB, [P, NC, 2, 2, T])
        s = 72
        self.LN = [k.at(f"rLN{z}", (s + 18 * z) * KB, [P, 2, 2, 2, P]) for z in range(2)]
        self.MQ = [k.at(f"rMQ{z}", (s + 18 * z + 4) * KB, [P, 2, 2, 2, P]) for z in range(2)]
        self.D = [k.at(f"rD{z}", (s + 18 * z + 8) * KB, [P, 4, P]) for z in range(2)]
        self.DT = [k.at(f"rDT{z}", (s + 18 * z + 10) * KB, [P, 4, P]) for z in range(2)]
        self.AX = [k.at(f"rAX{z}", (s + 18 * z + 12) * KB, [P, 2, 4, HEAD]) for z in range(2)]
        self.VT = [k.at(f"rVT{z}", (s + 18 * z + 14) * KB, [P, 2, P]) for z in range(2)]
        self.BKT = [k.at(f"rBKT{z}", (s + 18 * z + 15) * KB, [P, 3, 2, P]) for z in range(2)]
        self.E = [k.at(f"rE{lv}", (108 + 2 * lv) * KB, [P, 4, P]) for lv in range(self.LEVELS)]
        self.LOWER = k.at("rLOWER", 118 * KB, [P, self.LEVELS, 64])
        self.PT = k.at("rPT", 119 * KB + 256, [P, NC, 4])
        self.YC, self.YSQ = big("YC", 72), big("YSQ", 80)
        self.TOH2 = k.at("rTOH2", 88 * KB, [16, NC, P])
        self.S16b = k.at("rS16b", 92 * KB, [16, T])
        self.Oh, self.Ol = big("Oh", 96, F32R), big("Ol", 104, F32R)
        self.loads = [k.loads_before + 16 * n for n in (8, 9, 10)]
        k.loads_before += 16 * 10

    def pe(self, pe):
        sh, k, st = self.sh, self.k, self.st
        sh.norm(pe, "pe")

        def project(x, between=None):
            hi, lo = self.split[x]
            sh.pe_stage(pe, st[x], lambda kg, kc: (hi[:, kc, :], lo[:, kc, :]),
                        lambda kg, kc: k.dve_done.wait(pe, f"r.rlo{kc}" if x == "r" else f"r.{x}lo"), between)
        project("r")
        pe.wait_ge(k.mixer_loads, self.loads[0])
        pe.wait_ge(k.rstd_ready, sh.norm_n["pe"])
        for x, w, bank, cols, src in (("w", self.W1, 5, slice(0, 64), self.XW), ("a", self.A1, 6, slice(0, 64), self.XA),
                                      ("g", self.G1, 7, slice(0, 128), self.XG), ("h", self.G1, 4, slice(128, 160), self.XG)):
            if x != "h":
                k.dve_done.wait(pe, f"r.x{x}1")
            n = cols.stop - cols.start
            for c in range(NC):
                ins = pe.matmul(k.bank[bank][:n, :T], w[:, c, cols], src[:, c, :], start=c == 0, stop=c == NC - 1)
            k.pe_done.done(ins, f"r.l1{x}")
        for n in range(12):
            kind, pair = "wag"[n // 4], n % 4
            k.act_done.wait(pe, "r.t" + kind)
            k.act_done.wait(pe, f"r.l2{n - 4}" if n >= 4 else "r.tg")
            for j in range(2):
                c = 2 * pair + j
                out, f = k.bank[4 + n % 4][:, j * T:(j + 1) * T], slice(c * P, (c + 1) * P)
                if kind == "g":
                    pe.matmul(out, self.G2[:, 0, f], self.LG[:, 0, :], start=True, stop=False)
                    ins = pe.matmul(out, self.G2[:32, 1, f], self.LG[:32, 1, :], start=False, stop=True)
                else:
                    w, t = (self.W2, 0) if kind == "w" else (self.A2, 1)
                    ins = pe.matmul(out, w[:64, f], self.LT[:64, t, :], start=True, stop=True)
            k.pe_done.done(ins, f"r.l2{n}")
        def key_norms():
            k.act_done.wait(pe, "r.sq")
            k.act_done.wait(pe, "r.l28")
            for c in range(NC):
                ins = pe.matmul(k.bank[4][:16, :T], k.sel[:, 16 * c:16 * (c + 1)], self.SQ[:, c, :], start=c == 0, stop=c == NC - 1)
            k.pe_done.done(ins, "r.ss")
        project("k")
        project("v", key_norms)

        k.dve_done.wait(pe, "r.bp")
        pe.wait_ge(k.banks_freed, RING + st["v"].base + NC)
        k.dve_done.wait(pe, "r.rn")
        pe.wait_ge(k.mixer_loads, self.loads[1])
        for b in range(4):
            if b:
                k.act_done.wait(pe, f"r.l2{8 + b}")
            for j in range(2):
                ins = pe.matmul(k.bank[4 + b][:, j * T:(j + 1) * T], self.TOH[:, 2 * b + j, :], self.S16[:], start=True, stop=True)
            k.pe_done.done(ins, f"r.rb{b}")
        for b in range(4):
            for j in range(2):
                ins = pe.matmul(k.bank[b][:, j * T:(j + 1) * T], k.head_ones, self.BV[:, 2 * b + j, :], start=True, stop=True)
            k.pe_done.done(ins, f"r.bs{b}")

        for c in range(-1, NC + 1):
            after = self.pe_after(pe, c - 1) if c >= 1 else {}
            before = self.pe_before(pe, c + 1) if c + 1 < NC else {}
            if c == -1:
                for step in ("l", "g1", "t", "g2"):
                    before[step]()
                continue
            inv = self.pe_invert(pe, c) if c < NC else {}
            for step in ("e1", "x1", "c1", "w", "e2", "gt", "u", "c2", "ht", "e3", "y", "c3", "l", "e4", "g1", "c4",
                         "t", "e5", "g2", "c5"):
                for part in (inv, after, before):
                    if step in part:
                        part[step]()

        for j in (1, 2):
            for c in range(NC):
                k.dve_done.wait(pe, f"r.u{c}" if j == 1 else f"r.z1{c}")
                if j == 1:
                    k.pool_done.wait(pe, f"r.gti{c}")
                    k.act_done.wait(pe, "r.y7")
                    k.dve_done.wait(pe, "r.ht7")
                k.pe_done.done(pe.matmul(k.bank[c][:, :P], self.gti(c, j), self.z(c, j - 1), start=True, stop=True), f"r.z{j}{c}")
        for c in range(NC):
            k.dve_done.wait(pe, f"r.z2{c}")
            k.dve_done.wait(pe, f"r.ht{c}")
            for j in (1, 2, 3):
                ins = pe.matmul(k.bank[c][:, T + (j - 1) * 64:T + j * 64], self.z(c, j - 1),
                                self.AR[:, c, j // 2, 1, (j % 2) * 64:(j % 2 + 1) * 64], start=True, stop=True)
            k.pe_done.done(ins, f"r.ys{c}")

        for b in range(4):
            k.dve_done.wait(pe, "r.y7" if b else "r.y4")
            for j in range(2):
                ins = pe.matmul(k.bank[4 + b][:, j * T:(j + 1) * T], k.head_ones, self.AR[:, 2 * b + j, :, 0, :], start=True, stop=True)
            k.pe_done.done(ins, f"r.mean{b}")
        k.dve_done.wait(pe, "r.yc3")
        for c in range(NC):
            if c % 2 == 0:
                k.act_done.wait(pe, f"r.ysq{c // 2}")
            ins = pe.matmul(k.bank[4][:16, :T], k.sel[:, 16 * c:16 * (c + 1)], self.YSQ[:, c, :], start=c == 0, stop=c == NC - 1)
        k.pe_done.done(ins, "r.yss")
        k.dve_done.wait(pe, "r.yr")
        pe.wait_ge(k.mixer_loads, self.loads[2])
        for b in range(4):
            for j in range(2):
                ins = pe.matmul(k.bank[4 + b][:, j * T:(j + 1) * T], self.TOH2[:, 2 * b + j, :], self.S16b[:], start=True, stop=True)
            k.pe_done.done(ins, f"r.yb{b}")
        if sh.memory:
            k.dve_done.wait(pe, "r.yn0")
            sh.memory.pe_project(pe)
            k.dve_done.wait(pe, "r.yn3")
            pe.wait_ge(k.rstd_ready, sh.norm_n["pe"])
            sh.memory.pe_values(pe)
        sh.pe_stage(pe, st["o"], lambda kg, kc: (self.Oh[:, kc, :], self.Ol[:, kc, :]),
                    lambda kg, kc: k.dve_done.wait(pe, f"r.ol{kc // 2}"))

    def gti(self, c, j):
        return self.BK[:, c, 0, 0, (j - 1) * P:j * P]

    def z(self, c, j):
        return self.BK[:, c, 1, j // 2, (j % 2) * P:(j % 2 + 1) * P]

    def pe_before(self, pe, c):
        k, z, AR, BK = self.k, c % 2, self.AR, self.BK

        def freed(steps, label, first_steps, first_label):
            if c >= 2:
                steps.wait(pe, f"{label}{c - 2}")
            elif c == 1:
                first_steps.wait(pe, f"{first_label}0")

        def l():
            if c == 0:
                k.act_done.wait(pe, "r.bk1")
                k.dve_done.wait(pe, "r.bk1")
            freed(k.act_done, "r.x1", k.act_done, "r.g2b")
            for u in range(4):
                hf, e = u // 2, u % 2
                ins = pe.matmul(k.bank[2][:, u * P:(u + 1) * P], AR[:, c, hf, 0, :], BK[:, c, 0, e, hf * P:(hf + 1) * P],
                                start=True, stop=True)
            k.pe_done.done(ins, f"r.l{c}")

        def gram(kind, hf, bank, label):
            for e in range(2):
                ins = pe.matmul(k.bank[bank][:, e * T:(e + 1) * T], BK[:, c, kind, e, hf * P:(hf + 1) * P],
                                AR[:, c, hf, :, :].rearrange("p k t -> p (k t)"), start=True, stop=True)
            k.pe_done.done(ins, label)

        def g1():
            freed(k.act_done, "r.w", k.act_done, "r.g1a")
            gram(0, 0, 3, f"r.g1a{c}")
            freed(k.dve_done, "r.gt", k.act_done, "r.g1b")
            gram(0, 1, 4, f"r.g1b{c}")

        def t():
            freed(k.dve_done, "r.u", k.act_done, "r.t1")
            for hf in range(2):
                pe.transpose(k.bank[5][:, hf * P:(hf + 1) * P], AR[:, c, hf, 0, :], k.ident)
                ins = pe.transpose(k.bank[5][:, (2 + hf) * P:(3 + hf) * P], self.V[:, c, hf * P:(hf + 1) * P], k.ident)
            k.pe_done.done(ins, f"r.t1{c}")
            freed(k.dve_done, "r.ht", k.act_done, "r.t2")
            for kind in range(2):
                for hf in range(2):
                    for e in range(2):
                        o = (2 * kind + hf) * P + e * HEAD
                        ins = pe.matmul(k.bank[6][:, o:o + HEAD], BK[:, c, kind, e, hf * P:(hf + 1) * P],
                                        k.ident[:, e * HEAD:(e + 1) * HEAD], start=True, stop=True)
            k.pe_done.done(ins, f"r.t2{c}")

        def g2():
            freed(k.act_done, "r.y", k.act_done, "r.g2a")
            gram(1, 0, 7, f"r.g2a{c}")
            k.dve_done.wait(pe, f"r.l{c}")
            gram(1, 1, 2, f"r.g2b{c}")
        return {"l": l, "g1": g1, "t": t, "g2": g2}

    def cols(self, t, u, b, side):
        return t[:, u, :].rearrange("p (n b) -> p n b", b=2 * b)[:, :, side * b:(side + 1) * b]

    def level_banks(self, c, lv):
        n = (self.LEVELS * c + lv) % 2
        return n, 1 - n

    def pe_invert(self, pe, c):
        k, z = self.k, c % 2
        D, DT, LN = self.D[z], self.DT[z], self.LN[z]
        steps = {}
        for lv in range(1, self.LEVELS + 1):
            a, b = self.level_banks(c, lv)

            def e(lv=lv, a=a):
                if lv == 1:
                    k.pool_done.wait(pe, f"r.dt{c}")
                    if c:
                        k.dve_done.wait(pe, f"r.cd5{c - 1}")
                else:
                    k.dve_done.wait(pe, f"r.cd{lv - 1}{c}")
                for u in range(4):
                    ins = pe.matmul(k.bank[a][:, u * 64:(u + 1) * 64], LN[:, u // 2, u % 2, 0, :],
                                    self.cols(D, u, 1 << lv, 0), start=True, stop=True)
                k.pe_done.done(ins, f"r.e{lv}{c}")

            def cc(lv=lv, a=a, b=b):
                k.dve_done.wait(pe, f"r.e{lv}{c}")
                if lv > 1:
                    k.dve_done.wait(pe, f"r.ct{lv - 1}{c}")
                elif c:
                    k.dve_done.wait(pe, f"r.ct5{c - 1}")
                E = self.E[lv - 1]
                for u in range(4):
                    ins = pe.matmul(k.bank[b][:, u * 64:(u + 1) * 64], DT[:, u, :], self.cols(E, u, 1 << lv, 0), start=True, stop=True)
                k.pe_done.done(ins, f"r.c{lv}{c}")
                for u in range(4):
                    ins = pe.matmul(k.bank[a][:, u * 64:(u + 1) * 64], E[:, u, :], self.cols(DT, u, 1 << lv, 1),
                                    start=True, stop=True)
                k.pe_done.done(ins, f"r.k{lv}{c}")
            steps[f"e{lv}"], steps[f"c{lv}"] = e, cc
        return steps

    def pe_after(self, pe, c):
        k, z = self.k, c % 2
        AX, VT, BKT, LN, MQ = self.AX[z], self.VT[z], self.BKT[z], self.LN[z], self.MQ[z]
        nxt = c + 1 < NC
        half_of = {0: (0, 0), 1: (0, 2), 2: (1, 1)}

        def x1():
            if nxt:
                k.act_done.wait(pe, f"r.g2b{c + 1}")
            else:
                k.act_done.wait(pe, f"r.x1{c - 1}")
            k.pool_done.wait(pe, f"r.mq{c}")
            k.act_done.wait(pe, f"r.t1{c}")
            for u in range(4):
                hf, e = u // 2, u % 2
                ins = pe.matmul(k.bank[2][:, u * 64:(u + 1) * 64], MQ[:, hf, e, 0, :], VT[:, hf, e * 64:(e + 1) * 64],
                                start=True, stop=True)
            k.pe_done.done(ins, f"r.x1{c}")

        def w():
            k.act_done.wait(pe, f"r.g1a{c + 1}" if nxt else f"r.w{c - 1}")
            k.act_done.wait(pe, f"r.x1{c}")
            k.dve_done.wait(pe, f"r.ct5{c}")
            for u in range(4):
                hf, e = u // 2, u % 2
                ins = pe.matmul(k.bank[3][:, u * P:(u + 1) * P], self.DT[z][:, u, :],
                                AX[:, :, u, :], start=True, stop=True)
            k.pe_done.done(ins, f"r.w{c}")

        def gt():
            if nxt:
                k.act_done.wait(pe, f"r.g1b{c + 1}")
            else:
                k.dve_done.wait(pe, f"r.gt{c - 1}")
            k.act_done.wait(pe, f"r.w{c}")
            k.act_done.wait(pe, f"r.t2{c}")
            for j in (1, 2):
                hf, n = half_of[j]
                ins = pe.matmul(k.bank[4][:, (j - 1) * P:j * P], AX[:, 0, 2 * hf:2 * hf + 2, :].rearrange("p e f -> p (e f)"), BKT[:, n, 0, :], start=True, stop=True)
            k.pe_done.done(ins, f"r.gt{c}")

        def u_():
            if nxt:
                k.act_done.wait(pe, f"r.t1{c + 1}")
            else:
                k.dve_done.wait(pe, f"r.u{c - 1}")
            for j in range(3):
                hf, n = half_of[j]
                out = k.bank[5][:, j * P:(j + 1) * P]
                pe.matmul(out, BKT[:, n, 0, :], AX[:, 1, 2 * hf:2 * hf + 2, :], start=True, stop=False)
                ins = pe.matmul(out, BKT[:, n, 1, :], VT[:, hf, :], start=False, stop=True)
            k.pe_done.done(ins, f"r.u{c}")

        def ht():
            if nxt:
                k.act_done.wait(pe, f"r.t2{c + 1}")
            else:
                k.dve_done.wait(pe, f"r.ht{c - 1}")
            for hf in range(2):
                for e in range(2):
                    ins = pe.matmul(k.bank[6][e * 64:(e + 1) * 64, hf * P:(hf + 1) * P], AX[:, 0, 2 * hf + e, :],
                                    LN[:, hf, e, 1, :], start=True, stop=True, skip_group_check=True)
            k.pe_done.done(ins, f"r.ht{c}")

        def y():
            if nxt:
                k.act_done.wait(pe, f"r.g2a{c + 1}")
            else:
                k.act_done.wait(pe, f"r.y{c - 1}")
            for hf in range(2):
                for e in range(2):
                    out = k.bank[7][e * 64:(e + 1) * 64, hf * P:(hf + 1) * P]
                    pe.matmul(out, AX[:, 1, 2 * hf + e, :], LN[:, hf, e, 1, :], start=True, stop=False, skip_group_check=True)
                    ins = pe.matmul(out, VT[:, hf, e * 64:(e + 1) * 64], MQ[:, hf, e, 1, :], start=False, stop=True,
                                    skip_group_check=True)
            k.pe_done.done(ins, f"r.y{c}")
        return {"x1": x1, "w": w, "gt": gt, "u": u_, "ht": ht, "y": y}

    def act(self, act):
        sh, k, st = self.sh, self.k, self.st
        d = lambda ins, label: k.act_done.done(ins, label)
        load = lambda dst, src: act.dma_start(dst, k.io[src]).then_inc(k.mixer_loads, 16)
        load(self.W1[:], "lora_w1")
        load(self.A1[:], "lora_a1")
        load(self.G1[:], "lora_g1")
        load(self.LOWER[:], "lower")
        load(self.W2[:64], "lora_w2")
        load(self.A2[:64], "lora_a2")
        load(self.G2[:, 0, :], "lora_g2a")
        load(self.G2[:32, 1, :], "lora_g2b")
        sh.norm(act, "act")

        def split(x, src):
            for half in range(2):
                sl = slice(4 * half, 4 * half + 4)
                k.dve_done.wait(act, f"r.x{x}{half}")
                d(act.activation(self.split[x][0][:, sl, :], src[:, sl, :], ACT.Copy), f"r.{x}hi{half}")
        for c in range(NC):
            k.dve_done.wait(act, f"r.xr{c}")
            d(act.activation(self.split["r"][0][:, c, :], self.XR[:, c, :], ACT.Copy), f"r.rhi{c}")
        sh.act_stage(act, st["r"])
        k.pe_done.wait(act, "r.l1w")
        d(act.activation(self.LT[:64, 0, :], k.bank[5][:64, :T], ACT.Tanh), "r.tw")
        k.pe_done.wait(act, "r.l1a")
        d(act.activation(self.LT[:64, 1, :], k.bank[6][:64, :T], ACT.Copy), "r.ta")
        k.pe_done.wait(act, "r.l1h")
        d(act.activation(self.LG[:, 0, :], k.bank[7][:, :T], ACT.Sigmoid), "r.tg0")
        d(act.activation(self.LG[:32, 1, :], k.bank[4][:32, :T], ACT.Sigmoid), "r.tg")
        split("k", self.XK)
        for n in range(12):
            kind, pair = "wag"[n // 4], n % 4
            k.pe_done.wait(act, f"r.l2{n}")
            if kind == "g":
                if pair == 0:
                    k.dve_done.wait(act, "r.klo")
                d(act.activation(self.G[:, 2 * pair:2 * pair + 2, :], k.bank[4 + n % 4][:].rearrange("p (c t) -> p c t", c=2),
                                 ACT.Copy), f"r.l2{n}")
            else:
                dst, b = (self.SIG, "w0") if kind == "w" else (self.A, "a0")
                for j in range(2):
                    c = 2 * pair + j
                    d(act.activation(dst[:, c, :], k.bank[4 + n % 4][:, j * T:(j + 1) * T], ACT.Sigmoid, bias=k.v1(b, c)), f"r.l2{n}")
        split("v", self.XV)
        sh.act_stage(act, st["k"])
        for c in range(NC):
            k.dve_done.wait(act, f"r.kk{c}")
            d(act.activation(self.SQ[:, c, :], self.KN[:, c, :], ACT.Square), "r.sq")
        load(self.TOH[:], "to_heads")
        sh.act_stage(act, st["v"])
        k.pe_done.wait(act, "r.ss")
        d(act.activation(self.S16[:], k.bank[4][:16, :T], ACT.Sqrt), "r.n16")
        k.dve_done.wait(act, "r.cs")
        d(act.activation(self.PP[:], self.CS[:], ACT.Exp, scale=-self.DECAY), "r.p")
        k.act_done.wait(act, "r.p")
        d(act.activation(self.PT[:], self.PP[:, :, CHUNK - 1::CHUNK], ACT.Copy), "r.pt")
        k.pool_done.wait(act, "r.dd")
        d(act.activation(self.SIG[:], self.SIG[:], ACT.Exp, scale=-self.DECAY), "r.pprev")
        k.dve_done.wait(act, "r.R")
        d(act.activation(self.PI[:], self.CS[:], ACT.Exp, scale=self.DECAY), "r.pinv")
        for b in range(4):
            k.pe_done.wait(act, f"r.bs{b}")
            d(act.activation(self.BV[:, 2 * b:2 * b + 2, :], k.bank[b][:].rearrange("p (c t) -> p c t", c=2), ACT.Copy), f"r.bs{b}")
        k.dve_done.wait(act, "r.B")
        for e, m in enumerate((LOW, HIGH)):
            d(act.activation(self.BK[:, :, 0, e, :], self.A[:], ACT.Copy, scale=k.col(m)), "r.bk0")
        k.dve_done.wait(act, "r.K")
        d(act.activation(self.BK[:, :, 1, 0, :], self.K[:], ACT.Copy, scale=k.col(LOW)), "r.bk1")
        for c in range(-1, NC + 1):
            if c >= 1:
                self.act_after(act, c - 1)
            if c + 1 < NC:
                self.act_before(act, c + 1)
        k.pe_done.wait(act, "r.ys7")
        if sh.memory:
            act.dma_start(sh.memory.M[:], k.io["mem"]).then_inc(k.mem_loaded, 16)
        load(self.TOH2[:], "to_heads")
        for b in range(4):
            k.dve_done.wait(act, f"r.yc{b}")
            d(act.activation(self.YSQ[:, 2 * b:2 * b + 2, :], self.YC[:, 2 * b:2 * b + 2, :], ACT.Square), f"r.ysq{b}")
        k.pe_done.wait(act, "r.yss")
        d(act.activation(self.S16b[:], k.bank[4][:16, :T], ACT.Sqrt, bias=k.cols[:16, C_GN_EPS:C_GN_EPS + 1], scale=1.0 / HEAD), "r.ystd")
        if sh.memory:
            sh.memory.act_start(act)
        for b in range(4):
            k.dve_done.wait(act, f"r.yn{b}")
            for c in (2 * b, 2 * b + 1):
                d(act.activation(self.YC[:, c, :], self.YC[:, c, :], ACT.Identity, bias=k.v1("ln_b", c), scale=k.v1("ln_w", c)), f"r.yl{b}")
            if b:
                k.pool_done.wait(act, f"r.yg{b - 1}")
                d(act.activation(self.Oh[:, 2 * b - 2:2 * b, :], self.YC[:, 2 * b - 2:2 * b, :], ACT.Copy), f"r.oh{b - 1}")
        k.pool_done.wait(act, "r.yg3")
        d(act.activation(self.Oh[:, 6:8, :], self.YC[:, 6:8, :], ACT.Copy), "r.oh3")
        if sh.memory:
            sh.memory.act_finish(act)
        sh.act_resid(act, st["o"], self.next_gain)

    def act_before(self, act, c):
        k, z = self.k, c % 2
        d = lambda ins, label: k.act_done.done(ins, label)
        for hf in range(2):
            k.pe_done.wait(act, f"r.g1{'ab'[hf]}{c}")
            d(act.activation(self.LN[z][:, hf].rearrange("p e k t -> p (e k t)"), k.bank[3 + hf][:], ACT.Copy), f"r.g1{'ab'[hf]}{c}")
        k.pe_done.wait(act, f"r.t1{c}")
        d(act.activation(self.AX[z][:, 0], k.bank[5][:, :T].rearrange("p (u f) -> p u f", u=4), ACT.Copy), f"r.t1{c}")
        d(act.activation(self.VT[z][:], k.bank[5][:, T:].rearrange("p (h f) -> p h f", h=2), ACT.Copy), f"r.t1{c}")
        k.pe_done.wait(act, f"r.t2{c}")
        src = k.bank[6][:].rearrange("p (k h f) -> p h k f", k=2, h=2)
        d(act.activation(self.BKT[z][:, 0:2, :, :], src, ACT.Copy, scale=k.col(LOW)), f"r.t2{c}")
        d(act.activation(self.BKT[z][:, 2, :, :], src[:, 0, :, :], ACT.Copy, scale=k.col(HIGH)), f"r.t2{c}")
        for hf, bank in ((0, 7), (1, 2)):
            k.pe_done.wait(act, f"r.g2{'ab'[hf]}{c}")
            d(act.activation(self.MQ[z][:, hf].rearrange("p e k t -> p (e k t)"), k.bank[bank][:], ACT.Copy), f"r.g2{'ab'[hf]}{c}")

    def act_after(self, act, c):
        k, z = self.k, c % 2
        d = lambda ins, label: k.act_done.done(ins, label)
        k.pe_done.wait(act, f"r.x1{c}")
        d(act.activation(self.AX[z][:, 1], k.bank[2][:, :T].rearrange("p (u f) -> p u f", u=4), ACT.Copy), f"r.x1{c}")
        k.pe_done.wait(act, f"r.w{c}")
        d(act.activation(self.AX[z][:].rearrange("p k u f -> p u k f"), k.bank[3][:].rearrange("p (u k f) -> p u k f", u=4, k=2), ACT.Copy), f"r.w{c}")
        k.pe_done.wait(act, f"r.y{c}")
        d(act.activation(self.AR[:, c, :, 0, :], k.bank[7][:, :T].rearrange("p (h t) -> p h t", h=2), ACT.Copy), f"r.y{c}")

    def dve(self, dve):
        sh, k, st = self.sh, self.k, self.st

        def d(ins, label):
            k.dve_done.done(ins, label)

        def dw(ins, label):
            k.dve_done.done(ins, label)
            k.dve_done.wait(dve, label)
        sh.norm(dve, "dve")
        dve.wait_ge(k.rstd_ready, sh.norm_n["dve"])
        def mixed(x, j, dst):
            for c in range(NC):
                d(dve.scalar_tensor_tensor(dst[:, c, :], self.DX[:, c, :], k.v1(f"mu{j}", c), self.H[:, c, :], ALU.mult, ALU.add),
                  f"r.x{x}{c // 4}")

        def hidden(c):
            d(dve.scalar_tensor_tensor(self.H[:, c, :], k.X[:, c, :], k.v1("mix_norm0", c), k.R[:], ALU.mult, ALU.mult), f"r.h{c}")

        def shifted(c):
            k.dve_done.wait(dve, f"r.h{c}")
            d(dve.tensor_tensor(self.DX[:, c, 1:], self.H[:, c, :-1], self.H[:, c, 1:], ALU.subtract), f"r.dx1{c}")
            d(dve.tensor_scalar(self.DX[:, c, 0:1], self.H[:, c, 0:1], -1.0, None, ALU.mult), f"r.dx{c}")

        def first_mixed(c):
            k.dve_done.wait(dve, f"r.dx{c}")
            d(dve.scalar_tensor_tensor(self.XR[:, c, :], self.DX[:, c, :], k.v1("mu0", c), self.H[:, c, :], ALU.mult, ALU.add), f"r.xr{c}")

        def first_low(c):
            k.act_done.wait(dve, f"r.rhi{c}")
            d(dve.tensor_tensor(self.split["r"][1][:, c, :], self.XR[:, c, :], self.split["r"][0][:, c, :].bitcast(F32),
                                ALU.subtract), f"r.rlo{c}")

        def low(x, src):
            for half in range(2):
                sl = slice(4 * half, 4 * half + 4)
                k.act_done.wait(dve, f"r.{x}hi{half}")
                d(dve.tensor_tensor(self.split[x][1][:, sl, :], src[:, sl, :], self.split[x][0][:, sl, :].bitcast(F32), ALU.subtract), f"r.{x}lo")
        flat = lambda t: (lambda i, q: t[:, bass.ds(RING * i + q, 1), :].rearrange("p a t -> p (a t)"))
        for c in range(NC + 3):
            for step, part in enumerate((hidden, shifted, first_mixed, first_low)):
                if 0 <= c - step < NC:
                    part(c - step)
        mixed("w", 1, self.XW)
        mixed("a", 4, self.XA)
        mixed("g", 5, self.XG)
        sh.dve_project(dve, st["r"], flat(self.R), scaled=False)
        mixed("k", 2, self.XK)
        mixed("v", 3, self.XV)
        low("k", self.XK)
        k.act_done.wait(dve, "r.vhi0")
        low("v", self.XV)
        sh.dve_project(dve, st["k"], flat(self.K), scaled=False)
        dve.wait_ge(k.banks_freed, RING + st["k"].base + NC)
        for c in range(NC):
            d(dve.tensor_scalar(self.KN[:, c, :], self.K[:, c, :], k.v1("k_k", c), None, ALU.mult), f"r.kk{c}")
        k.act_done.wait(dve, "r.l27")
        for c in range(NC):
            d(dve.tensor_scalar(self.TA[:, c, :], self.A[:, c, :], 1.0, k.v1("k_a", c), ALU.subtract, ALU.mult), "r.ta")
        k.dve_done.wait(dve, "r.ta")
        dw(dve.scalar_tensor_tensor(self.K[:], self.TA[:], 1.0, self.K[:], ALU.add, ALU.mult), "r.kp")

        def sums():
            for c in range(NC):
                for half in range(2):
                    sl = slice(half * P, (half + 1) * P)
                    d(dve.tensor_tensor_scan(self.CS[:, c, sl], k.mask("reset"), self.SIG[:, c, sl], 0.0, ALU.mult, ALU.add), "r.cs")
            for c in range(NC):
                d(dve.scalar_tensor_tensor(self.BV[:, c, :], self.R[:, c, :], k.v1("r_k", c), self.K[:, c, :], ALU.mult, ALU.mult), "r.bp")
        sh.dve_project(dve, st["v"], flat(self.V), scaled=False, between=sums)
        k.act_done.wait(dve, "r.n16")
        dw(dve.tensor_scalar(self.S16[:], self.S16[:], 1e-12, None, ALU.max), "r.m16")
        d(dve.reciprocal(self.S16[:], self.S16[:]), "r.rn")
        halves = lambda t: t.rearrange("p c (h t) -> p c h t", h=2)
        k.act_done.wait(dve, "r.p")
        d(dve.tensor_tensor(self.AR[:, :, :, 1, :], halves(self.R[:]), halves(self.PP[:]), ALU.mult), "r.R")
        for b in range(4):
            k.pe_done.wait(dve, f"r.rb{b}")
            sl = slice(2 * b, 2 * b + 2)
            ps = k.bank[4 + b][:].rearrange("p (c t) -> p c t", c=2)
            d(dve.tensor_tensor(self.KN[:, sl, :], self.KN[:, sl, :], ps, ALU.mult), "r.kn")
        k.dve_done.wait(dve, "r.kn")
        dw(dve.tensor_tensor(self.A[:], self.KN[:], self.A[:], ALU.mult), "r.b")
        k.act_done.wait(dve, "r.pprev")
        d(dve.scalar_tensor_tensor(self.AR[:, :, :, 0, :], halves(self.KN[:]), -1.0, halves(self.SIG[:]), ALU.mult, ALU.mult), "r.A")
        k.act_done.wait(dve, "r.pinv")
        d(dve.tensor_tensor(self.A[:], self.A[:], self.PI[:], ALU.mult), "r.B")
        d(dve.tensor_tensor(self.K[:], self.K[:], self.PI[:], ALU.mult), "r.K")
        k.dve_done.wait(dve, "r.K")
        d(dve.tensor_scalar(self.BK[:, :, 1, 1, :], self.K[:], k.col(HIGH), None, ALU.mult), "r.bk1")
        k.act_done.wait(dve, "r.bk1")
        k.pool_done.wait(dve, "r.bv")
        dve.wait_ge(k.mixer_loads, self.loads[0])

        for c in range(-1, NC + 1):
            after = self.dve_after(dve, c - 1) if c >= 1 else {}
            before = self.dve_before(dve, c + 1) if c + 1 < NC else {}
            inv = self.dve_invert(dve, c) if 0 <= c < NC else {}
            for step in ("e1", "c1", "e2", "gt", "u", "c2", "ht", "e3", "c3", "l", "e4", "c4", "e5", "c5"):
                for part in (inv, after, before):
                    if step in part:
                        part[step]()

        for j in (1, 2):
            for c in range(NC):
                k.pe_done.wait(dve, f"r.z{j}{c}")
                zj = self.z(c, j)
                d(dve.scalar_tensor_tensor(zj, k.bank[c][:, :P], self.PT[:, c, j:j + 1], zj, ALU.mult, ALU.add), f"r.z{j}{c}")
        for c in range(NC):
            k.pe_done.wait(dve, f"r.ys{c}")
            y1, y2 = self.AR[:, c, 0, 0, 64:], self.AR[:, c, 1, 0, :]
            d(dve.tensor_tensor(y1, y1, k.bank[c][:, T:T + 64], ALU.add), f"r.y{c}")
            d(dve.tensor_tensor(y2, y2, k.bank[c][:, T + 64:T + 192], ALU.add), f"r.y{c}")
        for b in range(4):
            k.pe_done.wait(dve, f"r.mean{b}")
            sl = slice(2 * b, 2 * b + 2)
            ps = k.bank[4 + b][:].rearrange("p (c h t) -> p c h t", c=2, h=2)
            d(dve.scalar_tensor_tensor(halves(self.YC[:, sl, :]), ps, -1.0 / HEAD, self.AR[:, sl, :, 0, :], ALU.mult, ALU.add), f"r.yc{b}")
        k.act_done.wait(dve, "r.ystd")
        d(dve.reciprocal(self.S16b[:], self.S16b[:]), "r.yr")
        for b in range(4):
            if b == 1 and sh.memory:
                sh.memory.dve_start(dve)
            k.pe_done.wait(dve, f"r.yb{b}")
            sl = slice(2 * b, 2 * b + 2)
            ps = k.bank[4 + b][:].rearrange("p (c t) -> p c t", c=2)
            d(dve.tensor_tensor(self.YC[:, sl, :], self.YC[:, sl, :], ps, ALU.mult), f"r.yn{b}")
            if b:
                self.dve_bonus(dve, b - 1)
        self.dve_bonus(dve, 3)
        for b in range(4):
            k.act_done.wait(dve, f"r.oh{b}")
            sl = slice(2 * b, 2 * b + 2)
            d(dve.tensor_tensor(self.Ol[:, sl, :], self.YC[:, sl, :], self.Oh[:, sl, :].bitcast(F32), ALU.subtract), f"r.ol{b}")
        if sh.memory:
            sh.memory.dve_finish(dve)
        sh.dve_resid(dve, st["o"], 1.0, self.next_gain)

    def dve_bonus(self, dve, b):
        k, sl = self.k, slice(2 * b, 2 * b + 2)
        k.act_done.wait(dve, f"r.yl{b}")
        k.dve_done.done(dve.tensor_tensor(self.YC[:, sl, :], self.YC[:, sl, :], self.BV[:, sl, :], ALU.add), f"r.yv{b}")

    def dve_before(self, dve, c):
        k, z = self.k, c % 2

        def l():
            k.pe_done.wait(dve, f"r.l{c}")
            k.dve_done.done(dve.tensor_tensor(self.D[z][:], k.bank[2][:].rearrange("p (u t) -> p u t", u=4),
                                              bcast(k.mask("pair0_lower"), 4), ALU.mult), f"r.l{c}")
        return {"l": l}

    def dve_invert(self, dve, c):
        k, z = self.k, c % 2
        steps = {}

        def side(t, b, s):
            return t[:].rearrange("p u (n b) -> p u n b", b=2 * b)[:, :, :, s * b:(s + 1) * b]

        for lv in range(1, self.LEVELS + 1):
            b = 1 << lv

            def e(lv=lv, b=b):
                k.pe_done.wait(dve, f"r.e{lv}{c}")
                ps = k.bank[self.level_banks(c, lv)[0]][:, :T].rearrange("p (u n b) -> p u n b", u=4, b=b)
                m = self.LOWER[:, lv - 1, :].rearrange("p (n b) -> p n b", b=b).unsqueeze(1).broadcast_to([P, 4, 64 // b, b])
                k.dve_done.done(dve.tensor_tensor(side(self.E[lv - 1], b, 0), ps, m, ALU.mult), f"r.e{lv}{c}")

            def cc(lv=lv, b=b):
                a, other = self.level_banks(c, lv)
                for t, s, bank, made, label in ((self.D[z], 0, other, "r.c", "r.cd"), (self.DT[z], 1, a, "r.k", "r.ct")):
                    k.pe_done.wait(dve, f"{made}{lv}{c}")
                    ps = k.bank[bank][:, :T].rearrange("p (u n b) -> p u n b", u=4, b=b)
                    v = side(t, b, s)
                    k.dve_done.done(dve.tensor_tensor(v, v, ps, ALU.add), f"{label}{lv}{c}")
            steps[f"e{lv}"], steps[f"c{lv}"] = e, cc
        return steps

    def dve_after(self, dve, c):
        k = self.k

        def gt():
            k.pe_done.wait(dve, f"r.gt{c}")
            dst = self.BK[:, c, 0, 0, :].rearrange("p (j t) -> p j t", j=2)
            k.dve_done.done(dve.tensor_tensor(dst, k.bank[4][:, :T].rearrange("p (j t) -> p j t", j=2),
                                              bcast(k.head_ones, 2), ALU.mult), f"r.gt{c}")

        def u():
            k.pe_done.wait(dve, f"r.u{c}")
            for j in range(3):
                k.dve_done.done(dve.scalar_tensor_tensor(self.z(c, j), k.bank[5][:, j * P:(j + 1) * P], self.PT[:, c, j:j + 1],
                                                         k.head_ones, ALU.mult, ALU.mult), f"r.u{c}")

        def ht():
            k.pe_done.wait(dve, f"r.ht{c}")
            r = self.AR[:, c, :, 1, :]
            k.dve_done.done(dve.tensor_tensor(r, r, k.bank[6][:, :T].rearrange("p (h t) -> p h t", h=2), ALU.add), f"r.ht{c}")
        return {"gt": gt, "u": u, "ht": ht}

    def pool(self, pool):
        sh, k, st = self.sh, self.k, self.st
        d = lambda ins, label: k.pool_done.done(ins, label)
        for x in "rkv":
            sh.pool_stage(pool, st[x])
        k.dve_done.wait(pool, "r.cs")
        d(pool.tensor_tensor(self.SIG[:], self.CS[:], self.SIG[:], ALU.subtract), "r.dd")
        k.dve_done.wait(pool, "r.K")
        for lv in range(self.LEVELS):
            d(pool.memset(self.E[lv][:], 0.0), "r.zero")
        k.act_done.wait(pool, "r.bs3")
        d(pool.tensor_tensor(self.BV[:], self.BV[:], self.V[:], ALU.mult), "r.bv")
        ident4 = bcast(k.ident, 4)
        for c in range(-1, NC + 1):
            if c + 1 < NC:
                n, z = c + 1, (c + 1) % 2
                k.dve_done.wait(pool, f"r.l{n}")
                d(pool.tensor_tensor(self.D[z][:], self.D[z][:], ident4, ALU.add), f"r.d{n}")
                m = k.mask("strict", 2).unsqueeze(1).broadcast_to([P, 2, 2, P])
                for hf in range(2):
                    k.act_done.wait(pool, f"r.g1{'ab'[hf]}{n}")
                    d(pool.tensor_tensor(self.LN[z][:, hf], self.LN[z][:, hf], m, ALU.mult), f"r.ln{n}")
                    k.pool_done.wait(pool, f"r.ln{n}")
                    d(pool.tensor_tensor(self.DT[z][:, 2 * hf:2 * hf + 2, :], self.LN[z][:, hf, :, 0, :],
                                         bcast(k.mask("pair0"), 2), ALU.mult), f"r.dm{n}")
                k.pool_done.wait(pool, f"r.dm{n}")
                d(pool.tensor_tensor(self.DT[z][:], self.DT[z][:], ident4, ALU.add), f"r.dt{n}")
                for hf in range(2):
                    k.act_done.wait(pool, f"r.g2{'ab'[hf]}{n}")
                    d(pool.tensor_tensor(self.MQ[z][:, hf], self.MQ[z][:, hf], m, ALU.mult), f"r.mq{n}")
            if c >= 1:
                self.pool_after(pool, c - 1)
        for b in range(4):
            k.dve_done.wait(pool, f"r.yv{b}")
            sl = slice(2 * b, 2 * b + 2)
            d(pool.tensor_tensor(self.YC[:, sl, :], self.YC[:, sl, :], self.G[:, sl, :], ALU.mult), f"r.yg{b}")
        if sh.memory:
            sh.memory.pool(pool)
        sh.pool_stage(pool, st["o"])

    def pool_after(self, pool, c):
        k = self.k
        k.dve_done.wait(pool, f"r.gt{c}")
        g = self.BK[:, c, 0, 0, :].rearrange("p (j t) -> p j t", j=2)
        k.pool_done.done(pool.tensor_tensor(g, g, bcast(k.ident, 2), ALU.add), f"r.gti{c}")


def make_blocks(sh, blocks):
    out, n_ffn = [], 0
    flow = [b for b in blocks if b != "mem"]
    for n, b in enumerate(flow):
        nxt = flow[n + 1] if n + 1 < len(flow) else None
        gain = "final_norm" if nxt == "final" else GAIN_OF.get(nxt)
        if b.startswith("ffn"):
            out.append(FeedForward(sh, b, n_ffn, gain, own_norm=n == 0 or flow[n - 1] != "kv"))
            n_ffn += 1
        else:
            out.append(MIXERS[b.rstrip("01")](sh, b, gain))
    return out


MIXERS = {"rwkv": Rwkv7, "xattn": CrossAttention, "gmlp": GatedMlp, "final": FinalNorm, "hgrn": Hgrn2, "kv": DilatedKeys, "dil": DilatedAttention}


def program(nc, io, blocks, counts):
    with ExitStack() as ctx:
        k = Resources(nc, ctx, io, counts)
        sh = Shared(k, blocks)
        first = GAIN_OF[[b for b in blocks if b != "mem"][0]]
        st0 = sh.stages[0]
        memory = Memory(sh) if "mem" in blocks else None
        sh.memory = memory
        body = make_blocks(sh, blocks)
        prelude_mem = "mem" in blocks and "rwkv" not in blocks
        block = ctx.enter_context(nc.Block())

        @block.sync
        def _(sp):
            for half in range(2):
                sl = slice(NC // 2 * half, NC // 2 * (half + 1))
                sp.dma_start(k.X[:, sl, :], io["x"][:, sl, :]).then_inc(k.x_loaded[half], 16)
            if prelude_mem:
                sp.dma_start(memory.M[:], io["mem"]).then_inc(k.mem_loaded, 16)
            for st in sh.stages:
                sh.sp_stage(sp, st)
            sp.wait_ge(k.banks_freed, RING + sh.n_slabs)
            for c in range(0, NC, 2):
                sp.dma_start(io["out"][:, c:c + 2, :], k.X[:, c:c + 2, :]).then_inc(k.out_stored, 16)
            sp.wait_ge(k.out_stored, 16 * (NC // 2))

        @block.gpsimd
        def _(pool):
            for q in range(RING):
                sh.pool_lo(pool, q, q, st0.width)
            if prelude_mem:
                memory.pool(pool)
            for b in body:
                b.pool(pool)

        @block.scalar
        def _(act):
            for dst, src in ((k.vec, "vec"), (k.cols, "cols"), (k.masks, "masks"), (k.sel, "sel")):
                act.dma_start(dst[:], io[src]).then_inc(k.loaded, 16)
            act.wait_ge(k.loaded, 16 * 4)
            if prelude_mem:
                for q in range(RING):
                    sh.act_hi(act, q, q, st0.width, 0)
                memory.act(act)
            for c in range(NC):
                act.wait_ge(k.x_loaded[c // (NC // 2)], 16)
                sh.prep(act, "act", k.X, first, c, split=first not in UNSPLIT)
                if c % 2 and not prelude_mem:
                    sh.act_hi(act, c // 2, c // 2, st0.width, 0)
            sh.prepped("act", split=first not in UNSPLIT)
            for b in body:
                b.act(act)

        @block.vector
        def _(dve):
            dve.sem_inc(k.banks_freed, RING)
            dve.sem_inc(k.silu_done, 2)
            dve.sem_inc(k.a_ready, 2)
            dve.sem_inc(k.al_ready, 2)
            dve.sem_inc(k.gelu_done, RING)
            dve.wait_ge(k.loaded, 16 * 4)
            if prelude_mem:
                for q in range(RING):
                    sh.dve_lo(dve, q, q, st0.width)
                memory.dve(dve)
            for c in range(NC):
                dve.wait_ge(k.x_loaded[c // (NC // 2)], 16)
                sh.prep(dve, "dve", k.X, first, c, split=first not in UNSPLIT)
                if c % 2 and not prelude_mem:
                    sh.dve_lo(dve, c // 2, c // 2, st0.width)
            sh.prepped("dve", split=first not in UNSPLIT)
            for b in body:
                b.dve(dve)

        @block.tensor
        def _(pe):
            pe.wait_ge(k.loaded, 16 * 4)
            if prelude_mem:
                memory.pe(pe)
            for b in body:
                b.pe(pe)


def by_feature(a):
    return np.ascontiguousarray(a.reshape(T, -1, P).transpose(2, 1, 0))


def column(a):
    return a.reshape(-1, P).T


def slabs(w, group, tiles=None):
    k, n = w.shape
    s = w.reshape(k // (P * group), group, P, n // P, P).transpose(3, 0, 2, 1, 4)
    if tiles is not None:
        s = s[tiles]
    return s.reshape(-1, P, group * P)


def lay_out(a, blocks):
    a = {n: np.asarray(v) for n, v in a.items()}
    v = {"mem_norm": a["mem_norm"], "final_norm": a["final_norm"], "kv_norm": a["kv_norm_2"],
         "w0": a["rwkv_w0"][0], "a0": a["rwkv_a0"][0], "k_k": a["rwkv_k_k"][0], "k_a": a["rwkv_k_a"][0],
         "r_k": a["rwkv_r_k"][0].reshape(-1), "ln_w": a["rwkv_ln_w"][0], "ln_b": a["rwkv_ln_b"][0],
         "lb0": a["a_lb_logits_2"][0], "lb1": a["a_lb_logits_2"][1], "v_norm": a["gmlp_v_norm"][0],
         "a_out_gain": a["a_out_gain_2"][0], "k_gain": np.tile(a["k_gain_2"], (1, 2)).reshape(-1),
         "q_gain": np.tile(a["b_q_gain_2"][0], (1, 2)).reshape(-1)}
    for layer in range(2):
        for n in ("ffn1_norm", "mix_norm", "xattn_norm", "ffn2_norm"):
            v[f"{n}{layer}"] = a[n][layer]
        for j in range(3):
            v[f"norm_gain{layer}{j}"] = a["norm_gain_2"][layer, j]
    for j in range(6):
        v[f"mu{j}"] = a["rwkv_mu"][0, j]
    m = square_masks()
    out = {
        "vec": np.concatenate([column(v[n]) for n, _ in VECTORS], 1),
        "cols": column_masks(),
        "masks": np.stack([m[n] for n in MASKS], 1).astype(np.float32),
        "x": by_feature(a["x"][0]), "mem": by_feature(a["mem"][0]),
    }
    rkv = a["rwkv_w_rkv"][0]
    hg = a["a_w_in_2"][0]
    w = {"mem_kv": a["mem_w_kv"], "rwkv_o": a["rwkv_w_o"][0], "gmlp_uv": a["gmlp_w_uv"][0],
         "gmlp_o": a["gmlp_w_o"][0], "hgrn_o": a["a_w_out_2"][0], 
         "dil_o": a["b_w_o_2"][0]}
    for g in range(GROUPS):
        w[f"dil_q{g}"] = a["b_w_q_2"][0][:, g * D:(g + 1) * D]
        w[f"dil_k{g}"] = a["w_kv_2"][:, g * D:(g + 1) * D]
        w[f"dil_v{g}"] = a["w_kv_2"][:, (GROUPS + g) * D:(GROUPS + g + 1) * D]
    for j, x in enumerate("rkv"):
        w[f"rwkv_{x}"] = rkv[:, j * D:(j + 1) * D]
    for j, x in enumerate("qfig"):
        w[f"hgrn_{x}"] = hg[:, j * D:(j + 1) * D]
    for layer in range(2):
        w[f"xattn{layer}_q"], w[f"xattn{layer}_o"] = a["xattn_wq"][layer], a["xattn_wo"][layer]
    ffn = [(a["ffn1_w_in"][0], a["ffn1_w_out"][0]), (a["ffn2_w_in"][0], a["ffn2_w_out"][0]),
           (a["ffn1_w_in"][1], a["ffn1_w_out"][1]), (a["ffn2_w_in"][1], a["ffn2_w_out"][1])]
    ffn += [(a["ffn_w_in_2"][layer, j], a["ffn_w_out_2"][layer, j]) for layer in range(2) for j in range(2)]
    gate_up = np.arange(2 * FC).reshape(2, FC).T.reshape(-1)
    w8, w11 = [], []
    for st in plan(blocks)[0]:
        if st.name.startswith("ffn_in"):
            w8.append(slabs(ffn[int(st.name[-1])][0], 8, gate_up))
        elif st.name.startswith("ffn_out"):
            w11.append(slabs(ffn[int(st.name[-1])][1], WIDE))
        else:
            w8.append(slabs(w[st.name], 8))
    out["w8"], out["w11"] = np.concatenate(w8), np.concatenate(w11)
    extra_layout(out, a)
    return {n: np.ascontiguousarray(x) for n, x in out.items()}


def extra_layout(out, a):
    out["ws"] = a["gmlp_w_s"][0].transpose(2, 0, 1)
    out["bs"] = a["gmlp_b_s"][0].reshape(-1)
    out["bias_table"], pick = bias_constants()
    out["bias_rows"] = np.concatenate([a["rel_bias_2"], pick])
    for x in "wag":
        w1 = a[f"rwkv_{x}1"][0]
        out[f"lora_{x}1"] = w1.reshape(NC, P, -1).transpose(1, 0, 2)
    out["lora_w2"], out["lora_a2"] = a["rwkv_w2"][0], a["rwkv_a2"][0]
    out["lora_g2a"], out["lora_g2b"] = a["rwkv_g2"][0][:P], a["rwkv_g2"][0][P:]
    m = square_masks()
    out["lower"] = np.stack([m[f"pair{lv}"].T[:, np.arange(P) % (2 << lv) < (1 << lv)] for lv in range(1, 6)], 1).astype(np.float32)
    feature = np.arange(D) // HEAD
    out["to_heads"] = (np.arange(16)[:, None] == feature[None]).reshape(16, NC, P).astype(np.float32)
    out["sel"] = (feature.reshape(NC, P, 1) == np.arange(16)).transpose(1, 0, 2).reshape(P, NC * 16).astype(np.float32)


def kernel(**inputs):
    import concourse.bacc as bacc
    from concourse.bass_utils import run_bass_kernel_spmd

    arrays = lay_out(inputs, BLOCKS)
    counts = {}
    for _ in range(2):
        nc = bacc.Bacc("TRN2", target_bir_lowering=False, num_devices=1)
        io = {n: nc.dram_tensor(f"in_{n}", x.shape, F32, kind="ExternalInput").ap() for n, x in arrays.items()}
        io["out"] = nc.dram_tensor("out_x", (P, NC, T), F32, kind="ExternalOutput").ap()
        program(nc, io, BLOCKS, counts)
    r = run_bass_kernel_spmd(nc, [{f"in_{n}": x for n, x in arrays.items()}], core_ids=[0])
    return r.results[0]["out_x"].transpose(2, 1, 0).reshape(1, T, D)
```
